# Optimizing a Trainium2 kernel written in Bass

```python
import jax
import jax.numpy as jnp
from jax import lax
import numpy as np
import math

D_MODEL = 1024
BATCH = 1
SEQ = 512
DEPTH = 1

CHUNK = 64
Q_BLOCK = 128
N_MEM = 256
EPS = 1e-6
SB_HD = 128
SB_HEADS = D_MODEL // SB_HD
SB_W = SB_HEADS * SB_HD
ML_HEADS = 4
ML_HD = D_MODEL // ML_HEADS
ML_W = ML_HEADS * ML_HD
X_HEADS = 4
X_HD = D_MODEL // X_HEADS
X_W = X_HEADS * X_HD
CONV_W = 4
D_FF = 4 * D_MODEL
N_BRANCH = 3
IN_SIZES = (SB_W, SB_W, SB_W, ML_W, ML_W, ML_W, ML_W, ML_HEADS, ML_HEADS, X_W, N_BRANCH * D_MODEL)
IN_SPLITS = tuple(int(v) for v in np.cumsum(IN_SIZES)[:-1])
N_IN = int(sum(IN_SIZES))


def _rmsnorm(x, g):
    xf = x.astype(jnp.float32)
    y = xf * lax.rsqrt(jnp.mean(xf * xf, axis=-1, keepdims=True) + EPS)
    return (y * g.astype(jnp.float32)).astype(x.dtype)

def _split_heads(t, n):
    b, s, _ = t.shape
    return t.reshape(b, s, n, -1).transpose(0, 2, 1, 3)

def _merge_heads(t):
    b, h, s, d = t.shape
    return t.transpose(0, 2, 1, 3).reshape(b, s, h * d)

def _causal_conv(u, w, b):
    s = u.shape[1]
    up = jnp.pad(u, ((0, 0), (CONV_W - 1, 0), (0, 0)))
    return sum((up[:, j:j + s, :] * w[j] for j in range(CONV_W)), b)

def _stick_breaking(q, k, v):
    _, _, s_len, dh = q.shape
    scale = dh ** -0.5
    kf = k.astype(jnp.float32)
    vf = v.astype(jnp.float32)
    outs = []
    for blk in range(s_len // Q_BLOCK):
        start, end = blk * Q_BLOCK, (blk + 1) * Q_BLOCK
        qb = q[:, :, start:end].astype(jnp.float32)
        z = jnp.einsum('bhqd,bhkd->bhqk', qb, kf[:, :, :end]) * scale
        q_pos = start + jnp.arange(Q_BLOCK)
        k_pos = jnp.arange(end)
        causal = k_pos[None, :] < q_pos[:, None]
        log_1m = jnp.where(causal, jax.nn.log_sigmoid(-z), 0.0)
        later = lax.cumsum(log_1m, axis=3, reverse=True) - log_1m
        log_a = jnp.where(causal, jax.nn.log_sigmoid(z) + later, -jnp.inf)
        outs.append(jnp.einsum('bhqk,bhkd->bhqd', jnp.exp(log_a), vf[:, :, :end]))
    return jnp.concatenate(outs, axis=2)

def _mlstm(q, k, v, i_pre, f_pre):
    f32 = jnp.float32
    b, h, s_len, dh = q.shape
    nc = s_len // CHUNK
    q = q.astype(f32)
    k = k.astype(f32) * (dh ** -0.5)
    v = v.astype(f32)
    i_pre = i_pre.astype(f32)
    log_f = jax.nn.log_sigmoid(f_pre.astype(f32))

    def chunks(t):
        return jnp.moveaxis(t.reshape(b, h, nc, CHUNK, *t.shape[3:]), 2, 0)

    tri = jnp.tril(jnp.ones((CHUNK, CHUNK), dtype=bool))

    def step(carry, xs):
        c_prev, n_prev, m_prev = carry
        qc, kc, vc, ic, lfc = xs
        bcum = jnp.cumsum(lfc, axis=-1)
        d = jnp.where(tri, bcum[..., :, None] - bcum[..., None, :] + ic[..., None, :], -jnp.inf)
        m_inter = bcum + m_prev[..., None]
        m_t = jnp.maximum(m_inter, jnp.max(d, axis=-1))
        w = jnp.exp(d - m_t[..., None])
        s_inter = jnp.exp(m_inter - m_t)
        sc = jnp.einsum('bhtd,bhsd->bhts', qc, kc) * w
        num = jnp.einsum('bhts,bhsd->bhtd', sc, vc) + s_inter[..., None] * jnp.einsum('bhvk,bhtk->bhtv', c_prev, qc)
        den = jnp.sum(sc, axis=-1) + s_inter * jnp.einsum('bhtk,bhk->bht', qc, n_prev)
        h_c = num / jnp.maximum(jnp.abs(den), jnp.exp(-m_t))[..., None]
        b_end = bcum[..., -1]
        g = b_end[..., None] - bcum + ic
        m_new = jnp.maximum(b_end + m_prev, jnp.max(g, axis=-1))
        decay = jnp.exp(b_end + m_prev - m_new)
        wk = jnp.exp(g - m_new[..., None])
        c_new = decay[..., None, None] * c_prev + jnp.einsum('bhsv,bhsk->bhvk', vc * wk[..., None], kc)
        n_new = decay[..., None] * n_prev + jnp.einsum('bhs,bhsk->bhk', wk, kc)
        return (c_new, n_new, m_new), h_c

    init = (jnp.zeros((b, h, dh, dh), f32), jnp.zeros((b, h, dh), f32), jnp.zeros((b, h), f32))
    _, hs = lax.scan(step, init, (chunks(q), chunks(k), chunks(v), chunks(i_pre), chunks(log_f)))
    return jnp.moveaxis(hs, 0, 2).reshape(b, h, s_len, dh)

def _cross_attention(q, mk, mv, gq, gk):
    dh = q.shape[-1]
    qn = _rmsnorm(q, gq)
    kn = _rmsnorm(mk, gk)
    logits = jnp.einsum('bhsd,bhmd->bhsm', qn, kn).astype(jnp.float32) * (dh ** -0.5)
    p = jax.nn.softmax(logits, axis=-1)
    return jnp.einsum('bhsm,bhmd->bhsd', p.astype(mv.dtype), mv)

def first_inputs(seed: int = 0) -> dict:
    key = jax.random.key(seed)
    ks = jax.random.split(key, 24)
    f32 = jnp.float32
    L = DEPTH

    def nrm(k, shape, scale):
        return jax.random.normal(k, shape, f32) * scale

    def gain(k, shape):
        return 1.0 + 0.02 * jax.random.normal(k, shape, f32)

    b_i = nrm(ks[4], (L, ML_HEADS), 0.1)
    b_f = jnp.linspace(3.0, 6.0, ML_HEADS, dtype=f32)[None, :] + nrm(ks[5], (L, ML_HEADS), 0.1)
    return {
        "x": nrm(ks[0], (BATCH, SEQ, D_MODEL), 1.0),
        "mem": nrm(ks[1], (BATCH, N_MEM, D_MODEL), 1.0),
        "g_mix": gain(ks[2], (L, D_MODEL)),
        "w_in": nrm(ks[3], (L, D_MODEL, N_IN), D_MODEL ** -0.5),
        "b_if": jnp.concatenate([b_i, b_f], axis=-1),
        "b_gate": nrm(ks[6], (L, N_BRANCH * D_MODEL), 0.02),
        "conv_w": nrm(ks[7], (L, CONV_W, 2 * ML_W), CONV_W ** -0.5),
        "conv_b": nrm(ks[8], (L, 2 * ML_W), 0.02),
        "ml_norm_g": gain(ks[9], (L, ML_W)),
        "g_mem": gain(ks[10], (L, D_MODEL)),
        "w_mem_kv": nrm(ks[11], (L, D_MODEL, 2 * X_W), D_MODEL ** -0.5),
        "q_norm_g": gain(ks[12], (L, X_HD)),
        "k_norm_g": gain(ks[13], (L, X_HD)),
        "w_sb_proj": nrm(ks[14], (L, SB_W, D_MODEL), SB_W ** -0.5),
        "w_ml_proj": nrm(ks[15], (L, ML_W, D_MODEL), ML_W ** -0.5),
        "w_x_proj": nrm(ks[16], (L, X_W, D_MODEL), X_W ** -0.5),
        "w_out": nrm(ks[17], (L, D_MODEL, D_MODEL), D_MODEL ** -0.5),
        "g_mlp": gain(ks[18], (L, D_MODEL)),
        "w_ff1": nrm(ks[19], (L, D_MODEL, D_FF), D_MODEL ** -0.5),
        "w_ff2": nrm(ks[20], (L, D_FF, D_MODEL), D_FF ** -0.5),
    }

def first_block(x, mem, g_mix, w_in, b_if, b_gate, conv_w, conv_b, ml_norm_g, g_mem, w_mem_kv,
              q_norm_g, k_norm_g, w_sb_proj, w_ml_proj, w_x_proj, w_out, g_mlp, w_ff1, w_ff2):
    dt = x.dtype
    bsz, seq, _ = x.shape
    for l in range(DEPTH):
        h = _rmsnorm(x, g_mix[l])
        z = h @ w_in[l]
        (sb_q, sb_k, sb_v, ml_q, ml_k, ml_v, ml_o, ml_i, ml_f, x_q, gate_pre) = jnp.split(z, IN_SPLITS, axis=-1)

        y_sb = _merge_heads(_stick_breaking(_split_heads(sb_q, SB_HEADS), _split_heads(sb_k, SB_HEADS),
                                            _split_heads(sb_v, SB_HEADS))).astype(dt)

        qk = jax.nn.silu(_causal_conv(jnp.concatenate([ml_q, ml_k], axis=-1), conv_w[l], conv_b[l]))
        mq, mk = jnp.split(qk, 2, axis=-1)
        i_pre = (ml_i + b_if[l, :ML_HEADS]).transpose(0, 2, 1)
        f_pre = (ml_f + b_if[l, ML_HEADS:]).transpose(0, 2, 1)
        hm = _mlstm(_split_heads(mq, ML_HEADS), _split_heads(mk, ML_HEADS), _split_heads(ml_v, ML_HEADS), i_pre, f_pre)
        hm = _rmsnorm(hm, ml_norm_g[l].reshape(ML_HEADS, 1, ML_HD))
        y_ml = (_merge_heads(hm) * jax.nn.sigmoid(ml_o.astype(jnp.float32))).astype(dt)

        kv = _rmsnorm(mem, g_mem[l]) @ w_mem_kv[l]
        mem_k, mem_v = jnp.split(kv, 2, axis=-1)
        y_x = _merge_heads(_cross_attention(_split_heads(x_q, X_HEADS), _split_heads(mem_k, X_HEADS),
                                            _split_heads(mem_v, X_HEADS), q_norm_g[l], k_norm_g[l])).astype(dt)

        gates = jax.nn.sigmoid(gate_pre + b_gate[l]).reshape(bsz, seq, N_BRANCH, D_MODEL)
        mixed = (gates[:, :, 0] * (y_sb @ w_sb_proj[l])
                 + gates[:, :, 1] * (y_ml @ w_ml_proj[l])
                 + gates[:, :, 2] * (y_x @ w_x_proj[l]))
        x = x + mixed @ w_out[l]

        u = _rmsnorm(x, g_mlp[l]) @ w_ff1[l]
        x = x + jnp.square(jax.nn.relu(u)) @ w_ff2[l]
    return x


GRID_W = 64
CTX_LEN = 256
N_BRANCH_2 = 4
MIX_WIDTH = D_MODEL // N_BRANCH_2
POOL_WINDOWS = (2, 4, 8, 16)
POOL_GROUPS = len(POOL_WINDOWS)
FNET_GROUPS = 4
HYENA_ORDER = 2
HYENA_BANDS = 16
HYENA_POS_DIM = 1 + 2 * HYENA_BANDS
HYENA_FILTER_HIDDEN = 64
HYENA_DECAY_TARGET = 1e-2
HYENA_FAST_DECAY = 0.3
HYENA_SLOW_DECAY = 1.5
HYENA_DECAY_SHIFT = 0.05
SHORT_CONV = 3
NA_HEAD_DIM = 64
NA_HEADS = MIX_WIDTH // NA_HEAD_DIM
NA_WIN_H = 8
NA_WIN_W = 16
FFN_HIDDEN = 2816
NEG_INF = -1e30

POOL_OFF = 0
FNET_OFF = POOL_OFF + MIX_WIDTH
HYENA_OFF = FNET_OFF + MIX_WIDTH
NA_OFF = HYENA_OFF + 3 * MIX_WIDTH
GATE_OFF = NA_OFF + 3 * MIX_WIDTH
IN_WIDTH = GATE_OFF + N_BRANCH_2 * D_MODEL


def rmsnorm(x, g):
    xf = x.astype(jnp.float32)
    y = xf * lax.rsqrt(jnp.mean(xf * xf, axis=-1, keepdims=True) + EPS)
    return (y * g.astype(jnp.float32)).astype(x.dtype)

def ada_norm(x, g, shift, scale):
    return rmsnorm(x, g) * (1 + scale) + shift

def depthwise_conv(x, w, b):
    K = w.shape[0]
    pad = K // 2
    L = x.shape[1]
    xp = jnp.pad(x, ((0, 0), (pad, K - 1 - pad), (0, 0)))
    return sum(xp[:, j:j + L] * w[j] for j in range(K)) + b

def pool_mixer(u, pool_w, pool_scale):
    B, L, _ = u.shape
    ug = u.reshape(B, L, POOL_GROUPS, -1).astype(jnp.float32)
    csum = jnp.concatenate([jnp.zeros_like(ug[:, :1]), jnp.cumsum(ug, axis=1)], axis=1)
    t = np.arange(L)[:, None]
    win = np.array(POOL_WINDOWS)[None, :]
    lo = np.clip(t - win // 2, 0, L)
    hi = np.clip(t - win // 2 + win, 0, L)
    grp = np.arange(POOL_GROUPS)[None, :]
    cnt = (hi - lo).astype(np.float32)[None, :, :, None]
    y = (csum[:, hi, grp] - csum[:, lo, grp]) / cnt - ug
    y = jnp.einsum('blgc,gcd->blgd', y.astype(u.dtype), pool_w)
    return y.reshape(B, L, -1) * pool_scale

def fourier_mixer(u):
    B, L, _ = u.shape
    ug = u.reshape(B, L, FNET_GROUPS, -1).astype(jnp.float32)
    y = jnp.fft.fft2(ug, axes=(1, 3), norm='ortho').real
    return y.reshape(B, L, -1).astype(u.dtype)

def hyena_filters(L, p):
    f32 = jnp.float32
    t = jnp.linspace(0.0, 1.0, L, dtype=f32)[:, None]
    bands = jnp.linspace(1e-4, HYENA_BANDS - 1, HYENA_BANDS, dtype=f32)[None, :]
    ang = (2.0 * math.pi / L) * jnp.arange(L, dtype=f32)[:, None] * bands
    feats = jnp.concatenate([t, jnp.cos(ang), -jnp.sin(ang)], axis=-1)
    freq = p['hyena_freq'].astype(f32)
    h = jnp.sin(freq * (feats @ p['hyena_filt_w1'].astype(f32) + p['hyena_filt_b1'].astype(f32)))
    h = jnp.sin(freq * (h @ p['hyena_filt_w2'].astype(f32) + p['hyena_filt_b2'].astype(f32)))
    h = (h @ p['hyena_filt_w3'].astype(f32) + p['hyena_filt_b3'].astype(f32))
    h = h.reshape(L, HYENA_ORDER, 2, MIX_WIDTH)
    deltas = jnp.linspace(math.log(HYENA_DECAY_TARGET) / HYENA_SLOW_DECAY,
                          math.log(HYENA_DECAY_TARGET) / HYENA_FAST_DECAY, MIX_WIDTH, dtype=f32)
    decay = jnp.exp(-t[:, :, None, None] * jnp.abs(deltas))
    h = h * (decay + HYENA_DECAY_SHIFT)
    return h / (jnp.sum(jnp.abs(h), axis=(0, 2), keepdims=True) + EPS)

def long_conv(z, hf, hb, skip):
    L, C = hf.shape
    k = jnp.concatenate([hf, jnp.zeros((1, C), hf.dtype), hb[1:][::-1]], axis=0)
    zf = jnp.fft.rfft(z, n=2 * L, axis=1)
    kf = jnp.fft.rfft(k, axis=0)
    y = jnp.fft.irfft(zf * kf[None], n=2 * L, axis=1)[:, :L]
    return y + skip * z

def hyena_mixer(u, p):
    u_c = depthwise_conv(u, p['hyena_conv_w'], p['hyena_conv_b']).astype(jnp.float32)
    v, x1, x2 = jnp.split(u_c, 3, axis=-1)
    h = hyena_filters(u.shape[1], p)
    skip = p['hyena_skip'].astype(jnp.float32)
    z = v
    for n, gate in enumerate((x1, x2)):
        z = gate * long_conv(z, h[:, n, 0], h[:, n, 1], skip[n])
    return z.astype(u.dtype)

def neighbourhood_attention(q, k, v, k_ctx, v_ctx, rpb):
    B, L, _ = q.shape
    rows = L // GRID_W
    kh = min(NA_WIN_H, rows)
    grid = (B, rows, GRID_W, NA_HEADS, NA_HEAD_DIM)
    q, k, v = q.reshape(grid), k.reshape(grid), v.reshape(grid)
    kc = k_ctx.reshape(B, -1, NA_HEADS, NA_HEAD_DIM)
    vc = v_ctx.reshape(B, -1, NA_HEADS, NA_HEAD_DIM)
    r = np.arange(rows)
    r0 = np.clip(r - kh // 2, 0, rows - kh)
    row_idx = r0[:, None] + np.arange(kh)[None, :]
    col = np.arange(GRID_W)
    c0 = np.clip(col - NA_WIN_W // 2, 0, GRID_W - NA_WIN_W)
    col_ok = (col[None, :] >= c0[:, None]) & (col[None, :] < c0[:, None] + NA_WIN_W)
    dr = row_idx - r[:, None] + (NA_WIN_H - 1)
    dc = np.clip(col[None, :] - col[:, None], 1 - NA_WIN_W, NA_WIN_W - 1) + (NA_WIN_W - 1)
    bias = rpb.astype(jnp.float32)[:, dr[:, None, :, None], dc[None, :, None, :]]
    bias = jnp.where(col_ok[:, None, :], bias, NEG_INF)
    kb = k[:, row_idx]
    vb = v[:, row_idx]
    scale = NA_HEAD_DIM ** -0.5
    s_nb = jnp.einsum('brqhd,brikhd->bhrqik', q, kb).astype(jnp.float32) * scale + bias
    s_cx = jnp.einsum('brqhd,bchd->bhrqc', q, kc).astype(jnp.float32) * scale
    n_nb = kh * GRID_W
    s = jnp.concatenate([s_nb.reshape(B, NA_HEADS, rows, GRID_W, n_nb), s_cx], axis=-1)
    prob = jax.nn.softmax(s, axis=-1).astype(v.dtype)
    p_nb = prob[..., :n_nb].reshape(s_nb.shape)
    p_cx = prob[..., n_nb:]
    o = (jnp.einsum('bhrqik,brikhd->brqhd', p_nb, vb)
         + jnp.einsum('bhrqc,bchd->brqhd', p_cx, vc))
    return o.reshape(B, L, MIX_WIDTH)

def context_attention(q, k, v):
    B, C, _ = q.shape
    shp = (B, C, NA_HEADS, NA_HEAD_DIM)
    q, k, v = q.reshape(shp), k.reshape(shp), v.reshape(shp)
    s = jnp.einsum('bqhd,bkhd->bhqk', q, k).astype(jnp.float32) * (NA_HEAD_DIM ** -0.5)
    prob = jax.nn.softmax(s, axis=-1).astype(v.dtype)
    return jnp.einsum('bhqk,bkhd->bqhd', prob, v).reshape(B, C, MIX_WIDTH)

def token_mixer(proj, k_ctx, v_ctx, p, on_grid):
    def cols(off, width):
        return proj[..., off:off + width]
    y_pool = pool_mixer(cols(POOL_OFF, MIX_WIDTH), p['pool_w'], p['pool_scale'])
    y_fnet = fourier_mixer(cols(FNET_OFF, MIX_WIDTH))
    y_hyena = hyena_mixer(cols(HYENA_OFF, 3 * MIX_WIDTH), p)
    q = cols(NA_OFF, MIX_WIDTH)
    if on_grid:
        y_na = neighbourhood_attention(q, cols(NA_OFF + MIX_WIDTH, MIX_WIDTH),
                                       cols(NA_OFF + 2 * MIX_WIDTH, MIX_WIDTH),
                                       k_ctx, v_ctx, p['na_rpb'])
    else:
        y_na = context_attention(q, k_ctx, v_ctx)
    gates = jax.nn.sigmoid(cols(GATE_OFF, N_BRANCH_2 * D_MODEL))
    merged = 0
    for b, y in enumerate((y_pool, y_fnet, y_hyena, y_na)):
        merged = merged + gates[..., b * D_MODEL:(b + 1) * D_MODEL] * (y @ p['w_branch'][b])
    return merged @ p['w_out']

def conv_ffn(h, p):
    u, g = jnp.split(h @ p['ffn_w_up'], 2, axis=-1)
    g = depthwise_conv(g, p['ffn_conv_w'], p['ffn_conv_b'])
    return (jax.nn.silu(g) * u) @ p['ffn_w_down']

def second_inputs(seed: int = 0) -> dict:
    key = jax.random.key(seed)
    ks = iter(jax.random.split(key, 32))

    def nrm(shape, s):
        return jax.random.normal(next(ks), shape, jnp.float32) * s

    D, F, M, Hd = D_MODEL, FFN_HIDDEN, MIX_WIDTH, HYENA_FILTER_HIDDEN
    return {
        'x': nrm((BATCH, SEQ, D), 1.0),
        'c': nrm((BATCH, D), 1.0),
        'ctx': nrm((BATCH, CTX_LEN, D), 1.0),
        'c_ctx': nrm((D,), 1.0),
        'w_mod': nrm((DEPTH, D, 6 * D), 0.5 * D ** -0.5),
        'b_mod': nrm((DEPTH, 6 * D), 0.01),
        'norm1_g': 1.0 + nrm((DEPTH, D), 0.02),
        'norm2_g': 1.0 + nrm((DEPTH, D), 0.02),
        'w_in': nrm((DEPTH, D, IN_WIDTH), D ** -0.5),
        'pool_w': nrm((DEPTH, POOL_GROUPS, M // POOL_GROUPS, M // POOL_GROUPS), (M // POOL_GROUPS) ** -0.5),
        'pool_scale': 1.0 + nrm((DEPTH, M), 0.02),
        'hyena_conv_w': nrm((DEPTH, SHORT_CONV, 3 * M), SHORT_CONV ** -0.5),
        'hyena_conv_b': nrm((DEPTH, 3 * M), 0.01),
        'hyena_filt_w1': nrm((DEPTH, HYENA_POS_DIM, Hd), HYENA_POS_DIM ** -0.5),
        'hyena_filt_b1': nrm((DEPTH, Hd), 0.01),
        'hyena_filt_w2': nrm((DEPTH, Hd, Hd), Hd ** -0.5),
        'hyena_filt_b2': nrm((DEPTH, Hd), 0.01),
        'hyena_filt_w3': nrm((DEPTH, Hd, HYENA_ORDER * 2 * M), Hd ** -0.5),
        'hyena_filt_b3': nrm((DEPTH, HYENA_ORDER * 2 * M), 0.01),
        'hyena_freq': 1.0 + nrm((DEPTH, Hd), 0.1),
        'hyena_skip': nrm((DEPTH, HYENA_ORDER, M), 0.5),
        'na_rpb': nrm((DEPTH, NA_HEADS, 2 * NA_WIN_H - 1, 2 * NA_WIN_W - 1), 0.1),
        'w_branch': nrm((DEPTH, N_BRANCH_2, M, D), M ** -0.5),
        'w_out': nrm((DEPTH, D, D), D ** -0.5),
        'ffn_w_up': nrm((DEPTH, D, 2 * F), D ** -0.5),
        'ffn_conv_w': nrm((DEPTH, SHORT_CONV, F), SHORT_CONV ** -0.5),
        'ffn_conv_b': nrm((DEPTH, F), 0.01),
        'ffn_w_down': nrm((DEPTH, F, D), F ** -0.5),
        'final_norm_g': 1.0 + nrm((D,), 0.02),
    }

def second_block(x, c, ctx, c_ctx, w_mod, b_mod, norm1_g, norm2_g, w_in, pool_w, pool_scale,
              hyena_conv_w, hyena_conv_b, hyena_filt_w1, hyena_filt_b1, hyena_filt_w2,
              hyena_filt_b2, hyena_filt_w3, hyena_filt_b3, hyena_freq, hyena_skip, na_rpb,
              w_branch, w_out, ffn_w_up, ffn_conv_w, ffn_conv_b, ffn_w_down, final_norm_g):
    xc = ctx
    c_act = jax.nn.silu(c)
    cc_act = jax.nn.silu(c_ctx)[None]
    for l in range(DEPTH):
        last = l == DEPTH - 1
        p = {
            'pool_w': pool_w[l], 'pool_scale': pool_scale[l],
            'hyena_conv_w': hyena_conv_w[l], 'hyena_conv_b': hyena_conv_b[l],
            'hyena_filt_w1': hyena_filt_w1[l], 'hyena_filt_b1': hyena_filt_b1[l],
            'hyena_filt_w2': hyena_filt_w2[l], 'hyena_filt_b2': hyena_filt_b2[l],
            'hyena_filt_w3': hyena_filt_w3[l], 'hyena_filt_b3': hyena_filt_b3[l],
            'hyena_freq': hyena_freq[l], 'hyena_skip': hyena_skip[l], 'na_rpb': na_rpb[l],
            'w_branch': w_branch[l], 'w_out': w_out[l],
            'ffn_w_up': ffn_w_up[l], 'ffn_conv_w': ffn_conv_w[l],
            'ffn_conv_b': ffn_conv_b[l], 'ffn_w_down': ffn_w_down[l],
        }
        mod = (c_act @ w_mod[l] + b_mod[l])[:, None]
        mod_c = (cc_act @ w_mod[l] + b_mod[l])[:, None]
        sh1, sc1, g1, sh2, sc2, g2 = jnp.split(mod, 6, axis=-1)
        sh1c, sc1c, g1c, sh2c, sc2c, g2c = jnp.split(mod_c, 6, axis=-1)
        hc = ada_norm(xc, norm1_g[l], sh1c, sc1c)
        if last:
            kv_c = hc @ w_in[l][:, NA_OFF + MIX_WIDTH:NA_OFF + 3 * MIX_WIDTH]
        else:
            proj_c = hc @ w_in[l]
            kv_c = proj_c[..., NA_OFF + MIX_WIDTH:NA_OFF + 3 * MIX_WIDTH]
        k_c, v_c = jnp.split(kv_c, 2, axis=-1)
        hx = ada_norm(x, norm1_g[l], sh1, sc1)
        proj_x = hx @ w_in[l]
        x = x + g1 * token_mixer(proj_x, k_c, v_c, p, True)
        x = x + g2 * conv_ffn(ada_norm(x, norm2_g[l], sh2, sc2), p)
        if not last:
            xc = xc + g1c * token_mixer(proj_c, k_c, v_c, p, False)
            xc = xc + g2c * conv_ffn(ada_norm(xc, norm2_g[l], sh2c, sc2c), p)
    return rmsnorm(x, final_norm_g)


def setup_inputs(seed=0):
    out = dict(first_inputs(seed))
    for name, value in second_inputs(seed + 1).items():
        if name != "x":
            out[name + "_2"] = value
    return out


def reference(
    x, mem, g_mix, w_in, b_if, b_gate, conv_w, conv_b, ml_norm_g, g_mem, w_mem_kv, q_norm_g,
    k_norm_g, w_sb_proj, w_ml_proj, w_x_proj, w_out, g_mlp, w_ff1, w_ff2, c_2, ctx_2, c_ctx_2,
    w_mod_2, b_mod_2, norm1_g_2, norm2_g_2, w_in_2, pool_w_2, pool_scale_2, hyena_conv_w_2,
    hyena_conv_b_2, hyena_filt_w1_2, hyena_filt_b1_2, hyena_filt_w2_2, hyena_filt_b2_2,
    hyena_filt_w3_2, hyena_filt_b3_2, hyena_freq_2, hyena_skip_2, na_rpb_2, w_branch_2, w_out_2,
    ffn_w_up_2, ffn_conv_w_2, ffn_conv_b_2, ffn_w_down_2, final_norm_g_2,
):
    x = first_block(
        x, mem, g_mix, w_in, b_if, b_gate, conv_w, conv_b, ml_norm_g, g_mem, w_mem_kv, q_norm_g,
        k_norm_g, w_sb_proj, w_ml_proj, w_x_proj, w_out, g_mlp, w_ff1, w_ff2,
    )
    return second_block(
        x, c_2, ctx_2, c_ctx_2, w_mod_2, b_mod_2, norm1_g_2, norm2_g_2, w_in_2, pool_w_2,
        pool_scale_2, hyena_conv_w_2, hyena_conv_b_2, hyena_filt_w1_2, hyena_filt_b1_2,
        hyena_filt_w2_2, hyena_filt_b2_2, hyena_filt_w3_2, hyena_filt_b3_2, hyena_freq_2,
        hyena_skip_2, na_rpb_2, w_branch_2, w_out_2, ffn_w_up_2, ffn_conv_w_2, ffn_conv_b_2,
        ffn_w_down_2, final_norm_g_2,
    )


_drawn_inputs = setup_inputs


def setup_inputs(seed=0):
    import zlib

    import numpy as np

    out = dict(_drawn_inputs(seed))
    spreads = {}
    factors = {'g_mix': 4.226,
     'b_gate': 8.0,
     'conv_b': 64.0,
     'ml_norm_g': 8.0,
     'g_mem': 8.0,
     'q_norm_g': 8.0,
     'k_norm_g': 8.0,
     'g_mlp': 3.335,
     'ctx_2': 6.533,
     'c_ctx_2': 3.08,
     'b_mod_2': 8.0,
     'norm1_g_2': 8.0,
     'norm2_g_2': 40.668,
     'pool_scale_2': 59.437,
     'hyena_conv_b_2': 29.659,
     'hyena_filt_w1_2': 6.187,
     'hyena_filt_b1_2': 8.0,
     'hyena_filt_w2_2': 5.972,
     'hyena_filt_b2_2': 8.0,
     'hyena_filt_w3_2': 5.218,
     'hyena_filt_b3_2': 39.774,
     'hyena_freq_2': 8.0,
     'na_rpb_2': 200.0,
     'ffn_conv_b_2': 200.0,
     'final_norm_g_2': 25.722}
    for name, (base, spread) in spreads.items():
        noise = np.random.default_rng([zlib.crc32(name.encode()), seed]).standard_normal(out[name].shape)
        drawn = base * np.exp(spread * noise) if base else spread * noise
        out[name] = jnp.asarray(drawn.astype(out[name].dtype))
    for name, factor in factors.items():
        out[name] = (out[name] * factor).astype(out[name].dtype)
    return out
```

```python
from contextlib import ExitStack

import numpy as np
import concourse.bass as bass
from concourse import mybir

F32 = mybir.dt.float32
F32R = mybir.dt.float32r
ALU = mybir.AluOpType
ACT = mybir.ActivationFunctionType
AX = mybir.AxisListType.X

P = 128
D = 1024
KT = D // P
S = 512
TT = S // P
M = 256
MT = M // P
EPS = 1e-6
SB_HEADS, SB_HD = 8, 128
ML_HEADS, ML_HD = 4, 256
X_HEADS, X_HD = 4, 256
FF_TILES = 4 * D // P
MIX = 256
GATES2 = 4
NA_HEADS, NA_HD = 4, 64
GRID = 64
ROWS = S // GRID
FFN = 2816
FFN_TILES = FFN // P
NEG = -1e30

CHUNK = 1024
SLOTS = 4
LEAD = SLOTS - 1

COLS = [("g_mix", 8), ("b_gate", 24), ("conv_w", 64), ("conv_b", 16), ("ml_norm_g", 8), ("g_mem", 8),
        ("q_norm_g", 2), ("k_norm_g", 2), ("g_mlp", 8), ("norm1_g", 8), ("norm2_g", 8), ("b_mod", 48),
        ("c", 8), ("c_ctx", 8), ("pool_scale", 2), ("hy_conv_w", 18), ("hy_conv_b", 6), ("hy_skip", 4),
        ("ffn_conv_w", 66), ("ffn_conv_b", 22), ("final_g", 8), ("b_i", 1), ("b_f", 1),
        ("filt_b1", 1), ("filt_b2", 1), ("freq", 1)]
COL_AT, NCOLS = {}, 0
for _name, _n in COLS:
    COL_AT[_name] = NCOLS
    NCOLS += _n

CONSTS = ["ident", "ones", "neg_ones", "neg_lower", "keep_before", "hide_not_before", "hide_after",
          "sel0", "sel1", "sel2", "sel3"]


TWO_PI = 6.283185307179586
TWO_PI_PARTS = (6.28125, 0.0019350051879882812, TWO_PI - 6.28125 - 0.0019350051879882812)
ROUND = 1.5 * 2.0 ** 23
PI_BELOW = 3.1415925


class Counter:

    def __init__(self, sem, step=1):
        self.sem, self.step, self.n = sem, step, 0


class Event:

    def __init__(self, counter, k, loop=None, per=None):
        self.counter, self.k, self.loop, self.per = counter, k, loop, per

    def value(self, j, loop, back=0):
        if self.loop is None:
            return self.k
        per = self.loop.per[self.counter] if self.per is None else self.per
        if self.loop is not loop:
            return self.k + per * (self.loop.n - 1)
        if isinstance(j, int):
            return self.k + per * (j - back)
        return j * per + (self.k - per * back)


    def reached(self, loop, back=0):
        per = self.loop.per[self.counter] if self.loop and self.per is None else self.per or 0
        if self.loop is not None and self.loop is not loop:
            return self.k + per * (self.loop.n - 1)
        return self.k - per * back


class Last:

    def __init__(self, event, pending=None, name=None):
        self.event, self.pending, self.name = event, pending, name


class Loop:
    def __init__(self, prog, n, chunks):
        self.prog, self.n, self.chunks = prog, n, chunks
        self.bodies, self.per, self.base, self.marks, self.heads = {}, {}, {}, {}, {}


class Engine:

    def __init__(self, prog, sem):
        self.prog, self.steps, self.counter = prog, [], Counter(sem)

    def do(self, emit, *waits, counter=None):
        counter = counter or self.counter
        loop = self.prog.loop
        event = self.prog.count(counter)
        for w in waits:
            if isinstance(w, Last) and w.pending and w.event is not None:
                loop.heads.setdefault(self, []).append(w.event)
            elif loop and isinstance(w, Event) and w.loop is not loop:
                loop.heads.setdefault(self, []).append(w)
        if loop:
            waits = [w for w in waits if isinstance(w, Last) or w.loop is loop]

        def step(e, j):
            newest = {}
            for w in waits:
                back = 0
                if isinstance(w, Last):
                    if w.pending:
                        if w.name not in w.pending.marks:
                            continue
                        back, w = 1, w.pending.marks[w.name]
                    elif w.event is None:
                        continue
                    else:
                        w = w.event
                value, at = w.value(j, loop, back), w.reached(loop, back)
                if w.counter not in newest or at > newest[w.counter][0]:
                    newest[w.counter] = at, value
            for c, (_, value) in newest.items():
                if not isinstance(value, int) or value > 0:
                    e.wait_ge(c.sem, value)
            emit(e, j).then_inc(counter.sem, counter.step)

        (loop.bodies.setdefault(self, []) if loop else self.steps).append(step)
        return event

    def run(self, e):
        for s in self.steps:
            s(e, 0)


class Program:
    def __init__(self):
        self.loop, self.marks, self.chunk = None, {}, 0

    def count(self, counter):
        loop = self.loop
        if loop is None:
            counter.n += counter.step
            return Event(counter, counter.n)
        loop.base.setdefault(counter, counter.n)
        loop.per[counter] = loop.per.get(counter, 0) + counter.step
        return Event(counter, loop.base[counter] + loop.per[counter], loop)

    def mark(self, name, event):
        (self.loop.marks if self.loop else self.marks)[name] = event
        return event

    def last(self, name):
        if self.loop is None:
            return Last(self.marks.get(name))
        if name in self.loop.marks:
            return Last(self.loop.marks[name])
        return Last(self.marks.get(name), pending=self.loop, name=name)

    def loop_of(self, n, chunks, describe):
        if n == 0:
            return
        loop = self.loop = Loop(self, n, chunks)
        first = self.chunk
        describe()
        assert self.chunk == first + chunks and chunks % SLOTS == 0
        self.chunk = first + chunks * n
        self.loop = None
        for counter, per in loop.per.items():
            counter.n = loop.base[counter] + per * n
        self.marks.update(loop.marks)
        for engine, body in loop.bodies.items():
            def run(e, _, body=body, engine=engine):
                heads = {}
                for w in loop.heads.get(engine, []):
                    heads[w.counter] = max(heads.get(w.counter, 0), w.value(0, None))
                for c, value in heads.items():
                    if value > 0:
                        e.wait_ge(c.sem, value)
                if n == 1:
                    for s in body:
                        s(e, 0)
                else:
                    with e.Fori(0, n) as j:
                        for s in body:
                            s(e, j)
            engine.steps.append(run)


class Machine:

    def __init__(self, nc, total_chunks, stream):
        self.nc, self.prog, self.total, self.stream, self.loaded = nc, Program(), total_chunks, stream, 0
        sem = nc.alloc_semaphore
        self.pe, self.act, self.dve = (Engine(self.prog, sem(n)) for n in ("pe_done", "act_done", "dve_done"))
        self.pool, self.sp = (Engine(self.prog, sem(n)) for n in ("pool_done", "sp_done"))
        self.raw_in = [Counter(sem(f"raw_in{s}"), 16) for s in range(SLOTS)]
        self.hi_split, self.lo_split, self.used = (Counter(sem(n)) for n in ("hi_split", "lo_split", "chunk_used"))
        self.base = -(-nc.sbuf_base // 32) * 32 if isinstance(nc.sbuf_base, int) else 16896
        at = self.place
        self.raw = [at(f"raw{s}", 4 * s, [P, CHUNK]) for s in range(SLOTS)]
        self.whi = [at(f"whi{s}", 16 + 4 * s, [P, CHUNK], F32R) for s in range(SLOTS)]
        self.wlo = [at(f"wlo{s}", 32 + 4 * s, [P, CHUNK], F32R) for s in range(SLOTS)]
        self.bank = [nc.alloc_psum_tensor(f"bank{b}", [P, 512], F32) for b in range(8)]

    def place(self, name, kib, shape, dtype=F32):
        return self.nc.alloc_sbuf_tensor_at(name, shape, dtype, offset=self.base + int(kib * 1024))


    def chunk_event(self, counter, c):
        loop = self.prog.loop
        return Event(counter, c + 1, loop, loop.chunks if loop else 0) if loop else Event(counter, c + 1)

    def split_high(self, c):
        loop, slot = self.prog.loop, c % SLOTS
        raw = Event(self.raw_in[slot], 16 * (c // SLOTS + 1), loop, 16 * loop.chunks // SLOTS if loop else None)
        self.act.do(lambda e, j: e.activation(self.whi[slot][:], self.raw[slot][:], ACT.Copy),
                    raw, self.chunk_event(self.used, c - SLOTS), counter=self.hi_split)

    def take(self, matmuls, *waits):
        c, slot = self.prog.chunk, self.prog.chunk % SLOTS
        self.prog.chunk += 1
        if self.prog.loop or c + LEAD < self.total:
            self.split_high(c + LEAD)
        return self.pe.do(lambda e, j: matmuls(e, j, self.whi[slot], self.wlo[slot]),
                          self.chunk_event(self.lo_split, c), *waits, counter=self.used)

    def start_stream(self):
        for c in range(LEAD):
            self.split_high(c)

        def low_parts(e, _):
            with e.Fori(0, self.total // SLOTS) as j:
                for s in range(SLOTS):
                    e.wait_ge(self.hi_split.sem, j * SLOTS + (s + 1))
                    i = e.tensor_tensor(self.wlo[s][:], self.raw[s][:], self.whi[s][:].bitcast(F32), ALU.subtract)
                    i.then_inc(self.lo_split.sem, 1)
        self.pool.steps.append(low_parts)

    def load_chunks(self, upto):
        first, upto = self.loaded, min(upto, self.total)
        while self.loaded < min(SLOTS, upto) or (self.loaded < upto and self.loaded % SLOTS):
            c, s = self.loaded, self.loaded % SLOTS

            def one(e, _, c=c, s=s):
                if c >= SLOTS:
                    e.wait_ge(self.lo_split.sem, c - SLOTS + 1)
                e.dma_start(self.raw[s][:], self.stream[c]).then_inc(self.raw_in[s].sem, 16)
            self.sp.steps.append(one)
            self.loaded += 1
        rounds = (upto - self.loaded) // SLOTS
        if rounds > 0:
            def many(e, _, first=self.loaded, rounds=rounds):
                with e.Fori(0, rounds) as j:
                    for s in range(SLOTS):
                        e.wait_ge(self.lo_split.sem, j * SLOTS + (first - SLOTS + s + 1))
                        e.dma_start(self.raw[s][:], self.stream[j * SLOTS + (first + s)]).then_inc(self.raw_in[s].sem, 16)
            self.sp.steps.append(many)
            self.loaded += rounds * SLOTS
        while self.loaded < upto:
            c, s = self.loaded, self.loaded % SLOTS

            def one(e, _, c=c, s=s):
                e.wait_ge(self.lo_split.sem, c - SLOTS + 1)
                e.dma_start(self.raw[s][:], self.stream[c]).then_inc(self.raw_in[s].sem, 16)
            self.sp.steps.append(one)
            self.loaded += 1

    def fetch(self, name, dst, src, *waits):
        self.load_chunks(self.prog.chunk + SLOTS)
        return self.sp.do(lambda e, j: e.dma_start(dst, src), *waits, counter=Counter(self.nc.alloc_semaphore(name), 16))


    def bank_free(self, b):
        return self.prog.last(f"bank{b} free")

    def free_bank(self, b, event):
        self.prog.mark(f"bank{b} free", event)

    def product_tile(self, b, hi, lo, *waits, kts=KT, cols=S, at=0, n=None):
        def mm(e, j, whi, wlo):
            out = self.bank[b][:, 0:cols]
            for k in range(kts):
                w = slice(k * P, (k + 1) * P)
                e.matmul(out, whi[:, w], hi[:, k, 0:cols], start=(k == 0), stop=False)
                e.matmul(out, whi[:, w], lo[:, k, 0:cols], start=False, stop=False)
                i = e.matmul(out, wlo[:, w], hi[:, k, 0:cols], start=False, stop=(k == kts - 1))
            return i
        return self.take(mm, self.bank_free(b), *waits)

    def product_rows(self, banks, hi, lo, k0, nk, width, total_k, *waits):
        def mm(e, j, whi, wlo):
            for t, b in enumerate(banks):
                tok = slice(t * P, (t + 1) * P)
                out = self.bank[b][:, 0:width]
                for n in range(nk):
                    k, w = k0 + n, slice(n * width, (n + 1) * width)
                    e.matmul(out, hi[:, k, tok], whi[:, w], start=(k == 0), stop=False)
                    e.matmul(out, lo[:, k, tok], whi[:, w], start=False, stop=False)
                    i = e.matmul(out, hi[:, k, tok], wlo[:, w], start=False, stop=(k == total_k - 1))
            return i
        if k0 == 0:
            waits = (*waits, *(self.bank_free(b) for b in banks))
        return self.take(mm, *waits)

    def split(self, hi, lo, src, *waits):
        a = self.act.do(lambda e, j: e.activation(hi(j), src(j), ACT.Copy), *waits)
        return self.dve.do(lambda e, j: e.tensor_tensor(lo(j), src(j), hi(j).bitcast(F32), ALU.subtract), a)


def program(nc, t):
    plan = stream_plan()
    m = Machine(nc, len(plan), t["stream"])
    pe, act, dve, pool, sp = m.pe, m.act, m.dve, m.pool, m.sp
    prog, last, mark, place, bank = m.prog, m.prog.last, m.prog.mark, m.place, m.bank

    consts = place("consts", 48, [P, len(CONSTS), P])
    cols = place("cols", 53.5, [P, NCOLS])
    small = place("small", 55, [P, 256])
    C = {n: consts[:, i, :] for i, n in enumerate(CONSTS)}
    ident, ones = C["ident"], C["ones"]
    epsc = small[:, 255:256]

    def col(name, i=0):
        return cols[:, COL_AT[name] + i:COL_AT[name] + i + 1]

    hhi, hlo = place("hhi", 56, [P, KT, S], F32R), place("hlo", 72, [P, KT, S], F32R)
    resid = place("resid", 88, [P, KT, S])
    sig = [place(f"sig{i}", 200 + 2 * i, [P, S]) for i in range(2)]
    prod = place("prod", 204, [P, S])

    got_consts = m.fetch("in_consts", consts[:], t["consts"])
    got_cols = m.fetch("in_cols", cols[:], t["cols"])
    x0 = place("x0", 104, [P, KT, S])
    got_x = m.fetch("in_x", x0[:], t["xT"])
    m.start_stream()
    eps_set = dve.do(lambda e, j: e.memset(epsc, EPS))

    def norm(src, n, hi, lo, gain, shift, sq, r, *ready):
        ev = None
        for k in range(KT):
            q = sq[k % 2]
            a = act.do(lambda e, j, k=k, q=q: e.activation(q[:, 0:n], src[:, k, 0:n], ACT.Square),
                       *ready, last(f"sq{k % 2} read"))
            ev = pe.do(lambda e, j, k=k, q=q: e.matmul(bank[7][:, 0:n], ones, q[:, 0:n], start=(k == 0), stop=(k == KT - 1)),
                       a, got_consts, m.bank_free(7))
            mark(f"sq{k % 2} read", ev)
        a = act.do(lambda e, j: e.activation(r[:, 0:n], bank[7][:, 0:n], ACT.Sqrt, bias=epsc, scale=1.0 / D), ev, eps_set)
        m.free_bank(7, a)
        rr = dve.do(lambda e, j: e.reciprocal(r[:, 0:n], r[:, 0:n]), a, got_cols)
        for k in range(KT):
            q = sq[k % 2]
            if hi is None:
                dve.do(lambda e, j, k=k: e.scalar_tensor_tensor(lo[:, k, 0:n], src[:, k, 0:n], gain(k), r[:, 0:n], ALU.mult, ALU.mult), rr)
                continue
            v = dve.do(lambda e, j, k=k, q=q: e.scalar_tensor_tensor(q[:, 0:n], src[:, k, 0:n], gain(k), r[:, 0:n], ALU.mult, ALU.mult),
                       rr, last(f"sq{k % 2} read"))
            if shift is not None:
                v = dve.do(lambda e, j, k=k, q=q: e.tensor_scalar(q[:, 0:n], q[:, 0:n], shift(k), None, ALU.add), v)
            mark(f"sq{k % 2} read", m.split(lambda j, k=k: hi[:, k, 0:n], lambda j, k=k: lo[:, k, 0:n],
                                            lambda j, q=q: q[:, 0:n], v))

    def dve_now():
        return Event(dve.counter, dve.counter.n)

    def act_now():
        return Event(act.counter, act.counter.n)

    def pe_now():
        return Event(pe.counter, pe.counter.n)

    def used_now():
        return Event(m.used, m.used.n)

    sq = [place(f"sqa{i}", 120 + 2 * i, [P, S]) for i in range(2)]
    norm(x0, S, hhi, hlo, lambda k: col("g_mix", k), None, sq, place("ra", 124, [P, S]), got_x)
    h_ready = dve_now()

    q = place("sb_q", 104, [P, KT, S])
    k_ = place("sb_k", 120, [P, KT, S])
    v = place("sb_v", 136, [P, TT, D])
    yhi, ylo = place("sb_yhi", 104, [P, KT, S], F32R), place("sb_ylo", 120, [P, KT, S], F32R)
    spl = place("sb_sp", 152, [P, 1280])
    att = place("sb_att", 157, [P, 1280])
    tmp = place("sb_tmp", 162, [P, 1280])
    tm2 = place("sb_tm2", 167, [P, 1280])

    def tiles_to(dst, scale, hi, lo, base=0, cols_=S, count=SLOTS):
        for u in range(count):
            b = prog.chunk % 4
            w = m.product_tile(b, hi, lo, h_ready, cols=cols_)
            ev = act.do(lambda e, j, u=u, b=b: e.activation(dst[:, j * SLOTS + (u + base), 0:cols_], bank[b][:, 0:cols_], ACT.Copy, scale=scale), w)
            m.free_bank(b, ev)

    def rows_to(hi, lo, width, toks, store):
        nk = CHUNK // width
        for k0 in range(0, KT, nk):
            w = m.product_rows(list(range(toks)), hi, lo, k0, nk, width, KT, h_ready)
        for tt in range(toks):
            m.free_bank(tt, store(tt, bank[tt][:, 0:width], w))

    tiles_to(q, SB_HD ** -0.5, hhi, hlo)
    tiles_to(q, SB_HD ** -0.5, hhi, hlo, base=4)
    prog.loop_of(2, SLOTS, lambda: tiles_to(k_, 1.0, hhi, hlo))
    prog.loop_of(2, SLOTS, lambda: rows_to(hhi, hlo, 512, TT, lambda tt, ps, w: act.do(
        lambda e, j: e.activation(v[:, tt, bass.ds(j * 512, 512)], ps, ACT.Copy), w)))
    sb_in = act_now()

    CUT = [0, 512, 896, 1152, 1280]
    kst = place("sb_kst", 172, [P, S])
    vst = place("sb_vst", 174, [P, TT, P])

    def span(c):
        return slice(CUT[c], CUT[c + 1])

    def diag(c):
        return slice(CUT[c], CUT[c] + P)

    def sb_head():
        ks = dve.do(lambda e, j: e.tensor_copy(kst[:], k_[:, j, :]), sb_in, last("sb kst read"))
        vs = dve.do(lambda e, j: e.tensor_copy(vst[:], v[:, :, bass.ds(j * P, P)]), sb_in, last("sb vst read"))
        for c in range(TT):
            z = pe.do(lambda e, j, c=c: e.matmul(bank[4 + c][:, 0:S - P * c], kst[:, c * P:(c + 1) * P], q[:, j, c * P:S],
                                                 start=True, stop=False, skip_group_check=True), ks, m.bank_free(4 + c))
        mark("sb kst read", z)
        for c in range(TT):
            a = act.do(lambda e, j, c=c: e.activation(tmp[:, span(c)], bank[4 + c][:, 0:S - P * c], ACT.Abs), z, last("sb tmp read"))
        a = act.do(lambda e, j: e.activation(tmp[:], tmp[:], ACT.Exp, scale=-1.0), a)
        a = act.do(lambda e, j: e.activation(tmp[:], tmp[:], ACT.Ln, bias=1.0), a)
        for c in range(TT):
            s1 = dve.do(lambda e, j, c=c: e.scalar_tensor_tensor(spl[:, span(c)], bank[4 + c][:, 0:S - P * c], 0.0, tmp[:, span(c)],
                                                                 ALU.max, ALU.add), a, last("sb spl read"))
        mark("sb tmp read", s1)
        for c in range(TT):
            s2 = dve.do(lambda e, j, c=c: e.tensor_tensor(spl[:, diag(c)], spl[:, diag(c)], C["keep_before"], ALU.mult), s1, got_consts)
        for c in range(TT):
            def sums(e, j, c=c):
                out = bank[4 + c]
                e.matmul(out[:, 0:P], ident, C["hide_not_before"], start=False, stop=False, skip_group_check=True)
                for jj in range(c, TT):
                    i = e.matmul(out[:, (jj - c) * P:S - P * c], C["neg_lower"] if jj == c else C["neg_ones"], spl[:, span(jj)],
                                 start=False, stop=(jj == TT - 1), skip_group_check=True)
                return i
            r = pe.do(sums, s2)
            x = act.do(lambda e, j, c=c: e.activation(att[:, span(c)], bank[4 + c][:, 0:S - P * c], ACT.Exp), r, last("sb att read"))
            m.free_bank(4 + c, x)
        mark("sb spl read", r)
        for c in range(TT):
            y = pe.do(lambda e, j, c=c: e.matmul(bank[3][:, c * P:S], vst[:, c, :], att[:, span(c)], start=(c == 0), stop=(c == TT - 1),
                                                 skip_group_check=True), x, vs, m.bank_free(3))
        mark("sb vst read", y)
        mark("sb att read", y)
        m.free_bank(3, m.split(lambda j: yhi[:, j, :], lambda j: ylo[:, j, :], lambda j: bank[3][:], y))

    prog.loop_of(SB_HEADS, 0, sb_head)

    def gated_projection(branch, bhi, blo, bias, kts=KT, scale_of=None):
        y_ready = dve_now()

        def body():
            for half in range(2):
                b = prog.chunk % 4
                w = m.product_tile(b, hhi, hlo, h_ready)
                g = act.do(lambda e, j, b=b, half=half: e.activation(sig[half][:], bank[b][:], ACT.Sigmoid, bias=bias(j * 2 + half)),
                           w, last(f"sig{half} read"))
                m.free_bank(b, g)
                b = prog.chunk % 4
                w = m.product_tile(b, bhi, blo, y_ready)
                if branch == 0:
                    x = dve.do(lambda e, j, b=b, half=half: e.tensor_tensor(resid[:, j * 2 + half, :], bank[b][:], sig[half][:], ALU.mult), w, g)
                    m.free_bank(b, x)
                else:
                    x = dve.do(lambda e, j, b=b, half=half: e.tensor_tensor(prod[:], bank[b][:], sig[half][:], ALU.mult), w, g, last("prod read"))
                    m.free_bank(b, x)
                    mark("prod read", dve.do(lambda e, j, half=half: e.tensor_tensor(resid[:, j * 2 + half, :], resid[:, j * 2 + half, :], prod[:], ALU.add), x))
                mark(f"sig{half} read", x)
        prog.loop_of(KT // 2, SLOTS, body)

    def colj(name, i):
        return cols[:, bass.ds(i + COL_AT[name], 1)]

    gated_projection(0, yhi, ylo, lambda i: colj("b_gate", i))

    sb_done = used_now()
    mq = place("ml_q", 104, [P, KT, S])
    mk = place("ml_k", 120, [P, KT, S])
    hm = place("ml_hm", 120, [P, ML_HEADS, TT, ML_HD])
    mv = place("ml_v", 136, [P, TT, ML_HEADS, ML_HD + 1])
    mo = place("ml_o", 152.25, [P, KT, S])
    wgt = place("ml_w", 168.5, [P, 1280])
    pmat = place("ml_p", 173.5, [P, 1280])
    kst2 = place("ml_kst", 178.5, [P, 2, S])
    rows = [place(f"ml_row{i}", 182.5 + 2 * i, [P, S]) for i in range(4)]
    pad = [place(f"ml_pad{i}", 182.5 + 2.25 * i, [P, S + 3]) for i in range(2)]
    acc = [place(f"ml_acc{i}", 187 + 2 * i, [P, S]) for i in range(2)]
    csig = place("ml_csig", 191, [P, S])
    selst = place("ml_sel", 193, [P, P])
    dg = place("ml_dg", 193.5, [P, TT, P])
    hst = place("ml_hst", 195.5, [P, TT, ML_HD])
    sqs = place("ml_sqs", 199.5, [P, 128])
    mhi, mlo = place("ml_yhi", 104, [P, KT, S], F32R), place("ml_ylo", 136, [P, KT, S], F32R)

    for i in range(2):
        zero = dve.do(lambda e, j, i=i: e.memset(pad[i][:, 0:3], 0.0), sb_done)
    onescol = dve.do(lambda e, j: e.memset(mv[:, :, :, ML_HD:ML_HD + 1], 1.0), sb_done)

    def conv_tiles(dst, first):
        for u in range(SLOTS):
            b, p = prog.chunk % 4, u % 2
            w = m.product_tile(b, hhi, hlo, h_ready)
            a = act.do(lambda e, j, b=b, p=p: e.activation(pad[p][:, 3:S + 3], bank[b][:], ACT.Copy), w, zero, last(f"pad{p} read"))
            m.free_bank(b, a)
            x = dve.do(lambda e, j, u=u, p=p: e.tensor_scalar(acc[p][:], pad[p][:, 0:S], colj("conv_w", j * SLOTS + (u + first)),
                                                              colj("conv_b", j * SLOTS + (u + first)), ALU.mult, ALU.add), a, last(f"acc{p} read"))
            for tap in range(1, 4):
                x = dve.do(lambda e, j, u=u, p=p, tap=tap: e.scalar_tensor_tensor(
                    acc[p][:], pad[p][:, tap:tap + S], colj("conv_w", j * SLOTS + (u + first + 16 * tap)), acc[p][:], ALU.mult, ALU.add), x)
            mark(f"pad{p} read", x)
            a = act.do(lambda e, j, p=p: e.activation(csig[:], acc[p][:], ACT.Sigmoid), x, last("csig read"))
            x = dve.do(lambda e, j, u=u, p=p: e.tensor_tensor(dst[:, j * SLOTS + u, :], acc[p][:], csig[:], ALU.mult), a, sb_done)
            mark(f"acc{p} read", x)
            mark("csig read", x)

    prog.loop_of(2, SLOTS, lambda: conv_tiles(mq, 0))
    prog.loop_of(2, SLOTS, lambda: conv_tiles(mk, 8))
    conv_done = dve_now()
    prog.loop_of(2, SLOTS, lambda: rows_to(hhi, hlo, 512, TT, lambda tt, ps, w: act.do(
        lambda e, j: e.activation(mv[:, tt, bass.ds(j * 2, 2), 0:ML_HD], ps.rearrange("p (h d) -> p h d", h=2), ACT.Copy), w, sb_done)))

    def out_gate_tiles():
        for u in range(SLOTS):
            b = prog.chunk % 4
            w = m.product_tile(b, hhi, hlo, h_ready)
            m.free_bank(b, act.do(lambda e, j, u=u, b=b: e.activation(mo[:, j * SLOTS + u, :], bank[b][:], ACT.Sigmoid), w, sb_done))
    prog.loop_of(2, SLOTS, out_gate_tiles)

    bi = prog.chunk % 4
    wi = m.product_tile(bi, hhi, hlo, h_ready)
    bf = prog.chunk % 4
    wf = m.product_tile(bf, hhi, hlo, h_ready)
    r_i, r_f, r_t, r_a = rows
    f1 = act.do(lambda e, j: e.activation(r_f[:], bank[bf][:], ACT.Identity, bias=col("b_f")), wf, conv_done)
    i1 = act.do(lambda e, j: e.activation(r_i[:], bank[bi][:], ACT.Identity, bias=col("b_i")), wi, conv_done)
    m.free_bank(bi, i1)
    m.free_bank(bf, f1)
    a = act.do(lambda e, j: e.activation(r_t[:], r_f[:], ACT.Abs), f1, i1)
    a = act.do(lambda e, j: e.activation(r_t[:], r_t[:], ACT.Exp, scale=-1.0), a)
    a = act.do(lambda e, j: e.activation(r_t[:], r_t[:], ACT.Ln, bias=1.0), a)
    x = dve.do(lambda e, j: e.scalar_tensor_tensor(r_f[:], r_f[:], 0.0, r_t[:], ALU.min, ALU.subtract), a)
    x1 = dve.do(lambda e, j: e.memset(r_a[:], 1.0), conv_done)
    x = dve.do(lambda e, j: e.tensor_tensor_scan(r_t[:], r_a[:], r_f[:], 0.0, ALU.mult, ALU.add), x, x1)
    x = dve.do(lambda e, j: e.tensor_tensor(r_i[:], r_i[:], r_t[:], ALU.subtract), x)
    x = dve.do(lambda e, j: e.tensor_tensor_scan(r_f[:], r_a[:], r_i[:], 0.0, ALU.mult, ALU.max), x)
    x = dve.do(lambda e, j: e.tensor_tensor(r_t[:], r_t[:], r_f[:], ALU.add), x)
    acol = small[:, 0:16].rearrange("p (t h) -> p t h", t=TT)
    gcol = small[:, 16:32].rearrange("p (t h) -> p t h", t=TT)
    for tt in range(TT):
        ta = pe.do(lambda e, j, tt=tt: e.transpose(bank[4][:, tt * P:(tt + 1) * P], r_i[:, tt * P:(tt + 1) * P], ident), x, m.bank_free(4))
        tg = pe.do(lambda e, j, tt=tt: e.transpose(bank[5][:, tt * P:(tt + 1) * P], r_t[:, tt * P:(tt + 1) * P], ident), x, m.bank_free(5))
    ac = act.do(lambda e, j: e.activation(acol, bank[4][:].rearrange("p (t c) -> p t c", t=TT)[:, :, 0:ML_HEADS], ACT.Copy), tg)
    m.free_bank(4, ac)
    gc = act.do(lambda e, j: e.activation(gcol, bank[5][:].rearrange("p (t c) -> p t c", t=TT)[:, :, 0:ML_HEADS], ACT.Exp, scale=-1.0), tg)
    m.free_bank(5, gc)
    ml_in = act_now()

    ssq = small[:, 32:48]
    den = small[:, 48:52]
    rden = small[:, 52:56]

    def ml_head():
        sl = dve.do(lambda e, j: e.tensor_copy(selst[:], consts[:, j + CONSTS.index("sel0"), :]), last("selst read"))
        ks = dve.do(lambda e, j: e.tensor_copy(kst2[:], mk[:, bass.ds(j * 2, 2), :]), conv_done, last("ml kst read"))
        mx = pe.do(lambda e, j: e.matmul(bank[3][:], selst[:], r_f[:], start=True, stop=True), sl, ml_in, m.bank_free(3))
        mark("selst read", mx)
        for c in range(TT):
            def scores(e, j, c=c):
                for k in range(2):
                    i = e.matmul(bank[4 + c][:, 0:S - P * c], kst2[:, k, c * P:(c + 1) * P], mq[:, j * 2 + k, c * P:S],
                                 start=(k == 0), stop=(k == 1))
                return i
            sc = pe.do(scores, ks, m.bank_free(4 + c))
        mark("ml kst read", sc)
        for c in range(TT):
            d = dve.do(lambda e, j, c=c: e.tensor_tensor(dg[:, c, :], bank[3][:, c * P:(c + 1) * P], C["hide_after"], ALU.add), mx, last("dg read"))
        for c in range(TT):
            a = act.do(lambda e, j, c=c: e.activation(wgt[:, diag(c)], dg[:, c, :], ACT.Exp, bias=small[:, bass.ds(j + c * 4, 1)]),
                       d, ac, last("wgt read"))
            if c < TT - 1:
                a = act.do(lambda e, j, c=c: e.activation(wgt[:, CUT[c] + P:CUT[c + 1]], bank[3][:, (c + 1) * P:S], ACT.Exp,
                                                          bias=small[:, bass.ds(j + c * 4, 1)]))
        mark("dg read", a)
        m.free_bank(3, a)
        for c in range(TT):
            x = dve.do(lambda e, j, c=c: e.scalar_tensor_tensor(pmat[:, span(c)], bank[4 + c][:, 0:S - P * c], ML_HD ** -0.5, wgt[:, span(c)],
                                                                ALU.mult, ALU.mult), sc, a, last("pmat read"))
        mark("wgt read", x)
        for i in range(TT):
            def sums(e, j, i=i):
                for c in range(i + 1):
                    at = CUT[c] + (i - c) * P
                    ins = e.matmul(bank[4 + i][:, 0:ML_HD + 1], pmat[:, at:at + P], mv[:, c, j, :], start=(c == 0), stop=(c == i))
                return ins
            n = pe.do(sums, x, onescol)
            d = act.do(lambda e, j, i=i: e.activation(den[:, i:i + 1], bank[4 + i][:, ML_HD:ML_HD + 1], ACT.Abs), n, last("den read"))
            d = dve.do(lambda e, j, i=i: e.tensor_scalar(den[:, i:i + 1], den[:, i:i + 1], small[:, bass.ds(j + (16 + i * 4), 1)], None, ALU.max), d, gc)
            d = dve.do(lambda e, j, i=i: e.reciprocal(rden[:, i:i + 1], den[:, i:i + 1]), d, last("rden read"))
            a = act.do(lambda e, j, i=i: e.activation(hm[:, j, i, :], bank[4 + i][:, 0:ML_HD], ACT.Copy, scale=rden[:, i:i + 1]), d, ks)
            m.free_bank(4 + i, a)
            a2 = act.do(lambda e, j, i=i: e.activation(hst[:, i, :], hm[:, j, i, :], ACT.Square, accum_out=small[:, bass.ds(j + (32 + i * 4), 1)]), a, last("hst read"))
        mark("rden read", a)
        mark("den read", d)
        mark("hst read", a2)
        mark("pmat read", n)

    prog.loop_of(ML_HEADS, 0, ml_head)
    a = act.do(lambda e, j: e.activation(ssq, ssq, ACT.Sqrt, bias=epsc, scale=1.0 / ML_HD), act_now())
    rms = dve.do(lambda e, j: e.reciprocal(ssq, ssq), a)
    v_read = pe_now()

    def ml_out():
        for i in range(TT):
            x = dve.do(lambda e, j, i=i: e.tensor_scalar(hst[:, i, :], hm[:, j, i, :], small[:, bass.ds(j + (32 + i * 4), 1)], None, ALU.mult),
                       rms, last("hst turned"))
        for c in range(2):
            def turn(e, j, c=c):
                for i in range(TT):
                    ins = e.transpose(bank[4 + c][:, i * P:(i + 1) * P], hst[:, i, c * P:(c + 1) * P], ident)
                return ins
            tr = pe.do(turn, x, m.bank_free(4 + c))
            y = dve.do(lambda e, j, c=c: e.scalar_tensor_tensor(rows[c][:], bank[4 + c][:], colj("ml_norm_g", j * 2 + c), mo[:, j * 2 + c, :],
                                                                ALU.mult, ALU.mult), tr, v_read, last(f"row{c} read"))
            m.free_bank(4 + c, y)
            mark(f"row{c} read", m.split(lambda j, c=c: mhi[:, j * 2 + c, :], lambda j, c=c: mlo[:, j * 2 + c, :], lambda j, c=c: rows[c][:], y))
        mark("hst turned", tr)

    prog.loop_of(ML_HEADS, 0, ml_out)
    gated_projection(1, mhi, mlo, lambda i: colj("b_gate", i + 8))

    ml_done = used_now()
    mem = place("x_mem", 104, [P, KT, M])
    memhi, memlo = place("x_memhi", 112, [P, KT, M], F32R), place("x_memlo", 120, [P, KT, M], F32R)
    xk = place("x_k", 128, [P, KT, M])
    xv = place("x_v", 136, [P, MT, D])
    xq = place("x_q", 144, [P, KT, S])
    xhi, xlo = place("x_yhi", 144, [P, KT, S], F32R), place("x_ylo", 160, [P, KT, S], F32R)
    xsq = place("x_sq", 176, [P, 2, S])
    xqst = place("x_qst", 180, [P, 2, S])
    xvst = place("x_vst", 184, [P, MT, X_HD])
    xp = place("x_p", 186, [P, TT, M])
    xpt = place("x_pt", 190, [P, MT, S])
    xr = place("x_r", 194, [P, S])
    xs = [place(f"x_s{i}", 196 + 2 * i, [P, S]) for i in range(2)]
    got_mem = m.fetch("in_mem", mem[:], t["memT"], ml_done)
    norm(mem, M, memhi, memlo, lambda k: col("g_mem", k), None, xs, xr, got_mem, ml_done)
    mem_ready = dve_now()

    def mem_tiles(dst, hi, lo, ready, scale=None):
        for u in range(SLOTS):
            b = prog.chunk % 4
            w = m.product_tile(b, hi, lo, ready, cols=M)
            m.free_bank(b, act.do(lambda e, j, u=u, b=b: e.activation(dst[:, j * SLOTS + u, :], bank[b][:, 0:M], ACT.Copy), w, ml_done))
    prog.loop_of(2, SLOTS, lambda: mem_tiles(xk, memhi, memlo, mem_ready))

    def mem_rows():
        for k0 in range(0, KT, 2):
            w = m.product_rows([0, 1], memhi, memlo, k0, 2, 512, KT, mem_ready)
        for tt in range(MT):
            m.free_bank(tt, act.do(lambda e, j, tt=tt: e.activation(xv[:, tt, bass.ds(j * 512, 512)], bank[tt][:], ACT.Copy), w, ml_done))
    prog.loop_of(2, SLOTS, mem_rows)
    prog.loop_of(2, SLOTS, lambda: tiles_to(xq, 1.0, hhi, hlo))
    xq_done = act_now()

    gqk = small[:, 64:66]
    x = dve.do(lambda e, j: e.tensor_tensor(gqk, cols[:, COL_AT["q_norm_g"]:COL_AT["q_norm_g"] + 2],
                                            cols[:, COL_AT["k_norm_g"]:COL_AT["k_norm_g"] + 2], ALU.mult))
    gqk_set = dve.do(lambda e, j: e.tensor_scalar(gqk, gqk, X_HD ** -0.5, None, ALU.mult), x)

    def x_norms():
        a = act.do(lambda e, j: e.activation(xsq[:, :, 0:M], xk[:, bass.ds(j * 2, 2), :], ACT.Square), xq_done, last("xsq read"))

        def over_head(e, j):
            for k in range(2):
                i = e.matmul(bank[4][:, 0:M], ones, xsq[:, k, 0:M], start=(k == 0), stop=(k == 1))
            return i
        s_ = pe.do(over_head, a, m.bank_free(4))
        a = act.do(lambda e, j: e.activation(xr[:, 0:M], bank[4][:, 0:M], ACT.Sqrt, bias=epsc, scale=1.0 / X_HD), s_, last("xr read"))
        m.free_bank(4, a)
        x = dve.do(lambda e, j: e.reciprocal(xr[:, 0:M], xr[:, 0:M]), a)
        for k in range(2):
            x = dve.do(lambda e, j, k=k: e.scalar_tensor_tensor(xk[:, j * 2 + k, :], xk[:, j * 2 + k, :], gqk[:, k:k + 1], xr[:, 0:M],
                                                                ALU.mult, ALU.mult), x, gqk_set)
        mark("xr read", x)
        a = act.do(lambda e, j: e.activation(xsq[:], xq[:, bass.ds(j * 2, 2), :], ACT.Square), s_)

        def columns(e, j):
            for tt in range(TT):
                for k in range(2):
                    i = e.matmul(bank[5][:, tt:tt + 1], xsq[:, k, tt * P:(tt + 1) * P], ones[:, 0:1], start=(k == 0), stop=(k == 1))
            return i
        c = pe.do(columns, a, m.bank_free(5))
        mark("xsq read", c)
        m.free_bank(5, act.do(lambda e, j: e.activation(small[:, bass.ds(j * 4 + 68, 4)], bank[5][:, 0:TT], ACT.Sqrt, bias=epsc, scale=1.0 / X_HD), c))
    prog.loop_of(X_HEADS, 0, x_norms)
    rq_set = dve.do(lambda e, j: e.reciprocal(small[:, 68:84], small[:, 68:84]), act_now())

    mxs, nb, rsum, rinv = small[:, 84:88], small[:, 88:92], small[:, 92:96], small[:, 96:100]

    def x_head():
        qs = dve.do(lambda e, j: e.tensor_copy(xqst[:], xq[:, bass.ds(j * 2, 2), :]), rq_set, last("xqst read"))
        vs = dve.do(lambda e, j: e.tensor_copy(xvst[:], xv[:, :, bass.ds(j * X_HD, X_HD)]), last("xvst read"))
        for tt in range(TT):
            def logits(e, j, tt=tt):
                for k in range(2):
                    i = e.matmul(bank[4 + tt][:, 0:M], xqst[:, k, tt * P:(tt + 1) * P], xk[:, j * 2 + k, :], start=(k == 0), stop=(k == 1))
                return i
            lg = pe.do(logits, qs, m.bank_free(4 + tt))
            x = dve.do(lambda e, j, tt=tt: e.tensor_reduce(mxs[:, tt:tt + 1], bank[4 + tt][:, 0:M], AX, ALU.max), lg, last("mxs read"))
        mark("xqst read", lg)
        x = dve.do(lambda e, j: e.scalar_tensor_tensor(nb, mxs, -1.0, small[:, bass.ds(j * 4 + 68, 4)], ALU.mult, ALU.mult), x, last("nb read"))
        mark("mxs read", x)
        for tt in range(TT):
            a = act.do(lambda e, j, tt=tt: e.activation(xp[:, tt, :], bank[4 + tt][:, 0:M], ACT.Exp, bias=nb[:, tt:tt + 1],
                                                        scale=small[:, bass.ds(j * 4 + (68 + tt), 1)], accum_out=rsum[:, tt:tt + 1]), x, last("xp read"))
            m.free_bank(4 + tt, a)
        mark("nb read", a)
        x = dve.do(lambda e, j: e.reciprocal(rinv, rsum), a)
        for tt in range(TT):
            x2 = dve.do(lambda e, j, tt=tt: e.tensor_scalar(xp[:, tt, :], xp[:, tt, :], rinv[:, tt:tt + 1], None, ALU.mult), x)
        for mt in range(MT):
            def turn(e, j, mt=mt):
                for tt in range(TT):
                    i = e.transpose(bank[4 + mt][:, tt * P:(tt + 1) * P], xp[:, tt, mt * P:(mt + 1) * P], ident)
                return i
            tr = pe.do(turn, x2, m.bank_free(4 + mt))
            a = act.do(lambda e, j, mt=mt: e.activation(xpt[:, mt, :], bank[4 + mt][:], ACT.Copy), tr, last("xpt read"))
            m.free_bank(4 + mt, a)
        mark("xp read", tr)
        for c in range(2):
            def out(e, j, c=c):
                for mt in range(MT):
                    i = e.matmul(bank[6 + c][:], xvst[:, mt, c * P:(c + 1) * P], xpt[:, mt, :], start=(mt == 0), stop=(mt == MT - 1))
                return i
            y = pe.do(out, a, vs, m.bank_free(6 + c))
            m.free_bank(6 + c, m.split(lambda j, c=c: xhi[:, j * 2 + c, :], lambda j, c=c: xlo[:, j * 2 + c, :], lambda j, c=c: bank[6 + c][:], y))
        mark("xpt read", y)
        mark("xvst read", y)
    prog.loop_of(X_HEADS, 0, x_head)
    gated_projection(2, xhi, xlo, lambda i: colj("b_gate", i + 16))

    x_done = used_now()
    mixhi, mixlo = place("mixhi", 104, [P, KT, S], F32R), place("mixlo", 120, [P, KT, S], F32R)

    def split_all(hi, lo, src, n, *waits):
        def body():
            m.split(lambda j: hi[:, j, :], lambda j: lo[:, j, :], lambda j: src[:, j, :], *waits)
        prog.loop_of(n, 0, body)
        return dve_now()
    mix_ready = split_all(mixhi, mixlo, resid, KT, dve_now(), x_done)
    got_x = m.fetch("in_x_again", resid[:], t["xT"], mix_ready)

    def add_tiles(hi, lo, ready, *waits):
        for u in range(SLOTS):
            b = prog.chunk % 4
            w = m.product_tile(b, hi, lo, ready)
            m.free_bank(b, dve.do(lambda e, j, u=u, b=b: e.tensor_tensor(resid[:, j * SLOTS + u, :], bank[b][:], resid[:, j * SLOTS + u, :], ALU.add),
                                  w, *waits))
    prog.loop_of(2, SLOTS, lambda: add_tiles(mixhi, mixlo, mix_ready, got_x))

    out_done = used_now()
    sqb = [place(f"sqb{i}", 136 + 2 * i, [P, S]) for i in range(2)]
    norm(resid, S, hhi, hlo, lambda k: col("g_mlp", k), None, sqb, place("rb", 140, [P, S]), dve_now(), out_done)
    h_ready = dve_now()
    HALF = FF_TILES // 2
    uhi, ulo = place("ff_uhi", 104, [P, HALF, S], F32R), place("ff_ulo", 136, [P, HALF, S], F32R)
    fr = [place(f"ff_r{i}", 168 + 2 * i, [P, S]) for i in range(2)]
    ft = [place(f"ff_t{i}", 172 + 2 * i, [P, S]) for i in range(2)]

    def up_tiles(ready, free):
        for u in range(SLOTS):
            b, p = prog.chunk % 4, u % 2
            w = m.product_tile(b, hhi, hlo, ready)
            a = act.do(lambda e, j, b=b, p=p: e.activation(fr[p][:], bank[b][:], ACT.Relu), w, last(f"fr{p} read"))
            m.free_bank(b, a)
            x = dve.do(lambda e, j, p=p: e.tensor_tensor(ft[p][:], fr[p][:], fr[p][:], ALU.mult), a, last(f"ft{p} read"))
            mark(f"fr{p} read", x)
            mark(f"ft{p} read", m.split(lambda j, u=u: uhi[:, j * SLOTS + u, :], lambda j, u=u: ulo[:, j * SLOTS + u, :], lambda j, p=p: ft[p][:], x, free))

    def down(hi, lo, nk, ready, finish):
        for n in range(nk // 2):
            def mm(e, j, whi, wlo, n=n):
                for o in range(4):
                    for kk in range(2):
                        k, w = 2 * n + kk, slice((kk * 4 + o) * P, (kk * 4 + o + 1) * P)
                        e.matmul(bank[o][:], whi[:, w], hi[:, k, :], start=(k == 0), stop=False)
                        e.matmul(bank[o][:], whi[:, w], lo[:, k, :], start=False, stop=False)
                        i = e.matmul(bank[o][:], wlo[:, w], hi[:, k, :], start=False, stop=(k == nk - 1))
                return i
            w = m.take(mm, ready, *([m.bank_free(o) for o in range(4)] if n == 0 else []))
        for o in range(4):
            m.free_bank(o, finish(o, w))

    for half in range(2):
        free = used_now()
        prog.loop_of(HALF // SLOTS, SLOTS, lambda: up_tiles(h_ready, free))
        u_ready = dve_now()
        prog.loop_of(2, HALF // 2, lambda: down(uhi, ulo, HALF, u_ready, lambda o, w: dve.do(
            lambda e, j: e.tensor_tensor(resid[:, j * 4 + o, :], bank[o][:], resid[:, j * 4 + o, :], ALU.add), w)))

    ff_done = used_now()
    cact = place("cact", 104, [P, KT, 2])
    csg = place("csg", 104.25, [P, KT, 2])
    crhs = place("crhs", 104.5, [P, KT, 4], F32R)
    mod = place("mod", 202.5, [P, 48, 2])
    gsc = small[:, 100:148]
    cin = cols[:, COL_AT["c"]:COL_AT["c"] + 16].rearrange("p (w k) -> p k w", w=2)
    a = act.do(lambda e, j: e.activation(csg[:], cin, ACT.Sigmoid), ff_done)
    x = dve.do(lambda e, j: e.tensor_tensor(cact[:], csg[:], cin, ALU.mult), a)
    a = act.do(lambda e, j: e.activation(crhs[:, :, 0:2], cact[:], ACT.Copy), x)
    c_ready = dve.do(lambda e, j: e.tensor_tensor(crhs[:, :, 2:4], cact[:], crhs[:, :, 0:2].bitcast(F32), ALU.subtract), a)

    def mod_tiles():
        for u in range(SLOTS):
            b = prog.chunk % 4

            def mm(e, j, whi, wlo, b=b):
                for k in range(KT):
                    w = slice(k * P, (k + 1) * P)
                    e.matmul(bank[b][:, 0:4], whi[:, w], crhs[:, k, :], start=(k == 0), stop=False, skip_group_check=True)
                    i = e.matmul(bank[b][:, 0:2], wlo[:, w], crhs[:, k, 0:2], start=False, stop=(k == KT - 1), skip_group_check=True)
                return i
            w = m.take(mm, m.bank_free(b), c_ready)
            m.free_bank(b, dve.do(lambda e, j, u=u, b=b: e.tensor_reduce(mod[:, j * SLOTS + u, :], bank[b][:, 0:4].rearrange("p (s w) -> p w s", s=2), AX, ALU.add), w))
    prog.loop_of(48 // SLOTS, SLOTS, mod_tiles)
    x = dve_now()
    for w in range(2):
        x = dve.do(lambda e, j, w=w: e.tensor_tensor(mod[:, :, w], mod[:, :, w], cols[:, COL_AT["b_mod"]:COL_AT["b_mod"] + 48], ALU.add), x)
    SH1, SC1, G1, SH2, SC2, G2 = range(0, 48, 8)
    for at, which, gain, scale in ((0, 0, "norm1_g", SC1), (8, 1, "norm1_g", SC1), (16, 0, "norm2_g", SC2)):
        mod_ready = dve.do(lambda e, j, at=at, which=which, gain=gain, scale=scale: e.scalar_tensor_tensor(
            gsc[:, at:at + 8], mod[:, scale:scale + 8, which], 1.0, cols[:, COL_AT[gain]:COL_AT[gain] + 8], ALU.add, ALU.mult), x)

    feats = place("feats", 106, [33, S])
    fw1, fw2, fw3 = place("fw1", 108, [33, 64]), place("fw2", 108.25, [64, 64]), place("fw3", 108.5, [65, 1024])
    fh1, fh2 = place("fh1", 112.5, [64, S]), place("fh2", 114.5, [65, S])
    fa, fb = place("fa", 116.5, [64, S]), place("fb", 118.5, [64, S])
    filt = place("filt", 120.5, [P, TT, 1024])
    window = place("window", 138, [P, TT, MIX])
    fabs = place("fabs", 142, [P, 1024])
    fnorm = place("fnorm", 146, [P, 512])
    psum_, pdif = place("fsum", 148, [P, TT, 512]), place("fdif", 156, [P, TT, 512])
    fsh, fsl, fdh, fdl = (place(n, k, [P, TT, 512], F32R) for n, k in (("fsh", 164), ("fsl", 172), ("fdh", 180), ("fdl", 188)))
    kr, ks_ = place("hy_kr", 138, [P, TT, 512]), place("hy_ks", 146, [P, TT, 512])
    kt_ = place("hy_kt", 196, [P, 512])
    got = [m.fetch(f"in_f{i}", dst, t[src], ff_done) for i, (dst, src) in enumerate(
        ((feats[:], "feats"), (fw1[:], "filt_w1"), (fw2[:], "filt_w2"), (fw3[:], "filt_w3"), (window[:], "window")))]
    one_row = dve.do(lambda e, j: e.memset(fh2[64:65, :], 1.0), ff_done)

    def sine(dst, ps, bias, *waits):
        f = cols[0:64, COL_AT["freq"]:COL_AT["freq"] + 1]
        x = dve.do(lambda e, j: e.tensor_scalar(fa[:], ps, bias, f, ALU.add, ALU.mult), *waits)
        x = dve.do(lambda e, j: e.tensor_scalar(fb[:], fa[:], 1.0 / TWO_PI, ROUND, ALU.mult, ALU.add), x)
        x = dve.do(lambda e, j: e.tensor_scalar(fb[:], fb[:], -ROUND, None, ALU.add), x)
        for part in TWO_PI_PARTS:
            x = dve.do(lambda e, j, part=part: e.scalar_tensor_tensor(fa[:], fb[:], -part, fa[:], ALU.mult, ALU.add), x)
        x = dve.do(lambda e, j: e.tensor_scalar(fa[:], fa[:], PI_BELOW, -PI_BELOW, ALU.min, ALU.max), x)
        return act.do(lambda e, j: e.activation(dst, fa[:], ACT.Sin), x)

    p1 = pe.do(lambda e, j: e.matmul(bank[4][0:64, :], fw1[:], feats[:], start=True, stop=True), got[0], got[1], m.bank_free(4))
    s1 = sine(fh1[:], bank[4][0:64, :], cols[0:64, COL_AT["filt_b1"]:COL_AT["filt_b1"] + 1], p1)
    p2 = pe.do(lambda e, j: e.matmul(bank[5][0:64, :], fw2[:], fh1[:], start=True, stop=True), s1, got[2], m.bank_free(5))
    s2 = sine(fh2[0:64, :], bank[5][0:64, :], cols[0:64, COL_AT["filt_b2"]:COL_AT["filt_b2"] + 1], p2)
    m.free_bank(4, s2)
    m.free_bank(5, s2)
    for tt in range(TT):
        for half in range(2):
            b = 4 + half
            p3 = pe.do(lambda e, j, tt=tt, half=half, b=b: e.matmul(bank[b][:], fh2[:, tt * P:(tt + 1) * P], fw3[:, half * 512:(half + 1) * 512],
                                                                    start=True, stop=True), s2, one_row, got[3], m.bank_free(b))
            for dd in range(2):
                x = dve.do(lambda e, j, tt=tt, half=half, b=b, dd=dd: e.tensor_tensor(
                    filt[:, tt, half * 512 + dd * MIX:half * 512 + (dd + 1) * MIX], bank[b][:, dd * MIX:(dd + 1) * MIX], window[:, tt, :], ALU.mult), p3, got[4])
            m.free_bank(b, x)
        a = act.do(lambda e, j, tt=tt: e.activation(fabs[:], filt[:, tt, :], ACT.Abs), x, last("fabs read"))
        for half in range(2):
            b = 6 + half
            n = pe.do(lambda e, j, tt=tt, half=half, b=b: e.matmul(bank[b][:], ones, fabs[:, half * 512:(half + 1) * 512],
                                                                   start=(tt == 0), stop=(tt == TT - 1)), a, *([m.bank_free(b)] if tt == 0 else []))
        mark("fabs read", n)
    filt_made = x
    for o in range(2):
        a = act.do(lambda e, j, o=o: e.activation(fnorm[:, o * MIX:(o + 1) * MIX], bank[6 + o][:, 0:MIX], ACT.Copy), n)
        x = dve.do(lambda e, j, o=o: e.scalar_tensor_tensor(fnorm[:, o * MIX:(o + 1) * MIX], bank[6 + o][:, MIX:2 * MIX], EPS,
                                                            fnorm[:, o * MIX:(o + 1) * MIX], ALU.add, ALU.add), a)
        m.free_bank(6 + o, x)
    inv = dve.do(lambda e, j: e.reciprocal(fnorm[:], fnorm[:]), x)
    hf = filt[:].rearrange("p t (o d c) -> p t o d c", o=2, d=2)
    z0 = None
    for o in range(2):
        z0 = dve.do(lambda e, j, o=o: e.memset(filt[0:1, 0, o * 512 + MIX:(o + 1) * 512], 0.0), n, filt_made)
    for tt in range(TT):
        for o in range(2):
            cs = slice(o * MIX, (o + 1) * MIX)
            fo, ba = slice(o * 512, o * 512 + MIX), slice(o * 512 + MIX, (o + 1) * 512)
            x = dve.do(lambda e, j, tt=tt, cs=cs, fo=fo, ba=ba: e.tensor_tensor(psum_[:, tt, cs], filt[:, tt, fo], filt[:, tt, ba], ALU.add), z0)
            x = dve.do(lambda e, j, tt=tt, cs=cs, fo=fo, ba=ba: e.tensor_tensor(pdif[:, tt, cs], filt[:, tt, fo], filt[:, tt, ba], ALU.subtract), z0)
    m.split(lambda j: fsh[:], lambda j: fsl[:], lambda j: psum_[:], x)
    sd = m.split(lambda j: fdh[:], lambda j: fdl[:], lambda j: pdif[:], x)

    def spectrum(dst, hi, lo):
        for n in range(2):
            def mm(e, j, whi, wlo, n=n):
                for f in range(2):
                    for k in range(TT):
                        w = slice((f * TT + k) * P, (f * TT + k + 1) * P)
                        e.matmul(bank[2 * n + f][:], whi[:, w], hi[:, k, :], start=(k == 0), stop=False)
                        e.matmul(bank[2 * n + f][:], whi[:, w], lo[:, k, :], start=False, stop=False)
                        i = e.matmul(bank[2 * n + f][:], wlo[:, w], hi[:, k, :], start=False, stop=(k == TT - 1))
                return i
            w = m.take(mm, sd, *[m.bank_free(2 * n + f) for f in range(2)])
            for f in range(2):
                m.free_bank(2 * n + f, dve.do(lambda e, j, n=n, f=f: e.tensor_tensor(dst[:, 2 * n + f, :], bank[2 * n + f][:], kt_[:], ALU.mult), w, kn_set))
    kn_set = act.do(lambda e, j: e.activation(kt_[:], fnorm[:], ACT.Copy, scale=1.0 / S), inv)
    spectrum(kr, fsh, fsl)
    spectrum(ks_, fdh, fdl)
    spectra = dve_now()

    ctx = place("ctx", 104, [P, KT, M])
    chi, clo = place("ctxhi", 112, [P, KT, M], F32R), place("ctxlo", 120, [P, KT, M], F32R)
    kctx = place("kctx", 198.25, [P, 2, M])
    vctx = place("vctx", 200.25, [P, MT, MIX])
    sqc = [place(f"sqc{i}", 128 + i, [P, M]) for i in range(2)]
    got_ctx = m.fetch("in_ctx", ctx[:], t["ctxT"], spectra, used_now())
    spec_done = used_now()
    norm(ctx, M, chi, clo, lambda k: gsc[:, 8 + k:9 + k], lambda k: mod[:, SH1 + k, 1:2], sqc, place("rc", 130, [P, M]), got_ctx, mod_ready)
    ctx_ready = dve_now()
    for i in range(2):
        b = prog.chunk % 4
        w = m.product_tile(b, chi, clo, ctx_ready, cols=M)
        m.free_bank(b, act.do(lambda e, j, i=i, b=b: e.activation(kctx[:, i, :], bank[b][:, 0:M], ACT.Copy), w))
    for k0 in (0, 4):
        w = m.product_rows([0, 1], chi, clo, k0, 4, MIX, KT, ctx_ready)
    for tt in range(MT):
        m.free_bank(tt, act.do(lambda e, j, tt=tt: e.activation(vctx[:, tt, :], bank[tt][:, 0:MIX], ACT.Copy), w))
    ctx_done = used_now()

    sqd = [place(f"sqd{i}", 104 + 2 * i, [P, S]) for i in range(2)]
    norm(resid, S, hhi, hlo, lambda k: gsc[:, k:k + 1], lambda k: mod[:, SH1 + k, 0:1], sqd, place("rd", 108, [P, S]), dve_now(), ctx_done, act_now())
    h_ready = dve_now()
    pj = place("proj", 104, [P, 14, S])
    nv = place("na_v", 132, [P, TT, MIX])
    POOL, FNET, HY, NQ, NK = 0, 2, 4, 10, 12
    h_written = act_now()
    for i in range(14):
        b = prog.chunk % 4
        w = m.product_tile(b, hhi, hlo, h_ready)
        m.free_bank(b, act.do(lambda e, j, i=i, b=b: e.activation(pj[:, i, :], bank[b][:], ACT.Copy), w))
    for k0 in (0, 4):
        w = m.product_rows([0, 1, 2, 3], hhi, hlo, k0, 4, MIX, KT, h_ready)
    for tt in range(TT):
        m.free_bank(tt, act.do(lambda e, j, tt=tt: e.activation(nv[:, tt, :], bank[tt][:, 0:MIX], ACT.Copy), w))
    pj_done = act_now()
    yhi2, ylo2 = place("y2hi", 164, [P, 8, S], F32R), place("y2lo", 180, [P, 8, S], F32R)

    LEFT = 8
    plin = [place(f"pl{i}", 154 + 2.25 * i, [P, S + 2 * LEFT]) for i in range(3)]
    counts = place("counts", 160.75, [P, S])
    pw = place("pool_w", 162.75, [P, 2, P])
    cs64 = place("cs64", 196, [P, 2 * P])
    got_counts = m.fetch("in_counts", counts[:], t["pool_counts"][0], spec_done, pj_done)
    got_pw = m.fetch("in_pw", pw[:], t["pool_w"], spec_done, pj_done)
    got_cs = m.fetch("in_cs", cs64[:], t["cs64"], spec_done, pj_done)
    for i in range(2):
        pin, s2t, s4t = plin
        x = dve.do(lambda e, j: e.memset(pin[:, 0:LEFT], 0.0), pj_done, spec_done, last("pool read"))
        x = dve.do(lambda e, j: e.memset(pin[:, S + LEFT:S + 2 * LEFT], 0.0), last("pool read"))
        x = dve.do(lambda e, j, i=i: e.tensor_copy(pin[:, LEFT:S + LEFT], pj[:, POOL + i, :]), x)
        pn = S + 2 * LEFT

        def twice(dst, a_, w, x):
            return dve.do(lambda e, j: e.tensor_tensor(dst[:, 2 * w - 1:pn], a_[:, 2 * w - 1:pn], a_[:, w - 1:pn - w], ALU.add), x)
        if i == 0:
            x = twice(s2t, pin, 1, x)
            x4 = twice(s4t, s2t, 2, x)
            lo_, lo_off, hi_, hi_off = s2t, 0, s4t, 1
        else:
            x = twice(s2t, pin, 1, x)
            x = twice(s4t, s2t, 2, x)
            x = twice(s2t, s4t, 4, x)
            x4 = twice(s4t, s2t, 8, x)
            lo_, lo_off, hi_, hi_off = s2t, 3, s4t, 7
        x = x4
        for part, buf, off in ((slice(0, 64), lo_, lo_off), (slice(64, P), hi_, hi_off)):
            x = dve.do(lambda e, j, part=part, buf=buf, off=off: e.tensor_tensor(
                counts[part, :], buf[part, LEFT + off:LEFT + off + S], counts[part, :], ALU.mult), x, got_counts)
        x = dve.do(lambda e, j, i=i: e.tensor_tensor(counts[:], counts[:], pj[:, POOL + i, :], ALU.subtract), x)
        y = pe.do(lambda e, j, i=i: e.matmul(bank[4 + i][:], pw[:, i, :], counts[:], start=True, stop=True), x, got_pw, m.bank_free(4 + i))
        x = dve.do(lambda e, j, i=i: e.tensor_scalar(pin[:, 0:S], bank[4 + i][:], col("pool_scale", i), None, ALU.mult), y)
        m.free_bank(4 + i, x)
        mark("pool read", m.split(lambda j, i=i: yhi2[:, i, :], lambda j, i=i: ylo2[:, i, :], lambda j: pin[:, 0:S], x))
        if i == 0:
            got_counts = m.fetch("in_counts1", counts[:], t["pool_counts"][1], y)


    vh, vl = place("fn_vh", 172, [P, TT, 512], F32R), place("fn_vl", 188, [P, TT, 512], F32R)
    for tt in range(TT):
        for i in range(2):
            y = pe.do(lambda e, j, tt=tt, i=i: e.matmul(bank[4 + tt][:, i * 256:(i + 1) * 256], pj[:, FNET + i, tt * P:(tt + 1) * P], cs64[:],
                                                        start=(i == 0), stop=(i == 1), skip_group_check=True), pj_done, got_cs, m.bank_free(4 + tt))
        m.free_bank(4 + tt, m.split(lambda j, tt=tt: vh[:, tt, :], lambda j, tt=tt: vl[:, tt, :], lambda j, tt=tt: bank[4 + tt][:], y))
    v_ready = dve_now()

    def positions(sets, ready):
        for s, parts in enumerate(sets):
            for n in range(2):
                def mm(e, j, whi, wlo, s=s, n=n, parts=parts):
                    for i in range(2):
                        for kk in range(2):
                            w = slice(kk * 512, (kk + 1) * 512)
                            vhi, vlo = parts(2 * n + kk, i)
                            e.matmul(bank[i][:], vhi, whi[:, w], start=(s == 0 and n == 0 and kk == 0), stop=False)
                            e.matmul(bank[i][:], vlo, whi[:, w], start=False, stop=False)
                            ins = e.matmul(bank[i][:], vhi, wlo[:, w], start=False, stop=(s == 1 and n == 1 and kk == 1))
                    return ins
                w = m.take(mm, ready, *([m.bank_free(0), m.bank_free(1)] if s == n == 0 else []))
        return w

    def fourier_part(s):
        def part(k, i):
            w = slice(i * 256 + s * P, i * 256 + (s + 1) * P)
            return vh[:, k, w], vl[:, k, w]
        return part
    w = positions([fourier_part(0), fourier_part(1)], v_ready)
    for i in range(2):
        m.free_bank(i, m.split(lambda j, i=i: yhi2[:, 2 + i, :], lambda j, i=i: ylo2[:, 2 + i, :], lambda j, i=i: bank[i][:], w))
    fnet_done = used_now()

    hpad = place("hy_pad", 203, [P, S + 2])
    zh, zl = place("hy_zh", 154, [P, TT, MIX], F32R), place("hy_zl", 158, [P, TT, MIX], F32R)
    zc, zs = place("hy_zc", 104, [P, TT, MIX]), place("hy_zs", 108, [P, TT, MIX])
    t1, t2 = place("hy_t1", 176, [P, TT, MIX]), place("hy_t2", 192, [P, TT, MIX])
    ych, ycl = place("hy_ych", 154, [P, TT, MIX], F32R), place("hy_ycl", 158, [P, TT, MIX], F32R)
    ysh, ysl = place("hy_ysh", 203, [P, TT, MIX], F32R), place("hy_ysl", 172, [P, TT, MIX], F32R)
    x = dve.do(lambda e, j: e.memset(hpad[:, 0:1], 0.0), pj_done)
    x = dve.do(lambda e, j: e.memset(hpad[:, S + 1:S + 2], 0.0), pj_done)
    for i in range(6):
        a = act.do(lambda e, j, i=i: e.activation(hpad[:, 1:S + 1], pj[:, HY + i, :], ACT.Copy), x)
        x = dve.do(lambda e, j, i=i: e.tensor_scalar(pj[:, HY + i, :], hpad[:, 0:S], col("hy_conv_w", i), col("hy_conv_b", i), ALU.mult, ALU.add), a)
        for tap in (1, 2):
            x = dve.do(lambda e, j, i=i, tap=tap: e.scalar_tensor_tensor(pj[:, HY + i, :], hpad[:, tap:tap + S], col("hy_conv_w", 6 * tap + i),
                                                                         pj[:, HY + i, :], ALU.mult, ALU.add), x)
    for order in range(2):
        for i in range(2):
            def turn(e, j, i=i):
                for tt in range(TT):
                    ins = e.transpose(bank[4 + i][:, tt * P:(tt + 1) * P], pj[:, HY + i, tt * P:(tt + 1) * P], ident)
                return ins
            tr = pe.do(turn, x, m.bank_free(4 + i))
            zsrc = lambda j, i=i: bank[4 + i][:].rearrange("p (t c) -> p t c", t=TT)
            m.free_bank(4 + i, m.split(lambda j, i=i: zh[:, :, i * P:(i + 1) * P], lambda j, i=i: zl[:, :, i * P:(i + 1) * P], zsrc, tr, fnet_done, used_now()))
        z_ready = dve_now()
        for s, dst in enumerate((zc, zs)):
            for n in range(2):
                def mm(e, j, whi, wlo, n=n):
                    for f in range(2):
                        for k in range(TT):
                            w = slice((f * TT + k) * P, (f * TT + k + 1) * P)
                            out = bank[2 * n + f][:, 0:MIX]
                            e.matmul(out, whi[:, w], zh[:, k, :], start=(k == 0), stop=False)
                            e.matmul(out, whi[:, w], zl[:, k, :], start=False, stop=False)
                            ins = e.matmul(out, wlo[:, w], zh[:, k, :], start=False, stop=(k == TT - 1))
                    return ins
                w = m.take(mm, z_ready, *[m.bank_free(2 * n + f) for f in range(2)])
                for f in range(2):
                    m.free_bank(2 * n + f, act.do(lambda e, j, dst=dst, n=n, f=f: e.activation(dst[:, 2 * n + f, :], bank[2 * n + f][:, 0:MIX], ACT.Copy),
                                                  w, fnet_done, last("spectrum read")))
        zdone = act_now()
        cs = slice(order * MIX, (order + 1) * MIX)
        for (a1, b1, a2, b2, op, hi, lo) in ((zc, kr, zs, ks_, ALU.subtract, ych, ycl), (zc, ks_, zs, kr, ALU.add, ysh, ysl)):
            x1 = dve.do(lambda e, j, a1=a1, b1=b1, cs=cs: e.tensor_tensor(t1[:], a1[:], b1[:, :, cs], ALU.mult), zdone, last("t1 read"))
            x2 = dve.do(lambda e, j, a2=a2, b2=b2, cs=cs: e.tensor_tensor(t2[:], a2[:], b2[:, :, cs], ALU.mult), zdone)
            x = dve.do(lambda e, j, op=op: e.tensor_tensor(t1[:], t1[:], t2[:], op), x2)
            mark("t1 read", m.split(lambda j, hi=hi: hi[:], lambda j, lo=lo: lo[:], lambda j: t1[:], x))
        mark("spectrum read", x2)

        def part(hi, lo):
            return lambda k, i: (hi[:, k, i * P:(i + 1) * P], lo[:, k, i * P:(i + 1) * P])
        w = positions([part(ych, ycl), part(ysh, ysl)], dve_now())
        for i in range(2):
            x = dve.do(lambda e, j, i=i, order=order: e.scalar_tensor_tensor(pj[:, HY + i, :], pj[:, HY + i, :], col("hy_skip", 2 * order + i), bank[i][:],
                                                                            ALU.mult, ALU.add), w)
            m.free_bank(i, x)
            x = dve.do(lambda e, j, i=i, order=order: e.tensor_tensor(pj[:, HY + i, :], pj[:, HY + i, :], pj[:, HY + 2 + 2 * order + i, :], ALU.mult), x)
    for i in range(2):
        m.split(lambda j, i=i: yhi2[:, 4 + i, :], lambda j, i=i: ylo2[:, 4 + i, :], lambda j, i=i: pj[:, HY + i, :], x)
    hy_done, hy_pe = dve_now(), used_now()

    NE = 2 * ROWS - 2
    bias = place("na_bias", 138, [P, NA_HEADS, NE * GRID])
    hide = place("na_hide", 116, [P, NE * GRID])
    sc = place("na_sc", 154, [P, S + M])
    pr = place("na_p", 157, [P, S + M])
    qst = place("na_q", 160, [P, P])
    prt = place("na_pt", 104, [P, TT + MT, S])
    got_hide = m.fetch("in_hide", hide[:], t["na_hide"], hy_done, hy_pe)
    got_bias = m.fetch("in_bias", bias[:], t["rpb"], hy_done)
    for h in range(NA_HEADS):
        x = dve.do(lambda e, j, h=h: e.tensor_tensor(bias[:, h, :], bias[:, h, :], hide[:], ALU.add), got_hide, got_bias)
    bias_set = x
    nmx, nnb, nsum, ninv = (small[:, i:i + 1] for i in (160, 161, 162, 163))
    for h in range(NA_HEADS):
        i, ph = h // 2, slice(64 * (h % 2), 64 * (h % 2) + 64)

        def tile(h=h, i=i, ph=ph):
            x = dve.do(lambda e, j: e.tensor_copy(qst[:], pj[:, NQ + i, bass.ds(j * P, P)]), last("qst read"), hy_done)
            s1 = pe.do(lambda e, j: e.matmul(bank[4][:], qst[ph, :], pj[ph, NK + i, :], start=True, stop=True), x, m.bank_free(4))
            s2 = pe.do(lambda e, j: e.matmul(bank[5][:, 0:M], qst[ph, :], kctx[ph, i, :], start=True, stop=True), x, m.bank_free(5))
            mark("qst read", s2)
            x = dve.do(lambda e, j: e.scalar_tensor_tensor(sc[:, 0:S], bank[4][:], NA_HD ** -0.5, bias[:, h, bass.ds((j * -1 + (TT - 1)) * (2 * GRID), S)],
                                                           ALU.mult, ALU.add), s1, bias_set, last("na sc read"))
            m.free_bank(4, x)
            a = act.do(lambda e, j: e.activation(sc[:, S:S + M], bank[5][:, 0:M], ACT.Copy, scale=NA_HD ** -0.5), s2, last("na sc read"), hy_done)
            m.free_bank(5, a)
            x = dve.do(lambda e, j: e.tensor_reduce(nmx, sc[:], AX, ALU.max), a, x)
            x = dve.do(lambda e, j: e.tensor_scalar(nnb, nmx, -1.0, None, ALU.mult), x, last("na sc read"))
            a = act.do(lambda e, j: e.activation(pr[:], sc[:], ACT.Exp, bias=nnb, accum_out=nsum), x, last("na p read"))
            mark("na sc read", a)
            x = dve.do(lambda e, j: e.reciprocal(ninv, nsum), a)
            x = dve.do(lambda e, j: e.tensor_scalar(pr[:], pr[:], ninv, None, ALU.mult), x)
            for b, k0, nk in ((6, 0, TT), (7, TT, MT)):
                def turn(e, j, b=b, k0=k0, nk=nk):
                    for k in range(nk):
                        ins = e.transpose(bank[b][:, k * P:(k + 1) * P], pr[:, (k0 + k) * P:(k0 + k + 1) * P], ident)
                    return ins
                tr = pe.do(turn, x, m.bank_free(b))
                a = act.do(lambda e, j, b=b, k0=k0, nk=nk: e.activation(prt[:, k0:k0 + nk, bass.ds(j * P, P)],
                                                                       bank[b][:, 0:nk * P].rearrange("p (k c) -> p k c", k=nk), ACT.Copy),
                           tr, last("prt read"), hy_done)
                m.free_bank(b, a)
            mark("na p read", tr)
        prog.loop_of(TT, 0, tile)

        def out(e, j, h=h, ph=ph):
            for k in range(TT + MT):
                lhs = nv[:, k, h * NA_HD:(h + 1) * NA_HD] if k < TT else vctx[:, k - TT, h * NA_HD:(h + 1) * NA_HD]
                ins = e.matmul(bank[3][ph, :], lhs, prt[:, k, :], start=(k == 0), stop=(k == TT + MT - 1))
            return ins
        y = pe.do(out, act_now(), m.bank_free(3))
        mark("prt read", y)
        if h % 2:
            m.free_bank(3, m.split(lambda j, i=i: yhi2[:, 6 + i, :], lambda j, i=i: ylo2[:, 6 + i, :], lambda j: bank[3][:], y))
    y_ready = dve_now()

    mghi, mglo = place("mghi", 104, [P, KT, S], F32R), place("mglo", 120, [P, KT, S], F32R)
    gs = [place(f"gate{b}", 138 + 2 * b, [P, S]) for b in range(GATES2)]
    mg, mp = place("mg", 146, [P, S]), place("mgp", 148, [P, S])
    na_done = act_now()

    def merge_tiles():
        for u in range(4):
            for b in range(GATES2):
                w = m.product_tile(b, hhi, hlo, h_ready)
                g = act.do(lambda e, j, b=b: e.activation(gs[b][:], bank[b][:], ACT.Sigmoid), w, y_ready, last(f"gate{b} read"))
                m.free_bank(b, g)

            def mm(e, j, whi, wlo):
                for b in range(GATES2):
                    for k in range(2):
                        wt = slice((2 * b + k) * P, (2 * b + k + 1) * P)
                        e.matmul(bank[4 + b][:], whi[:, wt], yhi2[:, 2 * b + k, :], start=(k == 0), stop=False)
                        e.matmul(bank[4 + b][:], whi[:, wt], ylo2[:, 2 * b + k, :], start=False, stop=False)
                        ins = e.matmul(bank[4 + b][:], wlo[:, wt], yhi2[:, 2 * b + k, :], start=False, stop=(k == 1))
                return ins
            w = m.take(mm, y_ready, *[m.bank_free(4 + b) for b in range(GATES2)])
            x = dve.do(lambda e, j: e.tensor_tensor(mg[:], bank[4][:], gs[0][:], ALU.mult), w, g, last("mg read"))
            m.free_bank(4, x)
            mark("gate0 read", x)
            for b in range(1, GATES2):
                x = dve.do(lambda e, j, b=b: e.tensor_tensor(mp[:], bank[4 + b][:], gs[b][:], ALU.mult), x)
                m.free_bank(4 + b, x)
                mark(f"gate{b} read", x)
                x = dve.do(lambda e, j: e.tensor_tensor(mg[:], mg[:], mp[:], ALU.add), x)
            mark("mg read", m.split(lambda j, u=u: mghi[:, j * 4 + u, :], lambda j, u=u: mglo[:, j * 4 + u, :], lambda j: mg[:], x, na_done))
    prog.loop_of(2, 20, merge_tiles)
    mg_ready = dve_now()

    def gated_add(gate, store_at=None):
        return lambda b, at, w: dve.do(lambda e, j: e.scalar_tensor_tensor(resid[:, at(j), :], bank[b][:], mod[:, bass.ds(at(j) + gate, 1), 0:1].rearrange("p a b -> p (a b)"),
                                                                          resid[:, at(j), :], ALU.mult, ALU.add), w)

    def out_tiles():
        for u in range(SLOTS):
            b = prog.chunk % 4
            w = m.product_tile(b, mghi, mglo, mg_ready)
            m.free_bank(b, gated_add(G1)(b, lambda j, u=u: j * SLOTS + u, w))
    prog.loop_of(2, SLOTS, out_tiles)

    merged = used_now()
    sqe = [place(f"sqe{i}", 104 + 2 * i, [P, S]) for i in range(2)]
    norm(resid, S, hhi, hlo, lambda k: gsc[:, 16 + k:17 + k], lambda k: mod[:, SH2 + k, 0:1], sqe, place("re", 108, [P, S]), dve_now(), merged)
    h_ready = dve_now()
    fhi, flo = place("ffn_hi", 104, [P, FFN_TILES, S], F32R), place("ffn_lo", 148, [P, FFN_TILES, S], F32R)
    gpad = [place(f"gpad{i}", 192 + 2.25 * i, [P, S + 2]) for i in range(2)]
    gacc = [place(f"gacc{i}", 196.5 + 2 * i, [P, S]) for i in range(2)]
    gsg, gu = place("gsg", 200.5, [P, S]), place("gu", 203, [P, S])
    for i in range(2):
        x = dve.do(lambda e, j, i=i: e.memset(gpad[i][:, 0:1], 0.0), h_ready)
        gz = dve.do(lambda e, j, i=i: e.memset(gpad[i][:, S + 1:S + 2], 0.0), h_ready)

    def ffn_up():
        for p in range(2):
            b = prog.chunk % 4
            w = m.product_tile(b, hhi, hlo, h_ready)
            a = act.do(lambda e, j, b=b, p=p: e.activation(gpad[p][:, 1:S + 1], bank[b][:], ACT.Copy), w, gz, last(f"gpad{p} read"))
            m.free_bank(b, a)
            x = dve.do(lambda e, j, p=p: e.tensor_scalar(gacc[p][:], gpad[p][:, 0:S], colj("ffn_conv_w", j * 2 + p), colj("ffn_conv_b", j * 2 + p), ALU.mult, ALU.add),
                       a, last(f"gacc{p} read"))
            for tap in (1, 2):
                x = dve.do(lambda e, j, p=p, tap=tap: e.scalar_tensor_tensor(gacc[p][:], gpad[p][:, tap:tap + S], colj("ffn_conv_w", j * 2 + (p + tap * FFN_TILES)),
                                                                             gacc[p][:], ALU.mult, ALU.add), x)
            mark(f"gpad{p} read", x)
            a = act.do(lambda e, j, p=p: e.activation(gsg[:], gacc[p][:], ACT.Sigmoid), x, last("gsg read"))
            x = dve.do(lambda e, j, p=p: e.tensor_tensor(gacc[p][:], gacc[p][:], gsg[:], ALU.mult), a)
            mark("gsg read", x)
            b = prog.chunk % 4
            w = m.product_tile(b, hhi, hlo, h_ready)
            x = dve.do(lambda e, j, b=b, p=p: e.tensor_tensor(gu[:], bank[b][:], gacc[p][:], ALU.mult), w, x, last("gu read"))
            m.free_bank(b, x)
            mark(f"gacc{p} read", x)
            mark("gu read", m.split(lambda j, p=p: fhi[:, j * 2 + p, :], lambda j, p=p: flo[:, j * 2 + p, :], lambda j: gu[:], x))
    prog.loop_of(FFN_TILES // 2, SLOTS, ffn_up)
    f_ready = dve_now()
    for half in range(2):
        down(fhi, flo, FFN_TILES, f_ready, lambda o, w, half=half: gated_add(G2)(o, lambda j: half * 4 + o, w))

    done = used_now()
    result = place("result", 112, [P, KT, S])
    sqf = [place(f"sqf{i}", 104 + 2 * i, [P, S]) for i in range(2)]
    norm(resid, S, None, result, lambda k: col("final_g", k), None, sqf, place("rf", 108, [P, S]), dve_now(), done)
    out = m.fetch("out_done", t["out"], result[:], dve_now())
    m.load_chunks(m.total)
    assert prog.chunk == m.total, (prog.chunk, m.total)
    last_out = out

    with nc.Block() as block:
        block.tensor(pe.run)
        block.scalar(act.run)
        block.vector(dve.run)
        block.gpsimd(pool.run)

        @block.sync
        def _(e):
            sp.run(e)
            e.wait_ge(last_out.counter.sem, 16)



def stream_plan():
    plan = []
    full = list(range(KT))

    def tiles(w, first, n, ks=full):
        for i in range(n):
            plan.append((w, ks, first + i * P, P))

    def rows(w, first, width, n, k_tiles=KT):
        nk = CHUNK // width
        for i in range(n):
            for k0 in range(0, k_tiles, nk):
                plan.append((w, list(range(k0, k0 + nk)), first + i * width, width))

    def gated(gate_first, proj):
        for i in range(KT):
            tiles("w_in", gate_first + i * P, 1)
            tiles(proj, i * P, 1)
    sbq, sbk, sbv, mq, mk, mv, mo = (i * D for i in range(7))
    mi = 7 * D
    xq = mi + 2 * ML_HEADS
    gate = xq + D
    tiles("w_in", sbq, 8)
    tiles("w_in", sbk, 8)
    rows("w_in", sbv, 512, 2)
    gated(gate, "w_sb_proj")
    tiles("w_in", mq, 8)
    tiles("w_in", mk, 8)
    rows("w_in", mv, 512, 2)
    tiles("w_in", mo, 8)
    tiles("w_i", 0, 1)
    tiles("w_f", 0, 1)
    gated(gate + D, "w_ml_proj")
    tiles("w_mem_kv", 0, 8)
    rows("w_mem_kv", D, 512, 2)
    tiles("w_in", xq, 8)
    gated(gate + 2 * D, "w_x_proj")
    tiles("w_out", 0, 8)
    for half in range(2):
        tiles("w_ff1", half * 2 * D, 16)
        for g in range(2):
            for n in range(FF_TILES // 4):
                k = half * (FF_TILES // 2) + 2 * n
                plan.append(("w_ff2", [k, k + 1], g * 512, 512))
    tiles("w_mod", 0, 48)
    for mat in ("cos0", "sin0"):
        for n in range(2):
            plan.append((mat, "pairs", 2 * n, P))
    k_at = MIX * 6
    tiles("w_in_2", k_at, 2)
    rows("w_in_2", k_at + MIX, MIX, 1)
    tiles("w_in_2", 0, 14)
    rows("w_in_2", k_at + MIX, MIX, 1)
    for mat in ("fcos", "fsin"):
        rows(mat, 0, 512, 1, TT)
    for order in range(2):
        for mat in ("cos1", "sin1"):
            for n in range(2):
                plan.append((mat, "pairs", 2 * n, P))
        for mat in ("cos1", "sin1"):
            rows(mat, 0, 512, 1, TT)
    for i in range(KT):
        for b in range(GATES2):
            tiles("w_in_2", 8 * MIX + b * D + i * P, 1)
        plan.append(("w_branch", full, i * P, P))
    tiles("w_out_2", 0, 8)
    for i in range(FFN_TILES):
        tiles("w_up", FFN + i * P, 1)
        tiles("w_up", i * P, 1)
    for g in range(2):
        for n in range(FFN_TILES // 2):
            plan.append(("w_down", [2 * n, 2 * n + 1], g * 512, 512))
    return plan


def shape_constants():
    f = np.float32
    r = np.arange(P)
    before = (r[:, None] < r[None, :])
    sel = [np.where(r[:, None] == h, -1.0, 0.0) * np.ones((1, P)) for h in range(ML_HEADS)]
    consts = [np.eye(P), np.ones((P, P)), -np.ones((P, P)), np.where(r[:, None] >= r[None, :], -1.0, 0.0),
              np.where(before, 1.0, 0.0), np.where(before, 0.0, NEG), np.where(r[:, None] <= r[None, :], 0.0, NEG), *sel]
    out = {"consts": np.stack(consts, 1).astype(f)}
    n = np.arange(S)
    for name, a, b in (("0", 0.0, 0.5), ("1", 0.5, 0.5)):
        arg = 2 * np.pi * (n[:, None] + a) * (n[None, :] + b) / (2 * S)
        out["cos" + name], out["sin" + name] = np.cos(arg).astype(f), np.sin(arg).astype(f)
    arg = 2 * np.pi * (n[:, None] * n[None, :] % S) / S
    out["fcos"], out["fsin"] = np.cos(arg).astype(f), (-np.sin(arg)).astype(f)
    g = np.arange(64)
    arg = 2 * np.pi * (g[:, None] * g[None, :] % 64) / 64
    two = lambda a: np.kron(np.eye(2), a)
    out["cs64"] = (np.concatenate([two(np.cos(arg)), two(np.sin(arg))], 1) / np.sqrt(S * 64.0)).astype(f)
    win = np.array([2, 4, 8, 16])
    lo, hi = np.clip(n[None] - win[:, None] // 2, 0, S), np.clip(n[None] - win[:, None] // 2 + win[:, None], 0, S)
    out["pool_counts"] = np.repeat(1.0 / (hi - lo), 64, axis=0).reshape(2, P, S).astype(f)
    t = np.linspace(0.0, 1.0, S, dtype=f)[:, None]
    bands = np.linspace(1e-4, 15, 16, dtype=f)[None, :]
    ang = (f(2.0 * np.pi / S) * n.astype(f)[:, None] * bands).astype(f)
    out["feats"] = np.ascontiguousarray(np.concatenate([t, np.cos(ang), -np.sin(ang)], 1).T).astype(f)
    deltas = np.linspace(np.log(1e-2) / 1.5, np.log(1e-2) / 0.3, MIX, dtype=f)
    window = np.exp(-t * np.abs(deltas)) + f(0.05)
    out["window"] = np.ascontiguousarray(window.reshape(TT, P, MIX).transpose(1, 0, 2)).astype(f)
    c0 = np.clip(g - 8, 0, GRID - 16)
    ok = (g[None, :] >= c0[:, None]) & (g[None, :] < c0[:, None] + 16)
    out["na_hide"] = np.tile(np.where(ok, 0.0, NEG), (2, 2 * ROWS - 2)).astype(f)
    return out


def kernel(**inputs):
    from concourse import bacc
    from concourse.bass_utils import run_bass_kernel_spmd

    f = np.float32
    a = {k: np.asarray(v) for k, v in inputs.items()}
    const = shape_constants()

    def columns(v, n):
        return v.reshape(n, P).T

    def padded(v):
        out = np.zeros((P, 1), f)
        out[:v.size, 0] = v.reshape(-1)
        return out
    parts = {
        "g_mix": columns(a["g_mix"], 8), "b_gate": columns(a["b_gate"], 24), "conv_w": columns(a["conv_w"], 64),
        "conv_b": columns(a["conv_b"], 16), "ml_norm_g": columns(a["ml_norm_g"], 8), "g_mem": columns(a["g_mem"], 8),
        "q_norm_g": columns(a["q_norm_g"], 2), "k_norm_g": columns(a["k_norm_g"], 2), "g_mlp": columns(a["g_mlp"], 8),
        "norm1_g": columns(a["norm1_g_2"], 8), "norm2_g": columns(a["norm2_g_2"], 8), "b_mod": columns(a["b_mod_2"], 48),
        "c": columns(a["c_2"], 8), "c_ctx": columns(a["c_ctx_2"], 8), "pool_scale": columns(a["pool_scale_2"], 2),
        "hy_conv_w": columns(a["hyena_conv_w_2"], 18), "hy_conv_b": columns(a["hyena_conv_b_2"], 6),
        "hy_skip": columns(a["hyena_skip_2"], 4), "ffn_conv_w": columns(a["ffn_conv_w_2"], 66),
        "ffn_conv_b": columns(a["ffn_conv_b_2"], 22), "final_g": columns(a["final_norm_g_2"], 8),
        "b_i": padded(a["b_if"][0, :ML_HEADS]), "b_f": padded(a["b_if"][0, ML_HEADS:]),
        "filt_b1": padded(a["hyena_filt_b1_2"]), "filt_b2": padded(a["hyena_filt_b2_2"]), "freq": padded(a["hyena_freq_2"]),
    }
    gates_at = 7 * D
    w_i, w_f = np.zeros((D, P), f), np.zeros((D, P), f)
    w_i[:, :ML_HEADS] = a["w_in"][0][:, gates_at:gates_at + ML_HEADS]
    w_f[:, :ML_HEADS] = a["w_in"][0][:, gates_at + ML_HEADS:gates_at + 2 * ML_HEADS]
    mats = {"w_i": w_i, "w_f": w_f, "w_in_2": a["w_in_2"][0], "w_out_2": a["w_out_2"][0], "w_mod": a["w_mod_2"][0],
            "w_branch": a["w_branch_2"][0].reshape(GATES2 * MIX, D), "w_up": a["ffn_w_up_2"][0], "w_down": a["ffn_w_down_2"][0],
            **{n: a[n][0] for n in ("w_in", "w_mem_kv", "w_sb_proj", "w_ml_proj", "w_x_proj", "w_out", "w_ff1", "w_ff2")},
            **{n: const.pop(n) for n in ("cos0", "sin0", "cos1", "sin1", "fcos", "fsin")}}
    plan = stream_plan()
    stream = np.empty((len(plan), P, CHUNK), f)
    for dst, (name, ks, first, width) in zip(stream, plan):
        w = mats[name]
        if ks == "pairs":
            block = w.reshape(TT, P, TT, P)[:, :, first:first + 2].transpose(1, 2, 0, 3)
        else:
            block = w[ks[0] * P:(ks[-1] + 1) * P, first:first + width].reshape(len(ks), P, width).transpose(1, 0, 2)
        dst[:] = block.reshape(P, CHUNK)

    def turned(x, n):
        return np.ascontiguousarray(x.reshape(n, KT, P).transpose(2, 1, 0))
    pool_w = np.zeros((P, 2, P), f)
    for g in range(4):
        at = 64 * (g % 2)
        pool_w[at:at + 64, g // 2, at:at + 64] = a["pool_w_2"][0, g]
    table = np.zeros((NA_HEADS, 2 * ROWS - 1, 2 * GRID - 1), f)
    table[:, :, GRID - 16:GRID + 15] = a["na_rpb_2"][0]
    rpb = np.stack([table[:, 1 - low:2 * ROWS - 1 - low, GRID - 1 - cq:2 * GRID - 1 - cq] for low in range(2) for cq in range(GRID)])
    rpb = np.ascontiguousarray(rpb.reshape(P, NA_HEADS, (2 * ROWS - 2) * GRID))
    arrays = {
        "stream": stream, "xT": turned(a["x"], S), "memT": turned(a["mem"], M), "ctxT": turned(a["ctx_2"], M),
        "cols": np.ascontiguousarray(np.concatenate([parts[n] for n, _ in COLS], 1)), "pool_w": pool_w, "rpb": rpb,
        "filt_w1": a["hyena_filt_w1_2"][0], "filt_w2": a["hyena_filt_w2_2"][0],
        "filt_w3": np.concatenate([a["hyena_filt_w3_2"][0], a["hyena_filt_b3_2"]], 0), **const}
    nc = bacc.Bacc("TRN2", target_bir_lowering=False, num_devices=1)
    t = {n: nc.dram_tensor(f"in_{n}_dram", v.shape, mybir.dt.from_np(v.dtype), kind="ExternalInput").ap() for n, v in arrays.items()}
    t["out"] = nc.dram_tensor("out_dram", (P, KT, S), F32, kind="ExternalOutput").ap()
    program(nc, t)
    r = run_bass_kernel_spmd(nc, [{f"in_{n}_dram": v for n, v in arrays.items()}], core_ids=[0])
    out = r.results[0]["out_dram"]
    return np.ascontiguousarray(out.transpose(2, 1, 0)).reshape(1, S, D)
```

```python
from contextlib import ExitStack

import numpy as np
import concourse.bass as bass
from concourse import mybir

F32 = mybir.dt.float32
F32R = mybir.dt.float32r
ALU = mybir.AluOpType
ACT = mybir.ActivationFunctionType
AX = mybir.AxisListType.X

P = 128
D = 1024
KT = D // P
S = 512
TT = S // P
M = 256
MT = M // P
EPS = 1e-6
SB_HEADS, SB_HD = 8, 128
ML_HEADS, ML_HD = 4, 256
X_HEADS, X_HD = 4, 256
FF_TILES = 4 * D // P
MIX = 256
GATES2 = 4
NA_HEADS, NA_HD = 4, 64
GRID = 64
ROWS = S // GRID
FFN = 2816
FFN_TILES = FFN // P
NEG = -1e30

CHUNK = 1024
SLOTS = 4
LEAD = SLOTS - 1

COLS = [("g_mix", 8), ("b_gate", 24), ("conv_w", 64), ("conv_b", 16), ("ml_norm_g", 8), ("g_mem", 8),
        ("q_norm_g", 2), ("k_norm_g", 2), ("g_mlp", 8), ("norm1_g", 8), ("norm2_g", 8), ("b_mod", 48),
        ("c", 8), ("c_ctx", 8), ("pool_scale", 2), ("hy_conv_w", 18), ("hy_conv_b", 6), ("hy_skip", 4),
        ("ffn_conv_w", 66), ("ffn_conv_b", 22), ("final_g", 8), ("b_i", 1), ("b_f", 1),
        ("filt_b1", 1), ("filt_b2", 1), ("freq", 1)]
COL_AT, NCOLS = {}, 0
for _name, _n in COLS:
    COL_AT[_name] = NCOLS
    NCOLS += _n

CONSTS = ["ident", "ones", "neg_ones", "neg_lower", "keep_before", "hide_not_before", "hide_after",
          "sel0", "sel1", "sel2", "sel3"]


TWO_PI = 6.283185307179586
TWO_PI_PARTS = (6.28125, 0.0019350051879882812, TWO_PI - 6.28125 - 0.0019350051879882812)
ROUND = 1.5 * 2.0 ** 23
PI_BELOW = 3.1415925


class Counter:

    def __init__(self, sem, step=1):
        self.sem, self.step, self.n = sem, step, 0


class Event:

    def __init__(self, counter, k, loop=None, per=None):
        self.counter, self.k, self.loop, self.per = counter, k, loop, per

    def value(self, j, loop, back=0):
        if self.loop is None:
            return self.k
        per = self.loop.per[self.counter] if self.per is None else self.per
        if self.loop is not loop:
            return self.k + per * (self.loop.n - 1)
        if isinstance(j, int):
            return self.k + per * (j - back)
        return j * per + (self.k - per * back)


    def reached(self, loop, back=0):
        per = self.loop.per[self.counter] if self.loop and self.per is None else self.per or 0
        if self.loop is not None and self.loop is not loop:
            return self.k + per * (self.loop.n - 1)
        return self.k - per * back


class Last:

    def __init__(self, event, pending=None, name=None):
        self.event, self.pending, self.name = event, pending, name


class Loop:
    def __init__(self, prog, n, chunks):
        self.prog, self.n, self.chunks = prog, n, chunks
        self.bodies, self.per, self.base, self.marks, self.heads = {}, {}, {}, {}, {}


class Engine:

    def __init__(self, prog, sem):
        self.prog, self.steps, self.counter = prog, [], Counter(sem)

    def do(self, emit, *waits, counter=None):
        counter = counter or self.counter
        loop = self.prog.loop
        event = self.prog.count(counter)
        for w in waits:
            if isinstance(w, Last) and w.pending and w.event is not None:
                loop.heads.setdefault(self, []).append(w.event)
            elif loop and isinstance(w, Event) and w.loop is not loop:
                loop.heads.setdefault(self, []).append(w)
        if loop:
            waits = [w for w in waits if isinstance(w, Last) or w.loop is loop]

        def step(e, j):
            newest = {}
            for w in waits:
                back = 0
                if isinstance(w, Last):
                    if w.pending:
                        if w.name not in w.pending.marks:
                            continue
                        back, w = 1, w.pending.marks[w.name]
                    elif w.event is None:
                        continue
                    else:
                        w = w.event
                value, at = w.value(j, loop, back), w.reached(loop, back)
                if w.counter not in newest or at > newest[w.counter][0]:
                    newest[w.counter] = at, value
            for c, (_, value) in newest.items():
                if not isinstance(value, int) or value > 0:
                    e.wait_ge(c.sem, value)
            emit(e, j).then_inc(counter.sem, counter.step)

        (loop.bodies.setdefault(self, []) if loop else self.steps).append(step)
        return event

    def run(self, e):
        for s in self.steps:
            s(e, 0)


class Program:
    def __init__(self):
        self.loop, self.marks, self.chunk = None, {}, 0

    def count(self, counter):
        loop = self.loop
        if loop is None:
            counter.n += counter.step
            return Event(counter, counter.n)
        loop.base.setdefault(counter, counter.n)
        loop.per[counter] = loop.per.get(counter, 0) + counter.step
        return Event(counter, loop.base[counter] + loop.per[counter], loop)

    def mark(self, name, event):
        (self.loop.marks if self.loop else self.marks)[name] = event
        return event

    def last(self, name):
        if self.loop is None:
            return Last(self.marks.get(name))
        if name in self.loop.marks:
            return Last(self.loop.marks[name])
        return Last(self.marks.get(name), pending=self.loop, name=name)

    def loop_of(self, n, chunks, describe):
        if n == 0:
            return
        loop = self.loop = Loop(self, n, chunks)
        first = self.chunk
        describe()
        assert self.chunk == first + chunks and chunks % SLOTS == 0
        self.chunk = first + chunks * n
        self.loop = None
        for counter, per in loop.per.items():
            counter.n = loop.base[counter] + per * n
        self.marks.update(loop.marks)
        for engine, body in loop.bodies.items():
            def run(e, _, body=body, engine=engine):
                heads = {}
                for w in loop.heads.get(engine, []):
                    heads[w.counter] = max(heads.get(w.counter, 0), w.value(0, None))
                for c, value in heads.items():
                    if value > 0:
                        e.wait_ge(c.sem, value)
                if n == 1:
                    for s in body:
                        s(e, 0)
                else:
                    with e.Fori(0, n) as j:
                        for s in body:
                            s(e, j)
            engine.steps.append(run)


class Machine:

    def __init__(self, nc, total_chunks, stream):
        self.nc, self.prog, self.total, self.stream, self.loaded = nc, Program(), total_chunks, stream, 0
        sem = nc.alloc_semaphore
        self.pe, self.act, self.dve = (Engine(self.prog, sem(n)) for n in ("pe_done", "act_done", "dve_done"))
        self.pool, self.sp = (Engine(self.prog, sem(n)) for n in ("pool_done", "sp_done"))
        self.raw_in = [Counter(sem(f"raw_in{s}"), 16) for s in range(SLOTS)]
        self.hi_split, self.lo_split, self.used = (Counter(sem(n)) for n in ("hi_split", "lo_split", "chunk_used"))
        self.base = -(-nc.sbuf_base // 32) * 32 if isinstance(nc.sbuf_base, int) else 16896
        at = self.place
        self.raw = [at(f"raw{s}", 4 * s, [P, CHUNK]) for s in range(SLOTS)]
        self.whi = [at(f"whi{s}", 16 + 4 * s, [P, CHUNK], F32R) for s in range(SLOTS)]
        self.wlo = [at(f"wlo{s}", 32 + 4 * s, [P, CHUNK], F32R) for s in range(SLOTS)]
        self.bank = [nc.alloc_psum_tensor(f"bank{b}", [P, 512], F32) for b in range(8)]

    def place(self, name, kib, shape, dtype=F32):
        return self.nc.alloc_sbuf_tensor_at(name, shape, dtype, offset=self.base + int(kib * 1024))


    def chunk_event(self, counter, c):
        loop = self.prog.loop
        return Event(counter, c + 1, loop, loop.chunks if loop else 0) if loop else Event(counter, c + 1)

    def split_high(self, c):
        loop, slot = self.prog.loop, c % SLOTS
        raw = Event(self.raw_in[slot], 16 * (c // SLOTS + 1), loop, 16 * loop.chunks // SLOTS if loop else None)
        self.act.do(lambda e, j: e.activation(self.whi[slot][:], self.raw[slot][:], ACT.Copy),
                    raw, self.chunk_event(self.used, c - SLOTS), counter=self.hi_split)

    def take(self, matmuls, *waits, later=None):
        c, slot = self.prog.chunk, self.prog.chunk % SLOTS
        self.prog.chunk += 1
        if self.prog.loop or c + LEAD < self.total:
            if later is None:
                self.split_high(c + LEAD)
            else:
                later.append(lambda: self.split_high(c + LEAD))
        return self.pe.do(lambda e, j: matmuls(e, j, self.whi[slot], self.wlo[slot]),
                          self.chunk_event(self.lo_split, c), *waits, counter=self.used)

    def start_stream(self):
        for c in range(LEAD):
            self.split_high(c)

        def low_parts(e, _):
            with e.Fori(0, self.total // SLOTS) as j:
                for s in range(SLOTS):
                    e.wait_ge(self.hi_split.sem, j * SLOTS + (s + 1))
                    i = e.tensor_tensor(self.wlo[s][:], self.raw[s][:], self.whi[s][:].bitcast(F32), ALU.subtract)
                    i.then_inc(self.lo_split.sem, 1)
        self.pool.steps.append(low_parts)

    def load_chunks(self, upto):
        first, upto = self.loaded, min(upto, self.total)
        while self.loaded < min(SLOTS, upto) or (self.loaded < upto and self.loaded % SLOTS):
            c, s = self.loaded, self.loaded % SLOTS

            def one(e, _, c=c, s=s):
                if c >= SLOTS:
                    e.wait_ge(self.lo_split.sem, c - SLOTS + 1)
                e.dma_start(self.raw[s][:], self.stream[c]).then_inc(self.raw_in[s].sem, 16)
            self.sp.steps.append(one)
            self.loaded += 1
        rounds = (upto - self.loaded) // SLOTS
        if rounds > 0:
            def many(e, _, first=self.loaded, rounds=rounds):
                with e.Fori(0, rounds) as j:
                    for s in range(SLOTS):
                        e.wait_ge(self.lo_split.sem, j * SLOTS + (first - SLOTS + s + 1))
                        e.dma_start(self.raw[s][:], self.stream[j * SLOTS + (first + s)]).then_inc(self.raw_in[s].sem, 16)
            self.sp.steps.append(many)
            self.loaded += rounds * SLOTS
        while self.loaded < upto:
            c, s = self.loaded, self.loaded % SLOTS

            def one(e, _, c=c, s=s):
                e.wait_ge(self.lo_split.sem, c - SLOTS + 1)
                e.dma_start(self.raw[s][:], self.stream[c]).then_inc(self.raw_in[s].sem, 16)
            self.sp.steps.append(one)
            self.loaded += 1

    def fetch(self, name, dst, src, *waits):
        self.load_chunks(self.prog.chunk + SLOTS)
        return self.sp.do(lambda e, j: e.dma_start(dst, src), *waits, counter=Counter(self.nc.alloc_semaphore(name), 16))


    def bank_free(self, b):
        return self.prog.last(f"bank{b} free")

    def free_bank(self, b, event):
        self.prog.mark(f"bank{b} free", event)

    def product_tile(self, b, hi, lo, *waits, cols=S, later=None):
        def mm(e, j, whi, wlo):
            out = self.bank[b][:, 0:cols]
            for k in range(KT):
                w = slice(k * P, (k + 1) * P)
                e.matmul(out, whi[:, w], hi[:, k, 0:cols], start=(k == 0), stop=False)
                e.matmul(out, whi[:, w], lo[:, k, 0:cols], start=False, stop=False)
                i = e.matmul(out, wlo[:, w], hi[:, k, 0:cols], start=False, stop=(k == KT - 1))
            return i
        return self.take(mm, self.bank_free(b), *waits, later=later)

    def product_rows(self, banks, hi, lo, k0, nk, width, total_k, *waits):
        def mm(e, j, whi, wlo):
            for t, b in enumerate(banks):
                tok = slice(t * P, (t + 1) * P)
                out = self.bank[b][:, 0:width]
                for n in range(nk):
                    k, w = k0 + n, slice(n * width, (n + 1) * width)
                    e.matmul(out, hi[:, k, tok], whi[:, w], start=(k == 0), stop=False)
                    e.matmul(out, lo[:, k, tok], whi[:, w], start=False, stop=False)
                    i = e.matmul(out, hi[:, k, tok], wlo[:, w], start=False, stop=(k == total_k - 1))
            return i
        if k0 == 0:
            waits = (*waits, *(self.bank_free(b) for b in banks))
        return self.take(mm, *waits)

    def split(self, hi, lo, src, *waits):
        a = self.act.do(lambda e, j: e.activation(hi(j), src(j), ACT.Copy), *waits)
        return self.dve.do(lambda e, j: e.tensor_tensor(lo(j), src(j), hi(j).bitcast(F32), ALU.subtract), a)


def program(nc, t):
    plan = stream_plan()
    m = Machine(nc, len(plan), t["stream"])
    pe, act, dve, pool, sp = m.pe, m.act, m.dve, m.pool, m.sp
    prog, last, mark, place, bank = m.prog, m.prog.last, m.prog.mark, m.place, m.bank

    consts = place("consts", 48, [P, len(CONSTS), P])
    cols = place("cols", 53.5, [P, NCOLS])
    small = place("small", 55, [P, 256])
    C = {n: consts[:, i, :] for i, n in enumerate(CONSTS)}
    ident, ones = C["ident"], C["ones"]
    epsc = small[:, 255:256]

    def col(name, i=0):
        return cols[:, COL_AT[name] + i:COL_AT[name] + i + 1]

    hhi, hlo = place("hhi", 56, [P, KT, S], F32R), place("hlo", 72, [P, KT, S], F32R)
    resid = place("resid", 88, [P, KT, S])
    sig = [place(f"sig{i}", 184.5 + 2 * i, [P, S]) for i in range(2)]
    prod = place("prod", 188.5, [P, S])
    crhs = place("crhs", 206.5, [P, KT, 4], F32R)
    mod = place("mod", 206.625, [P, 48, 2])

    got_consts = m.fetch("in_consts", consts[:], t["consts"])
    got_cols = m.fetch("in_cols", cols[:], t["cols"])
    x0 = place("x0", 104, [P, KT, S])
    got_x = m.fetch("in_x", x0[:], t["xT"])
    m.start_stream()
    eps_set = dve.do(lambda e, j: e.memset(epsc, EPS))

    def norm(src, n, hi, lo, gain, shift, sq, r, *ready):
        ev = None
        for k in range(KT):
            q = sq[k % 2]
            a = act.do(lambda e, j, k=k, q=q: e.activation(q[:, 0:n], src[:, k, 0:n], ACT.Square),
                       *ready, last(f"sq{k % 2} read"))
            ev = pe.do(lambda e, j, k=k, q=q: e.matmul(bank[7][:, 0:n], ones, q[:, 0:n], start=(k == 0), stop=(k == KT - 1)),
                       a, got_consts, m.bank_free(7))
            mark(f"sq{k % 2} read", ev)
        a = act.do(lambda e, j: e.activation(r[:, 0:n], bank[7][:, 0:n], ACT.Sqrt, bias=epsc, scale=1.0 / D), ev, eps_set)
        m.free_bank(7, a)
        rr = dve.do(lambda e, j: e.reciprocal(r[:, 0:n], r[:, 0:n]), a, got_cols)
        for k in range(KT):
            q = sq[k % 2]
            if hi is None:
                dve.do(lambda e, j, k=k: e.scalar_tensor_tensor(lo[:, k, 0:n], src[:, k, 0:n], gain(k), r[:, 0:n], ALU.mult, ALU.mult), rr)
                continue
            v = dve.do(lambda e, j, k=k, q=q: e.scalar_tensor_tensor(q[:, 0:n], src[:, k, 0:n], gain(k), r[:, 0:n], ALU.mult, ALU.mult),
                       rr, last(f"sq{k % 2} read"))
            if shift is not None:
                v = dve.do(lambda e, j, k=k, q=q: e.tensor_scalar(q[:, 0:n], q[:, 0:n], shift(k), None, ALU.add), v)
            mark(f"sq{k % 2} read", m.split(lambda j, k=k: hi[:, k, 0:n], lambda j, k=k: lo[:, k, 0:n],
                                            lambda j, q=q: q[:, 0:n], v))

    cin = cols[:, COL_AT["c"]:COL_AT["c"] + 16].rearrange("p (w k) -> p k w", w=2)
    cact, csg = (small[:, i:i + 16].rearrange("p (k w) -> p k w", w=2) for i in (184, 200))
    a = act.do(lambda e, j: e.activation(csg, cin, ACT.Sigmoid), got_cols)
    x = dve.do(lambda e, j: e.tensor_tensor(cact, csg, cin, ALU.mult), a)
    a = act.do(lambda e, j: e.activation(crhs[:, :, 0:2], cact, ACT.Copy), x)
    c_ready = dve.do(lambda e, j: e.tensor_tensor(crhs[:, :, 2:4], cact, crhs[:, :, 0:2].bitcast(F32), ALU.subtract), a)

    def mod_chunk(b, at, on_act, on_dve):
        def mm(e, j, whi, wlo):
            for k in range(KT):
                w = slice(k * P, (k + 1) * P)
                e.matmul(bank[b][:, 0:4], whi[:, w], crhs[:, k, :], start=(k == 0), stop=False, skip_group_check=True)
                i = e.matmul(bank[b][:, 0:2], wlo[:, w], crhs[:, k, 0:2], start=False, stop=(k == KT - 1), skip_group_check=True)
            return i
        w = m.take(mm, m.bank_free(b), c_ready, later=on_act)
        on_dve.append(lambda: m.free_bank(b, dve.do(lambda e, j: e.tensor_reduce(
            mod[:, at(j), :], bank[b][:, 0:4].rearrange("p (s w) -> p w s", s=2), AX, ALU.add), w)))

    def run_all(steps):
        for step in steps:
            step()
        steps.clear()

    def raw_tile(b, dst, *waits, on_act=None):
        w = m.product_tile(b, hhi, hlo, h_ready, later=on_act)
        store = lambda: m.free_bank(b, act.do(lambda e, j: e.activation(dst(j), bank[b][:], ACT.Copy), w, *waits))
        if on_act is None:
            store()
        else:
            on_act.append(store)

    def dve_now():
        return Event(dve.counter, dve.counter.n)

    def act_now():
        return Event(act.counter, act.counter.n)

    def pe_now():
        return Event(pe.counter, pe.counter.n)

    def used_now():
        return Event(m.used, m.used.n)

    sq = [place(f"sqa{i}", 120 + 2 * i, [P, S]) for i in range(2)]
    norm(x0, S, hhi, hlo, lambda k: col("g_mix", k), None, sq, place("ra", 124, [P, S]), got_x)
    h_ready = dve_now()

    q = place("sb_q", 104, [P, KT, S])
    k_ = place("sb_k", 120, [P, KT, S])
    v = place("sb_v", 136, [P, TT, D])
    yhi, ylo = place("sb_yhi", 104, [P, KT, S], F32R), place("sb_ylo", 120, [P, KT, S], F32R)
    spl = place("sb_sp", 152, [P, 1280])
    att = place("sb_att", 157, [P, 1280])
    tmp = place("sb_tmp", 162, [P, 1280])
    tm2 = place("sb_tm2", 167, [P, 1280])

    def tiles_to(dst, scale, hi, lo, base=0, cols_=S, count=SLOTS):
        for u in range(count):
            b = prog.chunk % 4
            w = m.product_tile(b, hi, lo, h_ready, cols=cols_)
            ev = act.do(lambda e, j, u=u, b=b: e.activation(dst[:, j * SLOTS + (u + base), 0:cols_], bank[b][:, 0:cols_], ACT.Copy, scale=scale), w)
            m.free_bank(b, ev)

    def rows_to(hi, lo, width, toks, store):
        nk = CHUNK // width
        for k0 in range(0, KT, nk):
            w = m.product_rows(list(range(toks)), hi, lo, k0, nk, width, KT, h_ready)
        for tt in range(toks):
            m.free_bank(tt, store(tt, bank[tt][:, 0:width], w))

    tiles_to(q, SB_HD ** -0.5, hhi, hlo)
    tiles_to(q, SB_HD ** -0.5, hhi, hlo, base=4)
    prog.loop_of(2, SLOTS, lambda: tiles_to(k_, 1.0, hhi, hlo))
    prog.loop_of(2, SLOTS, lambda: rows_to(hhi, hlo, 512, TT, lambda tt, ps, w: act.do(
        lambda e, j: e.activation(v[:, tt, bass.ds(j * 512, 512)], ps, ACT.Copy), w)))
    sb_in = act_now()

    CUT = [0, 512, 896, 1152, 1280]
    mo = place("ml_o", 190.5, [P, KT, S])
    kst = place("sb_kst", 172, [P, S])
    vst = place("sb_vst", 174, [P, TT, P])

    def span(c):
        return slice(CUT[c], CUT[c + 1])

    def diag(c):
        return slice(CUT[c], CUT[c] + P)

    def sb_head():
        ks = dve.do(lambda e, j: e.tensor_copy(kst[:], k_[:, j, :]), sb_in, last("sb kst read"))
        vs = dve.do(lambda e, j: e.tensor_copy(vst[:], v[:, :, bass.ds(j * P, P)]), sb_in, last("sb vst read"))
        for c in range(TT):
            z = pe.do(lambda e, j, c=c: e.matmul(bank[4 + c][:, 0:S - P * c], kst[:, c * P:(c + 1) * P], q[:, j, c * P:S],
                                                 start=True, stop=False, skip_group_check=True), ks, m.bank_free(4 + c))
        mark("sb kst read", z)
        on_act, on_dve = [], []
        raw_tile(0, lambda j: resid[:, j, :], on_act=on_act)
        raw_tile(1, lambda j: mo[:, j, :], on_act=on_act)
        for c in range(TT):
            a = act.do(lambda e, j, c=c: e.activation(tmp[:, span(c)], bank[4 + c][:, 0:S - P * c], ACT.Abs), z, last("sb tmp read"))
        a = act.do(lambda e, j: e.activation(tmp[:], tmp[:], ACT.Exp, scale=-1.0), a)
        a = act.do(lambda e, j: e.activation(tmp[:], tmp[:], ACT.Ln, bias=1.0), a)
        run_all(on_act)
        for c in range(TT):
            s1 = dve.do(lambda e, j, c=c: e.scalar_tensor_tensor(spl[:, span(c)], bank[4 + c][:, 0:S - P * c], 0.0, tmp[:, span(c)],
                                                                 ALU.max, ALU.add), a, last("sb spl read"))
        mark("sb tmp read", s1)
        for c in range(TT):
            s2 = dve.do(lambda e, j, c=c: e.tensor_tensor(spl[:, diag(c)], spl[:, diag(c)], C["keep_before"], ALU.mult), s1, got_consts)
        for c in range(TT):
            def sums(e, j, c=c):
                out = bank[4 + c]
                e.matmul(out[:, 0:P], ident, C["hide_not_before"], start=False, stop=False, skip_group_check=True)
                for jj in range(c, TT):
                    i = e.matmul(out[:, (jj - c) * P:S - P * c], C["neg_lower"] if jj == c else C["neg_ones"], spl[:, span(jj)],
                                 start=False, stop=(jj == TT - 1), skip_group_check=True)
                return i
            r = pe.do(sums, s2)
            x = act.do(lambda e, j, c=c: e.activation(att[:, span(c)], bank[4 + c][:, 0:S - P * c], ACT.Exp), r, last("sb att read"))
            m.free_bank(4 + c, x)
        mark("sb spl read", r)
        mod_chunk(2, lambda j: j * 2, on_act, on_dve)
        mod_chunk(0, lambda j: j * 2 + 1, on_act, on_dve)
        for c in range(TT):
            y = pe.do(lambda e, j, c=c: e.matmul(bank[3][:, c * P:S], vst[:, c, :], att[:, span(c)], start=(c == 0), stop=(c == TT - 1),
                                                 skip_group_check=True), x, vs, m.bank_free(3))
        mark("sb vst read", y)
        run_all(on_act)
        run_all(on_dve)
        mark("sb att read", y)
        m.free_bank(3, m.split(lambda j: yhi[:, j, :], lambda j: ylo[:, j, :], lambda j: bank[3][:], y))

    prog.loop_of(SB_HEADS, SLOTS, sb_head)

    def stored_gates(first, raw, bhi, blo, bias):
        y_ready, raw_in = dve_now(), act_now()

        def body():
            for u in range(SLOTS):
                b, half = prog.chunk % 4, u % 2
                g = act.do(lambda e, j, u=u, half=half: e.activation(sig[half][:], raw[:, j * SLOTS + u, :], ACT.Sigmoid, bias=bias(j * SLOTS + u)),
                           raw_in, y_ready, last(f"sig{half} read"))
                w = m.product_tile(b, bhi, blo, y_ready)
                if first:
                    x = dve.do(lambda e, j, b=b, u=u, half=half: e.tensor_tensor(resid[:, j * SLOTS + u, :], bank[b][:], sig[half][:], ALU.mult), w, g)
                    m.free_bank(b, x)
                else:
                    x = dve.do(lambda e, j, b=b, half=half: e.tensor_tensor(prod[:], bank[b][:], sig[half][:], ALU.mult), w, g, last("prod read"))
                    m.free_bank(b, x)
                    mark("prod read", dve.do(lambda e, j, u=u: e.tensor_tensor(resid[:, j * SLOTS + u, :], resid[:, j * SLOTS + u, :], prod[:], ALU.add), x))
                mark(f"sig{half} read", x)
        prog.loop_of(2, SLOTS, body)

    def gated_projection(bhi, blo, bias):
        y_ready = dve_now()

        def body():
            for half in range(2):
                b = prog.chunk % 4
                w = m.product_tile(b, hhi, hlo, h_ready)
                g = act.do(lambda e, j, b=b, half=half: e.activation(sig[half][:], bank[b][:], ACT.Sigmoid, bias=bias(j * 2 + half)),
                           w, last(f"sig{half} read"))
                m.free_bank(b, g)
                b = prog.chunk % 4
                w = m.product_tile(b, bhi, blo, y_ready)
                x = dve.do(lambda e, j, b=b, half=half: e.tensor_tensor(prod[:], bank[b][:], sig[half][:], ALU.mult), w, g, last("prod read"))
                m.free_bank(b, x)
                mark("prod read", dve.do(lambda e, j, half=half: e.tensor_tensor(resid[:, j * 2 + half, :], resid[:, j * 2 + half, :], prod[:], ALU.add), x))
                mark(f"sig{half} read", x)
        prog.loop_of(KT // 2, SLOTS, body)

    def colj(name, i):
        return cols[:, bass.ds(i + COL_AT[name], 1)]

    stored_gates(True, resid, yhi, ylo, lambda i: colj("b_gate", i))

    sb_done = used_now()
    mq = place("ml_q", 104, [P, KT, S])
    mk = place("ml_k", 120, [P, KT, S])
    hm = place("ml_hm", 120, [P, ML_HEADS, TT, ML_HD])
    mv = place("ml_v", 136, [P, TT, ML_HEADS, ML_HD + 1])
    wgt = place("ml_w", 152.25, [P, 1280])
    pmat = place("ml_p", 157.25, [P, 1280])
    kst2 = place("ml_kst", 162.25, [P, 2, S])
    rows = [place(f"ml_row{i}", 166.25 + 2 * i, [P, S]) for i in range(4)]
    pad = [place(f"ml_pad{i}", 152.25 + 2.25 * i, [P, S + 3]) for i in range(2)]
    acc = [place(f"ml_acc{i}", 156.75 + 2 * i, [P, S]) for i in range(2)]
    csig = place("ml_csig", 160.75, [P, S])
    selst = place("ml_sel", 176.75, [P, P])
    dg = place("ml_dg", 177.25, [P, TT, P])
    hst = place("ml_hst", 179.25, [P, TT, ML_HD])
    mhi, mlo = place("ml_yhi", 104, [P, KT, S], F32R), place("ml_ylo", 136, [P, KT, S], F32R)

    for i in range(2):
        zero = dve.do(lambda e, j, i=i: e.memset(pad[i][:, 0:3], 0.0), sb_done)
    onescol = dve.do(lambda e, j: e.memset(mv[:, :, :, ML_HD:ML_HD + 1], 1.0), sb_done)

    bi = prog.chunk % 4
    wi = m.product_tile(bi, hhi, hlo, h_ready)
    bf = prog.chunk % 4
    wf = m.product_tile(bf, hhi, hlo, h_ready)
    r_i, r_f, r_t, r_a = rows
    f1 = act.do(lambda e, j: e.activation(r_f[:], bank[bf][:], ACT.Identity, bias=col("b_f")), wf, sb_done)
    i1 = act.do(lambda e, j: e.activation(r_i[:], bank[bi][:], ACT.Identity, bias=col("b_i")), wi, sb_done)
    m.free_bank(bi, i1)
    m.free_bank(bf, f1)
    a = act.do(lambda e, j: e.activation(r_t[:], r_f[:], ACT.Abs), f1, i1)
    a = act.do(lambda e, j: e.activation(r_t[:], r_t[:], ACT.Exp, scale=-1.0), a)
    a = act.do(lambda e, j: e.activation(r_t[:], r_t[:], ACT.Ln, bias=1.0), a)
    x = dve.do(lambda e, j: e.scalar_tensor_tensor(r_f[:], r_f[:], 0.0, r_t[:], ALU.min, ALU.subtract), a)
    x1 = dve.do(lambda e, j: e.memset(r_a[:], 1.0), sb_done)
    x = dve.do(lambda e, j: e.tensor_tensor_scan(r_t[:], r_a[:], r_f[:], 0.0, ALU.mult, ALU.add), x, x1)
    x = dve.do(lambda e, j: e.tensor_tensor(r_i[:], r_i[:], r_t[:], ALU.subtract), x)
    x = dve.do(lambda e, j: e.tensor_tensor_scan(r_f[:], r_a[:], r_i[:], 0.0, ALU.mult, ALU.max), x)
    x = dve.do(lambda e, j: e.tensor_tensor(r_t[:], r_t[:], r_f[:], ALU.add), x)
    acol = small[:, 0:16].rearrange("p (t h) -> p t h", t=TT)
    gcol = small[:, 16:32].rearrange("p (t h) -> p t h", t=TT)
    for tt in range(TT):
        ta = pe.do(lambda e, j, tt=tt: e.transpose(bank[4][:, tt * P:(tt + 1) * P], r_i[:, tt * P:(tt + 1) * P], ident), x, m.bank_free(4))
        tg = pe.do(lambda e, j, tt=tt: e.transpose(bank[5][:, tt * P:(tt + 1) * P], r_t[:, tt * P:(tt + 1) * P], ident), x, m.bank_free(5))
    ac = act.do(lambda e, j: e.activation(acol, bank[4][:].rearrange("p (t c) -> p t c", t=TT)[:, :, 0:ML_HEADS], ACT.Copy), tg)
    m.free_bank(4, ac)
    gc = act.do(lambda e, j: e.activation(gcol, bank[5][:].rearrange("p (t c) -> p t c", t=TT)[:, :, 0:ML_HEADS], ACT.Exp, scale=-1.0), tg)
    m.free_bank(5, gc)
    rows_in = act_now()

    def conv_tiles(dst, first):
        for u in range(SLOTS):
            b, p = prog.chunk % 4, u % 2
            w = m.product_tile(b, hhi, hlo, h_ready)
            a = act.do(lambda e, j, b=b, p=p: e.activation(pad[p][:, 3:S + 3], bank[b][:], ACT.Copy), w, zero, last(f"pad{p} read"))
            m.free_bank(b, a)
            x = dve.do(lambda e, j, u=u, p=p: e.tensor_scalar(acc[p][:], pad[p][:, 0:S], colj("conv_w", j * SLOTS + (u + first)),
                                                              colj("conv_b", j * SLOTS + (u + first)), ALU.mult, ALU.add), a, last(f"acc{p} read"))
            for tap in range(1, 4):
                x = dve.do(lambda e, j, u=u, p=p, tap=tap: e.scalar_tensor_tensor(
                    acc[p][:], pad[p][:, tap:tap + S], colj("conv_w", j * SLOTS + (u + first + 16 * tap)), acc[p][:], ALU.mult, ALU.add), x)
            mark(f"pad{p} read", x)
            a = act.do(lambda e, j, p=p: e.activation(csig[:], acc[p][:], ACT.Sigmoid), x, last("csig read"))
            x = dve.do(lambda e, j, u=u, p=p: e.tensor_tensor(dst[:, j * SLOTS + u, :], acc[p][:], csig[:], ALU.mult), a, sb_done)
            mark(f"acc{p} read", x)
            mark("csig read", x)

    def with_out_gates():
        conv_tiles(mq, 0)
        for u in range(SLOTS):
            act.do(lambda e, j, u=u: e.activation(mo[:, j * SLOTS + u, :], mo[:, j * SLOTS + u, :], ACT.Sigmoid), act_now())
    prog.loop_of(2, SLOTS, with_out_gates)
    prog.loop_of(2, SLOTS, lambda: conv_tiles(mk, 8))
    conv_done = dve_now()
    prog.loop_of(2, SLOTS, lambda: rows_to(hhi, hlo, 512, TT, lambda tt, ps, w: act.do(
        lambda e, j: e.activation(mv[:, tt, bass.ds(j * 2, 2), 0:ML_HD], ps.rearrange("p (h d) -> p h d", h=2), ACT.Copy), w, sb_done)))

    ml_in = act_now()

    ssq = small[:, 32:48]
    den = small[:, 48:52]
    rden = small[:, 52:56]

    def ml_head():
        sl = dve.do(lambda e, j: e.tensor_copy(selst[:], consts[:, j + CONSTS.index("sel0"), :]), last("selst read"))
        ks = dve.do(lambda e, j: e.tensor_copy(kst2[:], mk[:, bass.ds(j * 2, 2), :]), conv_done, last("ml kst read"))
        mx = pe.do(lambda e, j: e.matmul(bank[3][:], selst[:], r_f[:], start=True, stop=True), sl, ml_in, m.bank_free(3))
        mark("selst read", mx)
        for c in range(TT):
            def scores(e, j, c=c):
                for k in range(2):
                    i = e.matmul(bank[4 + c][:, 0:S - P * c], kst2[:, k, c * P:(c + 1) * P], mq[:, j * 2 + k, c * P:S],
                                 start=(k == 0), stop=(k == 1))
                return i
            sc = pe.do(scores, ks, m.bank_free(4 + c))
        mark("ml kst read", sc)
        on_act, on_dve = [], []
        for u in range(2):
            mod_chunk(u, lambda j, u=u: j * 4 + (16 + u), on_act, on_dve)
        for c in range(TT):
            d = dve.do(lambda e, j, c=c: e.tensor_tensor(dg[:, c, :], bank[3][:, c * P:(c + 1) * P], C["hide_after"], ALU.add), mx, last("dg read"))
        for c in range(TT):
            a = act.do(lambda e, j, c=c: e.activation(wgt[:, diag(c)], dg[:, c, :], ACT.Exp, bias=small[:, bass.ds(j + c * 4, 1)]),
                       d, ac, last("wgt read"))
            if c < TT - 1:
                a = act.do(lambda e, j, c=c: e.activation(wgt[:, CUT[c] + P:CUT[c + 1]], bank[3][:, (c + 1) * P:S], ACT.Exp,
                                                          bias=small[:, bass.ds(j + c * 4, 1)]))
        mark("dg read", a)
        m.free_bank(3, a)
        for c in range(TT):
            x = dve.do(lambda e, j, c=c: e.scalar_tensor_tensor(pmat[:, span(c)], bank[4 + c][:, 0:S - P * c], ML_HD ** -0.5, wgt[:, span(c)],
                                                                ALU.mult, ALU.mult), sc, a, last("pmat read"))
        mark("wgt read", x)
        run_all(on_act)
        run_all(on_dve)
        for i in range(TT):
            def sums(e, j, i=i):
                for c in range(i + 1):
                    at = CUT[c] + (i - c) * P
                    ins = e.matmul(bank[4 + i][:, 0:ML_HD + 1], pmat[:, at:at + P], mv[:, c, j, :], start=(c == 0), stop=(c == i))
                return ins
            n = pe.do(sums, x, onescol)
            if i == 1:
                mod_chunk(2, lambda j: j * 4 + 18, on_act, on_dve)
            d = act.do(lambda e, j, i=i: e.activation(den[:, i:i + 1], bank[4 + i][:, ML_HD:ML_HD + 1], ACT.Abs), n, last("den read"))
            d = dve.do(lambda e, j, i=i: e.tensor_scalar(den[:, i:i + 1], den[:, i:i + 1], small[:, bass.ds(j + (16 + i * 4), 1)], None, ALU.max), d, gc)
            d = dve.do(lambda e, j, i=i: e.reciprocal(rden[:, i:i + 1], den[:, i:i + 1]), d, last("rden read"))
            a = act.do(lambda e, j, i=i: e.activation(hm[:, j, i, :], bank[4 + i][:, 0:ML_HD], ACT.Copy, scale=rden[:, i:i + 1]), d, ks)
            m.free_bank(4 + i, a)
            a2 = act.do(lambda e, j, i=i: e.activation(hst[:, i, :], hm[:, j, i, :], ACT.Square, accum_out=small[:, bass.ds(j + (32 + i * 4), 1)]), a, last("hst read"))
        mod_chunk(0, lambda j: j * 4 + 19, on_act, on_dve)
        run_all(on_act)
        run_all(on_dve)
        mark("rden read", a)
        mark("den read", d)
        mark("hst read", a2)
        mark("pmat read", n)

    prog.loop_of(ML_HEADS, SLOTS, ml_head)
    a = act.do(lambda e, j: e.activation(ssq, ssq, ACT.Sqrt, bias=epsc, scale=1.0 / ML_HD), act_now())
    rms = dve.do(lambda e, j: e.reciprocal(ssq, ssq), a)
    v_read = pe_now()

    def ml_out():
        for i in range(TT):
            x = dve.do(lambda e, j, i=i: e.tensor_scalar(hst[:, i, :], hm[:, j, i, :], small[:, bass.ds(j + (32 + i * 4), 1)], None, ALU.mult),
                       rms, last("hst turned"))
        for c in range(2):
            def turn(e, j, c=c):
                for i in range(TT):
                    ins = e.transpose(bank[4 + c][:, i * P:(i + 1) * P], hst[:, i, c * P:(c + 1) * P], ident)
                return ins
            tr = pe.do(turn, x, m.bank_free(4 + c))
            y = dve.do(lambda e, j, c=c: e.scalar_tensor_tensor(rows[c][:], bank[4 + c][:], colj("ml_norm_g", j * 2 + c), mo[:, j * 2 + c, :],
                                                                ALU.mult, ALU.mult), tr, v_read, last(f"row{c} read"))
            m.free_bank(4 + c, y)
            mark(f"row{c} read", m.split(lambda j, c=c: mhi[:, j * 2 + c, :], lambda j, c=c: mlo[:, j * 2 + c, :], lambda j, c=c: rows[c][:], y))
        mark("hst turned", tr)

    prog.loop_of(ML_HEADS, 0, ml_out)
    gated_projection(mhi, mlo, lambda i: colj("b_gate", i + 8))

    ml_done = used_now()
    mem = place("x_mem", 104, [P, KT, M])
    memhi, memlo = place("x_memhi", 112, [P, KT, M], F32R), place("x_memlo", 120, [P, KT, M], F32R)
    xk = place("x_k", 128, [P, KT, M])
    xv = place("x_v", 136, [P, MT, D])
    xq = place("x_q", 144, [P, KT, S])
    xhi, xlo = place("x_yhi", 144, [P, KT, S], F32R), place("x_ylo", 160, [P, KT, S], F32R)
    xsq = place("x_sq", 176, [P, 2, S])
    xsqk = place("x_sqk", 200, [P, 2, M])
    xqst = place("x_qst", 180, [P, 2, S])
    xvst = place("x_vst", 184, [P, MT, X_HD])
    xp = place("x_p", 186, [P, TT, M])
    xpt = place("x_pt", 190, [P, MT, S])
    xr = place("x_r", 194, [P, S])
    xs = [place(f"x_s{i}", 196 + 2 * i, [P, S]) for i in range(2)]
    got_mem = m.fetch("in_mem", mem[:], t["memT"], ml_done)
    norm(mem, M, memhi, memlo, lambda k: col("g_mem", k), None, xs, xr, got_mem, ml_done)
    mem_ready = dve_now()

    def mem_tiles(dst, hi, lo, ready, scale=None):
        for u in range(SLOTS):
            b = prog.chunk % 4
            w = m.product_tile(b, hi, lo, ready, cols=M)
            m.free_bank(b, act.do(lambda e, j, u=u, b=b: e.activation(dst[:, j * SLOTS + u, :], bank[b][:, 0:M], ACT.Copy), w, ml_done))
    prog.loop_of(2, SLOTS, lambda: mem_tiles(xk, memhi, memlo, mem_ready))

    def mem_rows():
        for k0 in range(0, KT, 2):
            w = m.product_rows([0, 1], memhi, memlo, k0, 2, 512, KT, mem_ready)
        for tt in range(MT):
            m.free_bank(tt, act.do(lambda e, j, tt=tt: e.activation(xv[:, tt, bass.ds(j * 512, 512)], bank[tt][:], ACT.Copy), w, ml_done))
    prog.loop_of(2, SLOTS, mem_rows)
    xk_done = act_now()
    mem_done = used_now()
    xgate = place("x_gate", 104, [P, KT, S])

    gqk = small[:, 64:66]
    x = dve.do(lambda e, j: e.tensor_tensor(gqk, cols[:, COL_AT["q_norm_g"]:COL_AT["q_norm_g"] + 2],
                                            cols[:, COL_AT["k_norm_g"]:COL_AT["k_norm_g"] + 2], ALU.mult))
    gqk_set = dve.do(lambda e, j: e.tensor_scalar(gqk, gqk, X_HD ** -0.5, None, ALU.mult), x)

    def x_norms():
        for k in range(2):
            raw_tile(k, lambda j, k=k: xq[:, j * 2 + k, :], ml_done)
            squared = act.do(lambda e, j, k=k: e.activation(xsq[:, k, :], bank[k][:], ACT.Square), last("xsq read"))
            m.free_bank(k, squared)
        for k in range(2):
            raw_tile(2 + k, lambda j, k=k: xgate[:, j * 2 + k, :], mem_done)
        a = act.do(lambda e, j: e.activation(xsqk[:], xk[:, bass.ds(j * 2, 2), :], ACT.Square), xk_done, last("xsqk read"))

        def over_head(e, j):
            for k in range(2):
                i = e.matmul(bank[4][:, 0:M], ones, xsqk[:, k, :], start=(k == 0), stop=(k == 1))
            return i
        s_ = pe.do(over_head, a, m.bank_free(4))
        mark("xsqk read", s_)
        a = act.do(lambda e, j: e.activation(xr[:, 0:M], bank[4][:, 0:M], ACT.Sqrt, bias=epsc, scale=1.0 / X_HD), s_, last("xr read"))
        m.free_bank(4, a)
        x = dve.do(lambda e, j: e.reciprocal(xr[:, 0:M], xr[:, 0:M]), a)
        for k in range(2):
            x = dve.do(lambda e, j, k=k: e.scalar_tensor_tensor(xk[:, j * 2 + k, :], xk[:, j * 2 + k, :], gqk[:, k:k + 1], xr[:, 0:M],
                                                                ALU.mult, ALU.mult), x, gqk_set)
        mark("xr read", x)

        def columns(e, j):
            for tt in range(TT):
                for k in range(2):
                    i = e.matmul(bank[5][:, tt:tt + 1], xsq[:, k, tt * P:(tt + 1) * P], ones[:, 0:1], start=(k == 0), stop=(k == 1))
            return i
        c = pe.do(columns, squared, m.bank_free(5))
        mark("xsq read", c)
        m.free_bank(5, act.do(lambda e, j: e.activation(small[:, bass.ds(j * 4 + 68, 4)], bank[5][:, 0:TT], ACT.Sqrt, bias=epsc, scale=1.0 / X_HD), c))
    prog.loop_of(X_HEADS, SLOTS, x_norms)
    rq_set = dve.do(lambda e, j: e.reciprocal(small[:, 68:84], small[:, 68:84]), act_now())

    mxs, nb, rsum, rinv = small[:, 84:88], small[:, 88:92], small[:, 92:96], small[:, 96:100]

    def x_head():
        qs = dve.do(lambda e, j: e.tensor_copy(xqst[:], xq[:, bass.ds(j * 2, 2), :]), rq_set, last("xqst read"))
        vs = dve.do(lambda e, j: e.tensor_copy(xvst[:], xv[:, :, bass.ds(j * X_HD, X_HD)]), last("xvst read"))
        for tt in range(TT):
            def logits(e, j, tt=tt):
                for k in range(2):
                    i = e.matmul(bank[4 + tt][:, 0:M], xqst[:, k, tt * P:(tt + 1) * P], xk[:, j * 2 + k, :], start=(k == 0), stop=(k == 1))
                return i
            lg = pe.do(logits, qs, m.bank_free(4 + tt))
            x = dve.do(lambda e, j, tt=tt: e.tensor_reduce(mxs[:, tt:tt + 1], bank[4 + tt][:, 0:M], AX, ALU.max), lg, last("mxs read"))
        mark("xqst read", lg)
        on_act, on_dve = [], []
        for u in range(2):
            mod_chunk(u, lambda j, u=u: j * 4 + (32 + u), on_act, on_dve)
        x = dve.do(lambda e, j: e.scalar_tensor_tensor(nb, mxs, -1.0, small[:, bass.ds(j * 4 + 68, 4)], ALU.mult, ALU.mult), x, last("nb read"))
        mark("mxs read", x)
        for tt in range(TT):
            a = act.do(lambda e, j, tt=tt: e.activation(xp[:, tt, :], bank[4 + tt][:, 0:M], ACT.Exp, bias=nb[:, tt:tt + 1],
                                                        scale=small[:, bass.ds(j * 4 + (68 + tt), 1)], accum_out=rsum[:, tt:tt + 1]), x, last("xp read"))
            m.free_bank(4 + tt, a)
        mark("nb read", a)
        run_all(on_act)
        run_all(on_dve)
        x = dve.do(lambda e, j: e.reciprocal(rinv, rsum), a)
        for tt in range(TT):
            x2 = dve.do(lambda e, j, tt=tt: e.tensor_scalar(xp[:, tt, :], xp[:, tt, :], rinv[:, tt:tt + 1], None, ALU.mult), x)
        for mt in range(MT):
            def turn(e, j, mt=mt):
                for tt in range(TT):
                    i = e.transpose(bank[4 + mt][:, tt * P:(tt + 1) * P], xp[:, tt, mt * P:(mt + 1) * P], ident)
                return i
            tr = pe.do(turn, x2, m.bank_free(4 + mt))
            a = act.do(lambda e, j, mt=mt: e.activation(xpt[:, mt, :], bank[4 + mt][:], ACT.Copy), tr, last("xpt read"))
            m.free_bank(4 + mt, a)
        mark("xp read", tr)
        for u in range(2, 4):
            mod_chunk(u % 3, lambda j, u=u: j * 4 + (32 + u), on_act, on_dve)
        for c in range(2):
            def out(e, j, c=c):
                for mt in range(MT):
                    i = e.matmul(bank[6 + c][:], xvst[:, mt, c * P:(c + 1) * P], xpt[:, mt, :], start=(mt == 0), stop=(mt == MT - 1))
                return i
            y = pe.do(out, a, vs, m.bank_free(6 + c))
            m.free_bank(6 + c, m.split(lambda j, c=c: xhi[:, j * 2 + c, :], lambda j, c=c: xlo[:, j * 2 + c, :], lambda j, c=c: bank[6 + c][:], y))
        run_all(on_act)
        run_all(on_dve)
        mark("xpt read", y)
        mark("xvst read", y)
    prog.loop_of(X_HEADS, SLOTS, x_head)
    stored_gates(False, xgate, xhi, xlo, lambda i: colj("b_gate", i + 16))

    x_done = used_now()
    mixhi, mixlo = place("mixhi", 104, [P, KT, S], F32R), place("mixlo", 120, [P, KT, S], F32R)

    def split_all(hi, lo, src, n, *waits):
        def body():
            m.split(lambda j: hi[:, j, :], lambda j: lo[:, j, :], lambda j: src[:, j, :], *waits)
        prog.loop_of(n, 0, body)
        return dve_now()
    mix_ready = split_all(mixhi, mixlo, resid, KT, dve_now(), x_done)
    got_x = m.fetch("in_x_again", resid[:], t["xT"], mix_ready)

    def add_tiles(hi, lo, ready, *waits):
        for u in range(SLOTS):
            b = prog.chunk % 4
            w = m.product_tile(b, hi, lo, ready)
            m.free_bank(b, dve.do(lambda e, j, u=u, b=b: e.tensor_tensor(resid[:, j * SLOTS + u, :], bank[b][:], resid[:, j * SLOTS + u, :], ALU.add),
                                  w, *waits))
    prog.loop_of(2, SLOTS, lambda: add_tiles(mixhi, mixlo, mix_ready, got_x))

    out_done = used_now()
    sqb = [place(f"sqb{i}", 136 + 2 * i, [P, S]) for i in range(2)]
    norm(resid, S, hhi, hlo, lambda k: col("g_mlp", k), None, sqb, place("rb", 140, [P, S]), dve_now(), out_done)
    h_ready = dve_now()
    HALF = FF_TILES // 2
    uhi, ulo = place("ff_uhi", 104, [P, HALF, S], F32R), place("ff_ulo", 136, [P, HALF, S], F32R)
    fr = [place(f"ff_r{i}", 168 + 2 * i, [P, S]) for i in range(2)]
    ft = [place(f"ff_t{i}", 172 + 2 * i, [P, S]) for i in range(2)]

    def up_tiles(ready, free):
        for u in range(SLOTS):
            b, p = prog.chunk % 4, u % 2
            w = m.product_tile(b, hhi, hlo, ready)
            a = act.do(lambda e, j, b=b, p=p: e.activation(fr[p][:], bank[b][:], ACT.Relu), w, last(f"fr{p} read"))
            m.free_bank(b, a)
            x = dve.do(lambda e, j, p=p: e.tensor_tensor(ft[p][:], fr[p][:], fr[p][:], ALU.mult), a, last(f"ft{p} read"))
            mark(f"fr{p} read", x)
            mark(f"ft{p} read", m.split(lambda j, u=u: uhi[:, j * SLOTS + u, :], lambda j, u=u: ulo[:, j * SLOTS + u, :], lambda j, p=p: ft[p][:], x, free))

    def down(hi, lo, nk, ready, finish):
        for n in range(nk // 2):
            def mm(e, j, whi, wlo, n=n):
                for o in range(4):
                    for kk in range(2):
                        k, w = 2 * n + kk, slice((kk * 4 + o) * P, (kk * 4 + o + 1) * P)
                        e.matmul(bank[o][:], whi[:, w], hi[:, k, :], start=(k == 0), stop=False)
                        e.matmul(bank[o][:], whi[:, w], lo[:, k, :], start=False, stop=False)
                        i = e.matmul(bank[o][:], wlo[:, w], hi[:, k, :], start=False, stop=(k == nk - 1))
                return i
            w = m.take(mm, ready, *([m.bank_free(o) for o in range(4)] if n == 0 else []))
        for o in range(4):
            m.free_bank(o, finish(o, w))

    for half in range(2):
        free = used_now()
        prog.loop_of(HALF // SLOTS, SLOTS, lambda: up_tiles(h_ready, free))
        u_ready = dve_now()
        prog.loop_of(2, HALF // 2, lambda: down(uhi, ulo, HALF, u_ready, lambda o, w: dve.do(
            lambda e, j: e.tensor_tensor(resid[:, j * 4 + o, :], bank[o][:], resid[:, j * 4 + o, :], ALU.add), w)))

    ff_done = used_now()
    gsc = small[:, 100:148]
    x = dve_now()
    for w in range(2):
        x = dve.do(lambda e, j, w=w: e.tensor_tensor(mod[:, :, w], mod[:, :, w], cols[:, COL_AT["b_mod"]:COL_AT["b_mod"] + 48], ALU.add), x)
    SH1, SC1, G1, SH2, SC2, G2 = range(0, 48, 8)
    for at, which, gain, scale in ((0, 0, "norm1_g", SC1), (8, 1, "norm1_g", SC1), (16, 0, "norm2_g", SC2)):
        mod_ready = dve.do(lambda e, j, at=at, which=which, gain=gain, scale=scale: e.scalar_tensor_tensor(
            gsc[:, at:at + 8], mod[:, scale:scale + 8, which], 1.0, cols[:, COL_AT[gain]:COL_AT[gain] + 8], ALU.add, ALU.mult), x)

    ctx = place("ctx", 104, [P, KT, M])
    chi, clo = place("ctxhi", 112, [P, KT, M], F32R), place("ctxlo", 120, [P, KT, M], F32R)
    kctx = place("kctx", 198.25, [P, 2, M])
    vctx = place("vctx", 200.25, [P, MT, MIX])
    sqc = [place(f"sqc{i}", 128 + i, [P, M]) for i in range(2)]
    got_ctx = m.fetch("in_ctx", ctx[:], t["ctxT"], ff_done)
    norm(ctx, M, chi, clo, lambda k: gsc[:, 8 + k:9 + k], lambda k: mod[:, SH1 + k, 1:2], sqc, place("rc", 130, [P, M]), got_ctx, mod_ready)
    ctx_ready = dve_now()
    for i in range(2):
        b = prog.chunk % 4
        w = m.product_tile(b, chi, clo, ctx_ready, cols=M)
        m.free_bank(b, act.do(lambda e, j, i=i, b=b: e.activation(kctx[:, i, :], bank[b][:, 0:M], ACT.Copy), w))
    for k0 in (0, 4):
        w = m.product_rows([0, 1], chi, clo, k0, 4, MIX, KT, ctx_ready)
    for tt in range(MT):
        m.free_bank(tt, act.do(lambda e, j, tt=tt: e.activation(vctx[:, tt, :], bank[tt][:, 0:MIX], ACT.Copy), w))
    ctx_done = used_now()

    feats = place("feats", 156, [33, S])
    fw1, fw2, fw3 = place("fw1", 158, [33, 64]), place("fw2", 158.25, [64, 64]), place("fw3", 158.5, [65, 1024])
    fh1, fh2 = place("fh1", 162.5, [64, S]), place("fh2", 164.5, [65, S])
    fa, fb = place("fa", 166.5, [64, S]), place("fb", 168.5, [64, S])
    filt = place("filt", 138, [P, TT, 1024])
    window = place("window", 192, [P, TT, MIX])
    fabs = place("fabs", 188, [P, 1024])
    fnorm = place("fnorm", 154, [P, 512])
    psum_, pdif = place("fsum", 164, [P, TT, 512]), place("fdif", 180, [P, TT, 512])
    fsh, fsl, fdh, fdl = (place(n, k, [P, TT, 512], F32R) for n, k in (("fsh", 156), ("fsl", 164), ("fdh", 172), ("fdl", 180)))
    kr, ks_ = place("hy_kr", 138, [P, TT, 512]), place("hy_ks", 146, [P, TT, 512])
    kt_ = place("hy_kt", 196, [P, 512])
    got_f = [m.fetch(f"in_f{i}", dst, t[src], ff_done) for i, (dst, src) in enumerate(
        ((feats[:], "feats"), (fw1[:], "filt_w1"), (fw2[:], "filt_w2"), (fw3[:], "filt_w3"), (window[:], "window")))]
    one_row = dve.do(lambda e, j: e.memset(fh2[64:65, :], 1.0), ff_done)

    def sine(dst, ps, bias, *waits):
        f = cols[0:64, COL_AT["freq"]:COL_AT["freq"] + 1]
        x = dve.do(lambda e, j: e.tensor_scalar(fa[:], ps, bias, f, ALU.add, ALU.mult), *waits)
        x = dve.do(lambda e, j: e.tensor_scalar(fb[:], fa[:], 1.0 / TWO_PI, ROUND, ALU.mult, ALU.add), x)
        x = dve.do(lambda e, j: e.tensor_scalar(fb[:], fb[:], -ROUND, None, ALU.add), x)
        for part in TWO_PI_PARTS:
            x = dve.do(lambda e, j, part=part: e.scalar_tensor_tensor(fa[:], fb[:], -part, fa[:], ALU.mult, ALU.add), x)
        x = dve.do(lambda e, j: e.tensor_scalar(fa[:], fa[:], PI_BELOW, -PI_BELOW, ALU.min, ALU.max), x)
        return act.do(lambda e, j: e.activation(dst, fa[:], ACT.Sin), x)

    def filters(made):
        p1 = pe.do(lambda e, j: e.matmul(bank[4][0:64, :], fw1[:], feats[:], start=True, stop=True), got_f[0], got_f[1], m.bank_free(4))
        s1 = sine(fh1[:], bank[4][0:64, :], cols[0:64, COL_AT["filt_b1"]:COL_AT["filt_b1"] + 1], p1)
        yield
        p2 = pe.do(lambda e, j: e.matmul(bank[5][0:64, :], fw2[:], fh1[:], start=True, stop=True), s1, got_f[2], m.bank_free(5))
        s2 = sine(fh2[0:64, :], bank[5][0:64, :], cols[0:64, COL_AT["filt_b2"]:COL_AT["filt_b2"] + 1], p2)
        m.free_bank(4, s2)
        m.free_bank(5, s2)
        yield

        def absolute_sum(tt, ready):
            for half in range(2):
                b = 6 + half
                n = pe.do(lambda e, j, half=half, b=b: e.matmul(bank[b][:], ones, fabs[:, half * 512:(half + 1) * 512],
                                                                start=(tt == 0), stop=(tt == TT - 1)), ready, *([m.bank_free(b)] if tt == 0 else []))
            mark("fabs read", n)
            return n
        for tt in range(TT):
            for half in range(2):
                b = 4 + half
                p3 = pe.do(lambda e, j, tt=tt, half=half, b=b: e.matmul(bank[b][:], fh2[:, tt * P:(tt + 1) * P], fw3[:, half * 512:(half + 1) * 512],
                                                                        start=True, stop=True), s2, one_row, got_f[3], m.bank_free(b))
                for dd in range(2):
                    x = dve.do(lambda e, j, tt=tt, half=half, b=b, dd=dd: e.tensor_tensor(
                        filt[:, tt, half * 512 + dd * MIX:half * 512 + (dd + 1) * MIX], bank[b][:, dd * MIX:(dd + 1) * MIX], window[:, tt, :], ALU.mult), p3, got_f[4])
                m.free_bank(b, x)
            a = act.do(lambda e, j, tt=tt: e.activation(fabs[:], filt[:, tt, :], ACT.Abs), x, last("fabs read"))
            yield
            n = absolute_sum(tt, a)
        filt_made = x
        for o in range(2):
            a = act.do(lambda e, j, o=o: e.activation(fnorm[:, o * MIX:(o + 1) * MIX], bank[6 + o][:, 0:MIX], ACT.Copy), n)
            x = dve.do(lambda e, j, o=o: e.scalar_tensor_tensor(fnorm[:, o * MIX:(o + 1) * MIX], bank[6 + o][:, MIX:2 * MIX], EPS,
                                                                fnorm[:, o * MIX:(o + 1) * MIX], ALU.add, ALU.add), a)
            m.free_bank(6 + o, x)
        yield
        inv = dve.do(lambda e, j: e.reciprocal(fnorm[:], fnorm[:]), x)
        for o in range(2):
            z0 = dve.do(lambda e, j, o=o: e.memset(filt[0:1, 0, o * 512 + MIX:(o + 1) * 512], 0.0), n, filt_made)
        yield
        pooled = (pe_now(),)
        for tt in range(TT):
            for o in range(2):
                cs = slice(o * MIX, (o + 1) * MIX)
                fo, ba = slice(o * 512, o * 512 + MIX), slice(o * 512 + MIX, (o + 1) * 512)
                x = dve.do(lambda e, j, tt=tt, cs=cs, fo=fo, ba=ba: e.tensor_tensor(psum_[:, tt, cs], filt[:, tt, fo], filt[:, tt, ba], ALU.add), z0)
                x = dve.do(lambda e, j, tt=tt, cs=cs, fo=fo, ba=ba: e.tensor_tensor(pdif[:, tt, cs], filt[:, tt, fo], filt[:, tt, ba], ALU.subtract), z0, *pooled)
        yield
        m.split(lambda j: fsh[:], lambda j: fsl[:], lambda j: psum_[:], x)
        split_done = m.split(lambda j: fdh[:], lambda j: fdl[:], lambda j: pdif[:], x)
        norm_done = act.do(lambda e, j: e.activation(kt_[:], fnorm[:], ACT.Copy, scale=1.0 / S), inv)
        made.extend((split_done, norm_done))

    def spectrum(dst, hi, lo):
        for n in range(2):
            def mm(e, j, whi, wlo, n=n):
                for f in range(2):
                    for k in range(TT):
                        w = slice((f * TT + k) * P, (f * TT + k + 1) * P)
                        e.matmul(bank[2 * n + f][:], whi[:, w], hi[:, k, :], start=(k == 0), stop=False)
                        e.matmul(bank[2 * n + f][:], whi[:, w], lo[:, k, :], start=False, stop=False)
                        i = e.matmul(bank[2 * n + f][:], wlo[:, w], hi[:, k, :], start=False, stop=(k == TT - 1))
                return i
            w = m.take(mm, sd, *[m.bank_free(2 * n + f) for f in range(2)])
            for f in range(2):
                m.free_bank(2 * n + f, dve.do(lambda e, j, n=n, f=f: e.tensor_tensor(dst[:, 2 * n + f, :], bank[2 * n + f][:], kt_[:], ALU.mult), w, kn_set))

    sqd = [place(f"sqd{i}", 104 + 2 * i, [P, S]) for i in range(2)]
    norm(resid, S, hhi, hlo, lambda k: gsc[:, k:k + 1], lambda k: mod[:, SH1 + k, 0:1], sqd, place("rd", 108, [P, S]), dve_now(), ctx_done, act_now())
    h_ready = dve_now()
    pj = place("proj", 104, [P, 14, S])
    nv = place("na_v", 132, [P, TT, MIX])
    POOL, FNET, HY, NQ, NK = 0, 2, 4, 10, 12
    LEFT = 8
    plin = [place(f"pl{i}", 172 + 2.25 * i, [P, S + 2 * LEFT]) for i in range(3)]
    counts = place("counts", 178.75, [P, S])
    pw = place("pool_w", 180.75, [P, 2, P])
    got_counts = [m.fetch("in_counts", counts[:], t["pool_counts"][0], ff_done)]
    got_pw = m.fetch("in_pw", pw[:], t["pool_w"], ff_done)

    def pooling(i, stored):
        pin, s2t, s4t = plin
        x = dve.do(lambda e, j: e.memset(pin[:, 0:LEFT], 0.0), stored, last("pool read"))
        x = dve.do(lambda e, j: e.memset(pin[:, S + LEFT:S + 2 * LEFT], 0.0), last("pool read"))
        x = dve.do(lambda e, j, i=i: e.tensor_copy(pin[:, LEFT:S + LEFT], pj[:, POOL + i, :]), x)
        pn = S + 2 * LEFT

        def twice(dst, a_, w, x):
            return dve.do(lambda e, j: e.tensor_tensor(dst[:, 2 * w - 1:pn], a_[:, 2 * w - 1:pn], a_[:, w - 1:pn - w], ALU.add), x)
        if i == 0:
            x = twice(s2t, pin, 1, x)
            x4 = twice(s4t, s2t, 2, x)
            lo_, lo_off, hi_, hi_off = s2t, 0, s4t, 1
        else:
            x = twice(s2t, pin, 1, x)
            x = twice(s4t, s2t, 2, x)
            x = twice(s2t, s4t, 4, x)
            x4 = twice(s4t, s2t, 8, x)
            lo_, lo_off, hi_, hi_off = s2t, 3, s4t, 7
        x = x4
        for part, buf, off in ((slice(0, 64), lo_, lo_off), (slice(64, P), hi_, hi_off)):
            x = dve.do(lambda e, j, part=part, buf=buf, off=off: e.tensor_tensor(
                counts[part, :], buf[part, LEFT + off:LEFT + off + S], counts[part, :], ALU.mult), x, got_counts[i])
        x = dve.do(lambda e, j, i=i: e.tensor_tensor(counts[:], counts[:], pj[:, POOL + i, :], ALU.subtract), x)
        yield
        yield
        y = pe.do(lambda e, j: e.matmul(bank[4 + i][:], pw[:, i, :], counts[:], start=True, stop=True), x, got_pw, m.bank_free(4 + i))
        x = dve.do(lambda e, j, i=i: e.tensor_scalar(pj[:, POOL + i, :], bank[4 + i][:], col("pool_scale", i), None, ALU.mult), y)
        m.free_bank(4 + i, x)
        mark("pool read", x)
        if i == 0:
            got_counts.append(m.fetch("in_counts1", counts[:], t["pool_counts"][1], y))
        yield

    hpad = place("hy_pad", 203, [P, S + 2])
    dve.do(lambda e, j: e.memset(hpad[:, 0:1], 0.0), ff_done)
    pad_zero = dve.do(lambda e, j: e.memset(hpad[:, S + 1:S + 2], 0.0), ff_done)

    def short_convolution(i, stored):
        x = dve.do(lambda e, j: e.tensor_scalar(pj[:, HY + i, :], hpad[:, 0:S], col("hy_conv_w", i), col("hy_conv_b", i), ALU.mult, ALU.add), stored)
        for tap in (1, 2):
            x = dve.do(lambda e, j, tap=tap: e.scalar_tensor_tensor(pj[:, HY + i, :], hpad[:, tap:tap + S], col("hy_conv_w", 6 * tap + i),
                                                                    pj[:, HY + i, :], ALU.mult, ALU.add), x)
        mark("hpad read", x)

    made = []
    filter_steps = filters(made)
    beside = [filter_steps]
    for i in range(14):
        for steps in list(beside):
            if next(steps, "done") == "done":
                beside.remove(steps)
        b = prog.chunk % 4
        w = m.product_tile(b, hhi, hlo, h_ready)
        if HY <= i < NQ:
            stored = act.do(lambda e, j, b=b: e.activation(hpad[:, 1:S + 1], bank[b][:], ACT.Copy), w, pad_zero, last("hpad read"))
            short_convolution(i - HY, stored)
        else:
            stored = act.do(lambda e, j, i=i, b=b: e.activation(pj[:, i, :], bank[b][:], ACT.Copy), w)
        m.free_bank(b, stored)
        if i == POOL:
            beside.append(pooling(0, stored))
        elif i == POOL + 4:
            beside.append(pooling(1, tile1_stored))
        elif i == POOL + 1:
            tile1_stored = stored
    for k0 in (0, 4):
        w = m.product_rows([0, 1, 2, 3], hhi, hlo, k0, 4, MIX, KT, h_ready)
    for tt in range(TT):
        m.free_bank(tt, act.do(lambda e, j, tt=tt: e.activation(nv[:, tt, :], bank[tt][:, 0:MIX], ACT.Copy), w))
    pj_done = act_now()

    sd, kn_set = made
    spectrum(kr, fsh, fsl)
    spectrum(ks_, fdh, fdl)
    spectra = dve_now()

    spec_done = used_now()
    cs64 = place("cs64", 172, [P, 2 * P])
    got_cs = m.fetch("in_cs", cs64[:], t["cs64"], spec_done, pj_done)

    vh, vl = place("fn_vh", 164, [P, TT, 512], F32R), place("fn_vl", 154, [P, TT, 512], F32R)
    for tt in range(TT):
        for i in range(2):
            y = pe.do(lambda e, j, tt=tt, i=i: e.matmul(bank[4 + tt][:, i * 256:(i + 1) * 256], pj[:, FNET + i, tt * P:(tt + 1) * P], cs64[:],
                                                        start=(i == 0), stop=(i == 1), skip_group_check=True), pj_done, got_cs, m.bank_free(4 + tt))
        m.free_bank(4 + tt, m.split(lambda j, tt=tt: vh[:, tt, :], lambda j, tt=tt: vl[:, tt, :], lambda j, tt=tt: bank[4 + tt][:], y))
    v_ready = dve_now()

    def position_chunk(s, n, parts, ready, later=None):
        def mm(e, j, whi, wlo):
            for i in range(2):
                for kk in range(2):
                    w = slice(kk * 512, (kk + 1) * 512)
                    vhi, vlo = parts(2 * n + kk, i)
                    e.matmul(bank[i][:], vhi, whi[:, w], start=(s == 0 and n == 0 and kk == 0), stop=False)
                    e.matmul(bank[i][:], vlo, whi[:, w], start=False, stop=False)
                    ins = e.matmul(bank[i][:], vhi, wlo[:, w], start=False, stop=(s == 1 and n == 1 and kk == 1))
            return ins
        return m.take(mm, ready, *([m.bank_free(0), m.bank_free(1)] if s == n == 0 else []), later=later)

    def fourier_part(s):
        def part(k, i):
            w = slice(i * 256 + s * P, i * 256 + (s + 1) * P)
            return vh[:, k, w], vl[:, k, w]
        return part
    for s in range(2):
        for n in range(2):
            w = position_chunk(s, n, fourier_part(s), v_ready)
    for i in range(2):
        fnet_out = act.do(lambda e, j, i=i: e.activation(pj[:, FNET + i, :], bank[i][:], ACT.Copy), w)
        m.free_bank(i, fnet_out)
    fnet_done = used_now()

    NE = 2 * ROWS - 2
    bias = place("na_bias", 178, [P, NA_HEADS, NE * GRID])
    hide = place("na_hide", 192, [P, NE * GRID])
    got_hide = m.fetch("in_hide", hide[:], t["na_hide"], pj_done, spec_done)
    got_bias = m.fetch("in_bias", bias[:], t["rpb"], pj_done, spec_done)
    for h in range(NA_HEADS):
        x = dve.do(lambda e, j, h=h: e.tensor_tensor(bias[:, h, :], bias[:, h, :], hide[:], ALU.add), got_hide, got_bias)
    mix_in = x

    zh, zl = place("hy_zh", 154, [P, TT, MIX], F32R), place("hy_zl", 158, [P, TT, MIX], F32R)
    ych, ycl, yc = place("hy_ych", 154, [P, TT, MIX], F32R), place("hy_ycl", 158, [P, TT, MIX], F32R), place("hy_yc", 158, [P, TT, MIX])
    ysh, ysl, ys = place("hy_ysh", 162, [P, TT, MIX], F32R), place("hy_ysl", 166, [P, TT, MIX], F32R), place("hy_ys", 166, [P, TT, MIX])
    zc, zs = place("hy_zc", 170, [P, TT, MIX]), place("hy_zs", 174, [P, TT, MIX])
    t2 = place("hy_t2", 51, [P, 2, MIX])
    nvst = place("na_nvst", 49.5, [P, TT + MT, NA_HD])
    qz = [[place(f"na_q{hh}{i}", 136 + 0.5 * (2 * hh + i), [P, P]) for i in range(2)] for hh in range(2)]
    sc = place("na_sc", 192, [P, S + M])
    pr = place("na_p", 195, [P, S + M])
    prt = place("na_pt", 202.5, [P, TT + MT, P])
    nmx, nnb, nsum, ninv = (small[:, i:i + 1] for i in (160, 161, 162, 163))

    def hyena_order():
        turned = []
        for i, b in enumerate((2, 0)):
            def turn(e, j, i=i, b=b):
                for tt in range(TT):
                    ins = e.transpose(bank[b][:, tt * P:(tt + 1) * P], pj[:, HY + i, tt * P:(tt + 1) * P], ident)
                return ins
            turned.append(pe.do(turn, mix_in, last("hyena z made"), m.bank_free(b)))
        yield
        for i, b in enumerate((2, 0)):
            zsrc = lambda j, b=b: bank[b][:].rearrange("p (t c) -> p t c", t=TT)
            m.free_bank(b, m.split(lambda j, i=i: zh[:, :, i * P:(i + 1) * P], lambda j, i=i: zl[:, :, i * P:(i + 1) * P], zsrc,
                                   turned[i], fnet_done, last("hyena y read")))
        z_ready = dve_now()
        yield
        for dst in (zc, zs):
            on_act, used = [], []
            for n in range(2):
                def mm(e, j, whi, wlo, n=n):
                    for f in range(2):
                        for k in range(TT):
                            w = slice((f * TT + k) * P, (f * TT + k + 1) * P)
                            out = bank[n][:, f * MIX:(f + 1) * MIX]
                            e.matmul(out, whi[:, w], zh[:, k, :], start=(k == 0), stop=False, skip_group_check=True)
                            e.matmul(out, whi[:, w], zl[:, k, :], start=False, stop=False, skip_group_check=True)
                            ins = e.matmul(out, wlo[:, w], zh[:, k, :], start=False, stop=(k == TT - 1), skip_group_check=True)
                    return ins
                used.append(m.take(mm, z_ready, m.bank_free(n), later=on_act))
            yield
            for n in range(2):
                m.free_bank(n, act.do(lambda e, j, dst=dst, n=n: e.activation(dst[:, 2 * n:2 * n + 2, :], bank[n][:].rearrange("p (f c) -> p f c", f=2), ACT.Copy),
                                      used[n], fnet_done, last("spectrum read")))
            run_all(on_act)
            zdone, w = act_now(), used[-1]
            yield

        def times(y, a1, b1, a2, b2, op, g, *waits):
            cs = lambda j: bass.ds(j * MIX, MIX)
            x = dve.do(lambda e, j: e.tensor_tensor(y[:, g, :], a1[:, g, :], b1[:, g, cs(j)], ALU.mult), *waits)
            x = dve.do(lambda e, j: e.tensor_tensor(t2[:], a2[:, g, :], b2[:, g, cs(j)], ALU.mult), x)
            mark("spectrum read", x)
            return dve.do(lambda e, j: e.tensor_tensor(y[:, g, :], y[:, g, :], t2[:], op), x)

        def product(a1, b1, a2, b2, op, hi, lo, y):
            for g in (slice(0, 2), slice(2, 4)):
                x = times(y, a1, b1, a2, b2, op, g, zdone, w, last("hyena y read"))
            return m.split(lambda j: hi[:], lambda j: lo[:], lambda j: y[:], x)

        def part(hi, lo):
            return lambda k, i: (hi[:, k, i * P:(i + 1) * P], lo[:, k, i * P:(i + 1) * P])
        yield
        ready = product(zc, kr, zs, ks_, ALU.subtract, ych, ycl, yc)
        yield
        on_act = []
        for n in range(2):
            position_chunk(0, n, part(ych, ycl), ready, on_act)
        yield
        run_all(on_act)
        ready = product(zc, ks_, zs, kr, ALU.add, ysh, ysl, ys)
        yield
        for n in range(2):
            w_out = position_chunk(1, n, part(ysh, ysl), ready, on_act)
            yield
            run_all(on_act)
            if n == 0:
                yield
        mark("hyena y read", w_out)
        for i in range(2):
            x = dve.do(lambda e, j, i=i: e.scalar_tensor_tensor(pj[:, HY + i, :], pj[:, HY + i, :], colj("hy_skip", j * 2 + i), bank[i][:],
                                                                ALU.mult, ALU.add), w_out)
            m.free_bank(i, x)
            x = dve.do(lambda e, j, i=i: e.tensor_tensor(pj[:, HY + i, :], pj[:, HY + i, :], pj[:, j * 2 + (HY + 2 + i), :], ALU.mult), x)
        mark("hyena z made", x)
        yield

    for hh in range(2):
        for i in range(2):
            q_zero = dve.do(lambda e, j, hh=hh, i=i: e.memset(qz[hh][i][:], 0.0), pj_done, spec_done)

    def mixers():
        def scores(hh, tq):
            ph, at, q = slice(64 * hh, 64 * hh + 64), slice(tq * P, (tq + 1) * P), qz[hh][tq % 2]
            qs = dve.do(lambda e, j: e.tensor_copy(q[ph, :], pj[ph, j + NQ, at]), mix_in, q_zero, last(f"q{hh}{tq % 2} read"))
            s1 = pe.do(lambda e, j: e.matmul(bank[4][:], q[:], pj[:, j + NK, :], start=True, stop=True), qs, m.bank_free(4))
            s2 = pe.do(lambda e, j: e.matmul(bank[5][:, 0:M], q[:], kctx[:, j, :], start=True, stop=True), qs, m.bank_free(5))
            mark(f"q{hh}{tq % 2} read", s2)
            return s1, s2

        def stage_values(hh):
            act.do(lambda e, j: e.activation(nvst[:, 0:TT, :], nv[:, :, bass.ds(j * 2 * NA_HD + hh * NA_HD, NA_HD)], ACT.Copy), last("nvst read"))
            return act.do(lambda e, j: e.activation(nvst[:, TT:TT + MT, :], vctx[:, :, bass.ds(j * 2 * NA_HD + hh * NA_HD, NA_HD)], ACT.Copy))

        def softmax(hh, tq, s1, s2):
            rows_at = (TT - 1 - tq) * 2 * GRID
            x = dve.do(lambda e, j: e.scalar_tensor_tensor(sc[:, 0:S], bank[4][:], NA_HD ** -0.5, bias[:, j * 2 + hh, rows_at:rows_at + S],
                                                           ALU.mult, ALU.add), s1, mix_in, last("na sc read"))
            m.free_bank(4, x)
            x = dve.do(lambda e, j: e.tensor_scalar(sc[:, S:S + M], bank[5][:, 0:M], NA_HD ** -0.5, None, ALU.mult), s2)
            m.free_bank(5, x)
            x = dve.do(lambda e, j: e.tensor_reduce(nmx, sc[:], AX, ALU.max), x)
            x = dve.do(lambda e, j: e.tensor_scalar(nnb, nmx, -1.0, None, ALU.mult), x, last("na sc read"))
            a = act.do(lambda e, j: e.activation(pr[:], sc[:], ACT.Exp, bias=nnb, accum_out=nsum), x, last("na p read"))
            mark("na sc read", a)
            x = dve.do(lambda e, j: e.reciprocal(ninv, nsum), a)
            return dve.do(lambda e, j: e.tensor_scalar(pr[:], pr[:], ninv, None, ALU.mult), x)

        def outputs(hh, tq, probs):
            ph, at = slice(64 * hh, 64 * hh + 64), slice(tq * P, (tq + 1) * P)
            for b, k0, nk in ((6, 0, TT), (7, TT, MT)):
                def turn(e, j, b=b, k0=k0, nk=nk):
                    for k in range(nk):
                        ins = e.transpose(bank[b][:, k * P:(k + 1) * P], pr[:, (k0 + k) * P:(k0 + k + 1) * P], ident)
                    return ins
                tr = pe.do(turn, probs, m.bank_free(b))
                a = act.do(lambda e, j, b=b, k0=k0, nk=nk: e.activation(prt[:, k0:k0 + nk, :], bank[b][:, 0:nk * P].rearrange("p (k c) -> p k c", k=nk), ACT.Copy),
                           tr, last("prt read"), mix_in)
                m.free_bank(b, a)
            mark("na p read", tr)
            return a

        def weighted(hh, tq, staged):
            ph, at = slice(64 * hh, 64 * hh + 64), slice(tq * P, (tq + 1) * P)

            def out(e, j):
                for k in range(TT + MT):
                    ins = e.matmul(bank[3][ph, at], nvst[:, k, :], prt[:, k, :], start=(k == 0), stop=(k == TT + MT - 1), skip_group_check=True)
                return ins
            y = pe.do(out, staged, m.bank_free(3))
            mark("prt read", y)
            mark("nvst read", y)
            return y

        hyena = hyena_order()
        steps = [(hh, tq) for hh in range(2) for tq in range(TT)]
        scored = scores(*steps[0])
        for n, (hh, tq) in enumerate(steps):
            if tq == 0:
                stage_values(hh)
            next(hyena, None)
            probs = softmax(hh, tq, *scored)
            if n + 1 < len(steps):
                scored = scores(*steps[n + 1])
            staged = outputs(hh, tq, probs)
            next(hyena, None)
            y = weighted(hh, tq, staged)
        m.free_bank(3, act.do(lambda e, j: e.activation(pj[:, j + NQ, :], bank[3][:], ACT.Copy), y))
        for _ in hyena:
            pass

    prog.loop_of(2, 8, mixers)
    mixed, mixed_pe = (dve_now(), act_now()), (used_now(), pe_now())
    yhi2, ylo2 = place("yhi2", 154, [P, 8, S], F32R), place("ylo2", 170, [P, 8, S], F32R)
    for i, src in enumerate((POOL, POOL + 1, FNET, FNET + 1, HY, HY + 1, NQ, NQ + 1)):
        m.split(lambda j, i=i: yhi2[:, i, :], lambda j, i=i: ylo2[:, i, :], lambda j, src=src: pj[:, src, :], *mixed, *mixed_pe)
    y_ready = dve_now()

    mghi, mglo = place("mghi", 104, [P, KT, S], F32R), place("mglo", 120, [P, KT, S], F32R)
    gs = [place(f"gate{b}", 138 + 2 * b, [P, S]) for b in range(GATES2)]
    mg, mp = place("mg", 146, [P, S]), place("mgp", 148, [P, S])
    na_done = act_now()

    def merge_tiles():
        for u in range(4):
            for b in range(GATES2):
                w = m.product_tile(b, hhi, hlo, h_ready)
                g = act.do(lambda e, j, b=b: e.activation(gs[b][:], bank[b][:], ACT.Sigmoid), w, y_ready, last(f"gate{b} read"))
                m.free_bank(b, g)

            def mm(e, j, whi, wlo):
                for b in range(GATES2):
                    for k in range(2):
                        wt = slice((2 * b + k) * P, (2 * b + k + 1) * P)
                        e.matmul(bank[4 + b][:], whi[:, wt], yhi2[:, 2 * b + k, :], start=(k == 0), stop=False)
                        e.matmul(bank[4 + b][:], whi[:, wt], ylo2[:, 2 * b + k, :], start=False, stop=False)
                        ins = e.matmul(bank[4 + b][:], wlo[:, wt], yhi2[:, 2 * b + k, :], start=False, stop=(k == 1))
                return ins
            w = m.take(mm, y_ready, *[m.bank_free(4 + b) for b in range(GATES2)])
            x = dve.do(lambda e, j: e.tensor_tensor(mg[:], bank[4][:], gs[0][:], ALU.mult), w, g, last("mg read"))
            m.free_bank(4, x)
            mark("gate0 read", x)
            for b in range(1, GATES2):
                x = dve.do(lambda e, j, b=b: e.tensor_tensor(mp[:], bank[4 + b][:], gs[b][:], ALU.mult), x)
                m.free_bank(4 + b, x)
                mark(f"gate{b} read", x)
                x = dve.do(lambda e, j: e.tensor_tensor(mg[:], mg[:], mp[:], ALU.add), x)
            mark("mg read", m.split(lambda j, u=u: mghi[:, j * 4 + u, :], lambda j, u=u: mglo[:, j * 4 + u, :], lambda j: mg[:], x, na_done))
    prog.loop_of(2, 20, merge_tiles)
    mg_ready = dve_now()

    def gated_add(gate, store_at=None):
        return lambda b, at, w: dve.do(lambda e, j: e.scalar_tensor_tensor(resid[:, at(j), :], bank[b][:], mod[:, bass.ds(at(j) + gate, 1), 0:1].rearrange("p a b -> p (a b)"),
                                                                          resid[:, at(j), :], ALU.mult, ALU.add), w)

    def out_tiles():
        for u in range(SLOTS):
            b = prog.chunk % 4
            w = m.product_tile(b, mghi, mglo, mg_ready)
            m.free_bank(b, gated_add(G1)(b, lambda j, u=u: j * SLOTS + u, w))
    prog.loop_of(2, SLOTS, out_tiles)

    merged = used_now()
    sqe = [place(f"sqe{i}", 104 + 2 * i, [P, S]) for i in range(2)]
    norm(resid, S, hhi, hlo, lambda k: gsc[:, 16 + k:17 + k], lambda k: mod[:, SH2 + k, 0:1], sqe, place("re", 108, [P, S]), dve_now(), merged)
    h_ready = dve_now()
    fhi, flo = place("ffn_hi", 104, [P, FFN_TILES, S], F32R), place("ffn_lo", 148, [P, FFN_TILES, S], F32R)
    gpad = [place(f"gpad{i}", 192 + 2.25 * i, [P, S + 2]) for i in range(2)]
    gacc = [place(f"gacc{i}", 196.5 + 2 * i, [P, S]) for i in range(2)]
    gsg, gu = place("gsg", 200.5, [P, S]), place("gu", 203, [P, S])
    for i in range(2):
        x = dve.do(lambda e, j, i=i: e.memset(gpad[i][:, 0:1], 0.0), h_ready)
        gz = dve.do(lambda e, j, i=i: e.memset(gpad[i][:, S + 1:S + 2], 0.0), h_ready)

    def ffn_up():
        for p in range(2):
            b = prog.chunk % 4
            w = m.product_tile(b, hhi, hlo, h_ready)
            a = act.do(lambda e, j, b=b, p=p: e.activation(gpad[p][:, 1:S + 1], bank[b][:], ACT.Copy), w, gz, last(f"gpad{p} read"))
            m.free_bank(b, a)
            x = dve.do(lambda e, j, p=p: e.tensor_scalar(gacc[p][:], gpad[p][:, 0:S], colj("ffn_conv_w", j * 2 + p), colj("ffn_conv_b", j * 2 + p), ALU.mult, ALU.add),
                       a, last(f"gacc{p} read"))
            for tap in (1, 2):
                x = dve.do(lambda e, j, p=p, tap=tap: e.scalar_tensor_tensor(gacc[p][:], gpad[p][:, tap:tap + S], colj("ffn_conv_w", j * 2 + (p + tap * FFN_TILES)),
                                                                             gacc[p][:], ALU.mult, ALU.add), x)
            mark(f"gpad{p} read", x)
            a = act.do(lambda e, j, p=p: e.activation(gsg[:], gacc[p][:], ACT.Sigmoid), x, last("gsg read"))
            x = dve.do(lambda e, j, p=p: e.tensor_tensor(gacc[p][:], gacc[p][:], gsg[:], ALU.mult), a)
            mark("gsg read", x)
            b = prog.chunk % 4
            w = m.product_tile(b, hhi, hlo, h_ready)
            x = dve.do(lambda e, j, b=b, p=p: e.tensor_tensor(gu[:], bank[b][:], gacc[p][:], ALU.mult), w, x, last("gu read"))
            m.free_bank(b, x)
            mark(f"gacc{p} read", x)
            mark("gu read", m.split(lambda j, p=p: fhi[:, j * 2 + p, :], lambda j, p=p: flo[:, j * 2 + p, :], lambda j: gu[:], x))
    prog.loop_of(FFN_TILES // 2, SLOTS, ffn_up)
    f_ready = dve_now()
    for half in range(2):
        down(fhi, flo, FFN_TILES, f_ready, lambda o, w, half=half: gated_add(G2)(o, lambda j: half * 4 + o, w))

    done = used_now()
    result = place("result", 112, [P, KT, S])
    sqf = [place(f"sqf{i}", 104 + 2 * i, [P, S]) for i in range(2)]
    norm(resid, S, None, result, lambda k: col("final_g", k), None, sqf, place("rf", 108, [P, S]), dve_now(), done)
    out = m.fetch("out_done", t["out"], result[:], dve_now())
    m.load_chunks(m.total)
    assert prog.chunk == m.total, (prog.chunk, m.total)
    last_out = out

    with nc.Block() as block:
        block.tensor(pe.run)
        block.scalar(act.run)
        block.vector(dve.run)
        block.gpsimd(pool.run)

        @block.sync
        def _(e):
            sp.run(e)
            e.wait_ge(last_out.counter.sem, 16)



def stream_plan():
    plan = []
    full = list(range(KT))

    def tiles(w, first, n, ks=full):
        for i in range(n):
            plan.append((w, ks, first + i * P, P))

    def rows(w, first, width, n, k_tiles=KT):
        nk = CHUNK // width
        for i in range(n):
            for k0 in range(0, k_tiles, nk):
                plan.append((w, list(range(k0, k0 + nk)), first + i * width, width))

    def gated(gate_first, proj):
        for i in range(KT):
            tiles("w_in", gate_first + i * P, 1)
            tiles(proj, i * P, 1)
    sbq, sbk, sbv, mq, mk, mv, mo = (i * D for i in range(7))
    mi = 7 * D
    xq = mi + 2 * ML_HEADS
    gate = xq + D
    tiles("w_in", sbq, 8)
    tiles("w_in", sbk, 8)
    rows("w_in", sbv, 512, 2)
    for h in range(SB_HEADS):
        tiles("w_in", gate + h * P, 1)
        tiles("w_in", mo + h * P, 1)
        tiles("w_mod", 2 * h * P, 2)
    tiles("w_sb_proj", 0, 8)
    tiles("w_i", 0, 1)
    tiles("w_f", 0, 1)
    tiles("w_in", mq, 8)
    tiles("w_in", mk, 8)
    rows("w_in", mv, 512, 2)
    tiles("w_mod", 16 * P, 16)
    gated(gate + D, "w_ml_proj")
    tiles("w_mem_kv", 0, 8)
    rows("w_mem_kv", D, 512, 2)
    for h in range(X_HEADS):
        tiles("w_in", xq + h * X_HD, 2)
        tiles("w_in", gate + 2 * D + h * X_HD, 2)
    tiles("w_mod", 32 * P, 16)
    tiles("w_x_proj", 0, 8)
    tiles("w_out", 0, 8)
    for half in range(2):
        tiles("w_ff1", half * 2 * D, 16)
        for g in range(2):
            for n in range(FF_TILES // 4):
                k = half * (FF_TILES // 2) + 2 * n
                plan.append(("w_ff2", [k, k + 1], g * 512, 512))
    k_at = MIX * 6
    tiles("w_in_2", k_at, 2)
    rows("w_in_2", k_at + MIX, MIX, 1)
    tiles("w_in_2", 0, 14)
    rows("w_in_2", k_at + MIX, MIX, 1)
    for mat in ("cos0", "sin0"):
        for n in range(2):
            plan.append((mat, "pairs", 2 * n, P))
    for mat in ("fcos", "fsin"):
        rows(mat, 0, 512, 1, TT)
    for order in range(2):
        for mat in ("cos1", "sin1"):
            for n in range(2):
                plan.append((mat, "pairs", 2 * n, P))
        for mat in ("cos1", "sin1"):
            rows(mat, 0, 512, 1, TT)
    for i in range(KT):
        for b in range(GATES2):
            tiles("w_in_2", 8 * MIX + b * D + i * P, 1)
        plan.append(("w_branch", full, i * P, P))
    tiles("w_out_2", 0, 8)
    for i in range(FFN_TILES):
        tiles("w_up", FFN + i * P, 1)
        tiles("w_up", i * P, 1)
    for g in range(2):
        for n in range(FFN_TILES // 2):
            plan.append(("w_down", [2 * n, 2 * n + 1], g * 512, 512))
    return plan


def shape_constants():
    f = np.float32
    r = np.arange(P)
    before = (r[:, None] < r[None, :])
    sel = [np.where(r[:, None] == h, -1.0, 0.0) * np.ones((1, P)) for h in range(ML_HEADS)]
    consts = [np.eye(P), np.ones((P, P)), -np.ones((P, P)), np.where(r[:, None] >= r[None, :], -1.0, 0.0),
              np.where(before, 1.0, 0.0), np.where(before, 0.0, NEG), np.where(r[:, None] <= r[None, :], 0.0, NEG), *sel]
    out = {"consts": np.stack(consts, 1).astype(f)}
    n = np.arange(S)
    for name, a, b in (("0", 0.0, 0.5), ("1", 0.5, 0.5)):
        arg = 2 * np.pi * (n[:, None] + a) * (n[None, :] + b) / (2 * S)
        out["cos" + name], out["sin" + name] = np.cos(arg).astype(f), np.sin(arg).astype(f)
    arg = 2 * np.pi * (n[:, None] * n[None, :] % S) / S
    out["fcos"], out["fsin"] = np.cos(arg).astype(f), (-np.sin(arg)).astype(f)
    g = np.arange(64)
    arg = 2 * np.pi * (g[:, None] * g[None, :] % 64) / 64
    two = lambda a: np.kron(np.eye(2), a)
    out["cs64"] = (np.concatenate([two(np.cos(arg)), two(np.sin(arg))], 1) / np.sqrt(S * 64.0)).astype(f)
    win = np.array([2, 4, 8, 16])
    lo, hi = np.clip(n[None] - win[:, None] // 2, 0, S), np.clip(n[None] - win[:, None] // 2 + win[:, None], 0, S)
    out["pool_counts"] = np.repeat(1.0 / (hi - lo), 64, axis=0).reshape(2, P, S).astype(f)
    t = np.linspace(0.0, 1.0, S, dtype=f)[:, None]
    bands = np.linspace(1e-4, 15, 16, dtype=f)[None, :]
    ang = (f(2.0 * np.pi / S) * n.astype(f)[:, None] * bands).astype(f)
    out["feats"] = np.ascontiguousarray(np.concatenate([t, np.cos(ang), -np.sin(ang)], 1).T).astype(f)
    deltas = np.linspace(np.log(1e-2) / 1.5, np.log(1e-2) / 0.3, MIX, dtype=f)
    window = np.exp(-t * np.abs(deltas)) + f(0.05)
    out["window"] = np.ascontiguousarray(window.reshape(TT, P, MIX).transpose(1, 0, 2)).astype(f)
    c0 = np.clip(g - 8, 0, GRID - 16)
    ok = (g[None, :] >= c0[:, None]) & (g[None, :] < c0[:, None] + 16)
    out["na_hide"] = np.tile(np.where(ok, 0.0, NEG), (2, 2 * ROWS - 2)).astype(f)
    return out


def kernel(**inputs):
    from concourse import bacc
    from concourse.bass_utils import run_bass_kernel_spmd

    f = np.float32
    a = {k: np.asarray(v) for k, v in inputs.items()}
    const = shape_constants()

    def columns(v, n):
        return v.reshape(n, P).T

    def padded(v):
        out = np.zeros((P, 1), f)
        out[:v.size, 0] = v.reshape(-1)
        return out
    parts = {
        "g_mix": columns(a["g_mix"], 8), "b_gate": columns(a["b_gate"], 24), "conv_w": columns(a["conv_w"], 64),
        "conv_b": columns(a["conv_b"], 16), "ml_norm_g": columns(a["ml_norm_g"], 8), "g_mem": columns(a["g_mem"], 8),
        "q_norm_g": columns(a["q_norm_g"], 2), "k_norm_g": columns(a["k_norm_g"], 2), "g_mlp": columns(a["g_mlp"], 8),
        "norm1_g": columns(a["norm1_g_2"], 8), "norm2_g": columns(a["norm2_g_2"], 8), "b_mod": columns(a["b_mod_2"], 48),
        "c": columns(a["c_2"], 8), "c_ctx": columns(a["c_ctx_2"], 8), "pool_scale": columns(a["pool_scale_2"], 2),
        "hy_conv_w": columns(a["hyena_conv_w_2"], 18), "hy_conv_b": columns(a["hyena_conv_b_2"], 6),
        "hy_skip": columns(a["hyena_skip_2"], 4), "ffn_conv_w": columns(a["ffn_conv_w_2"], 66),
        "ffn_conv_b": columns(a["ffn_conv_b_2"], 22), "final_g": columns(a["final_norm_g_2"], 8),
        "b_i": padded(a["b_if"][0, :ML_HEADS]), "b_f": padded(a["b_if"][0, ML_HEADS:]),
        "filt_b1": padded(a["hyena_filt_b1_2"]), "filt_b2": padded(a["hyena_filt_b2_2"]), "freq": padded(a["hyena_freq_2"]),
    }
    gates_at = 7 * D
    w_i, w_f = np.zeros((D, P), f), np.zeros((D, P), f)
    w_i[:, :ML_HEADS] = a["w_in"][0][:, gates_at:gates_at + ML_HEADS]
    w_f[:, :ML_HEADS] = a["w_in"][0][:, gates_at + ML_HEADS:gates_at + 2 * ML_HEADS]
    mats = {"w_i": w_i, "w_f": w_f, "w_in_2": a["w_in_2"][0], "w_out_2": a["w_out_2"][0], "w_mod": a["w_mod_2"][0],
            "w_branch": a["w_branch_2"][0].reshape(GATES2 * MIX, D), "w_up": a["ffn_w_up_2"][0], "w_down": a["ffn_w_down_2"][0],
            **{n: a[n][0] for n in ("w_in", "w_mem_kv", "w_sb_proj", "w_ml_proj", "w_x_proj", "w_out", "w_ff1", "w_ff2")},
            **{n: const.pop(n) for n in ("cos0", "sin0", "cos1", "sin1", "fcos", "fsin")}}
    plan = stream_plan()
    stream = np.empty((len(plan), P, CHUNK), f)
    for dst, (name, ks, first, width) in zip(stream, plan):
        w = mats[name]
        if ks == "pairs":
            block = w.reshape(TT, P, TT, P)[:, :, first:first + 2].transpose(1, 2, 0, 3)
        else:
            block = w[ks[0] * P:(ks[-1] + 1) * P, first:first + width].reshape(len(ks), P, width).transpose(1, 0, 2)
        dst[:] = block.reshape(P, CHUNK)

    def turned(x, n):
        return np.ascontiguousarray(x.reshape(n, KT, P).transpose(2, 1, 0))
    pool_w = np.zeros((P, 2, P), f)
    for g in range(4):
        at = 64 * (g % 2)
        pool_w[at:at + 64, g // 2, at:at + 64] = a["pool_w_2"][0, g]
    table = np.zeros((NA_HEADS, 2 * ROWS - 1, 2 * GRID - 1), f)
    table[:, :, GRID - 16:GRID + 15] = a["na_rpb_2"][0]
    rpb = np.stack([table[:, 1 - low:2 * ROWS - 1 - low, GRID - 1 - cq:2 * GRID - 1 - cq] for low in range(2) for cq in range(GRID)])
    rpb = np.ascontiguousarray(rpb.reshape(P, NA_HEADS, (2 * ROWS - 2) * GRID))
    arrays = {
        "stream": stream, "xT": turned(a["x"], S), "memT": turned(a["mem"], M), "ctxT": turned(a["ctx_2"], M),
        "cols": np.ascontiguousarray(np.concatenate([parts[n] for n, _ in COLS], 1)), "pool_w": pool_w, "rpb": rpb,
        "filt_w1": a["hyena_filt_w1_2"][0], "filt_w2": a["hyena_filt_w2_2"][0],
        "filt_w3": np.concatenate([a["hyena_filt_w3_2"][0], a["hyena_filt_b3_2"]], 0), **const}
    nc = bacc.Bacc("TRN2", target_bir_lowering=False, num_devices=1)
    t = {n: nc.dram_tensor(f"in_{n}_dram", v.shape, mybir.dt.from_np(v.dtype), kind="ExternalInput").ap() for n, v in arrays.items()}
    t["out"] = nc.dram_tensor("out_dram", (P, KT, S), F32, kind="ExternalOutput").ap()
    program(nc, t)
    r = run_bass_kernel_spmd(nc, [{f"in_{n}_dram": v for n, v in arrays.items()}], core_ids=[0])
    out = r.results[0]["out_dram"]
    return np.ascontiguousarray(out.transpose(2, 1, 0)).reshape(1, S, D)
```

```python
from contextlib import ExitStack

import numpy as np
import concourse.bass as bass
from concourse import mybir

F32 = mybir.dt.float32
F32R = mybir.dt.float32r
ALU = mybir.AluOpType
ACT = mybir.ActivationFunctionType
AX = mybir.AxisListType.X

P = 128
D = 1024
KT = D // P
S = 512
TT = S // P
M = 256
MT = M // P
EPS = 1e-6
SB_HEADS, SB_HD = 8, 128
ML_HEADS, ML_HD = 4, 256
X_HEADS, X_HD = 4, 256
FF_TILES = 4 * D // P
MIX = 256
GATES2 = 4
NA_HEADS, NA_HD = 4, 64
GRID = 64
ROWS = S // GRID
FFN = 2816
FFN_TILES = FFN // P
NEG = -1e30

CHUNK = 1024
SLOTS = 4
LEAD = SLOTS - 1

COLS = [("g_mix", 8), ("b_gate", 24), ("conv_w", 64), ("conv_b", 16), ("ml_norm_g", 8), ("g_mem", 8),
        ("q_norm_g", 2), ("k_norm_g", 2), ("g_mlp", 8), ("norm1_g", 8), ("norm2_g", 8), ("b_mod", 48),
        ("c", 8), ("c_ctx", 8), ("pool_scale", 2), ("hy_conv_w", 18), ("hy_conv_b", 6), ("hy_skip", 4),
        ("ffn_conv_w", 66), ("ffn_conv_b", 22), ("final_g", 8), ("b_i", 1), ("b_f", 1),
        ("filt_b1", 1), ("filt_b2", 1), ("freq", 1)]
COL_AT, NCOLS = {}, 0
for _name, _n in COLS:
    COL_AT[_name] = NCOLS
    NCOLS += _n

CONSTS = ["ident", "ones", "neg_ones", "neg_lower", "keep_before", "hide_not_before", "hide_after",
          "sel0", "sel1", "sel2", "sel3"]


TWO_PI = 6.283185307179586
TWO_PI_PARTS = (6.28125, 0.0019350051879882812, TWO_PI - 6.28125 - 0.0019350051879882812)
ROUND = 1.5 * 2.0 ** 23
PI_BELOW = 3.1415925


class Counter:

    def __init__(self, sem, step=1):
        self.sem, self.step, self.n = sem, step, 0


class Event:

    def __init__(self, counter, k, loop=None, per=None):
        self.counter, self.k, self.loop, self.per = counter, k, loop, per

    def value(self, j, loop, back=0):
        if self.loop is None:
            return self.k
        per = self.loop.per[self.counter] if self.per is None else self.per
        if self.loop is not loop:
            return self.k + per * (self.loop.n - 1)
        if isinstance(j, int):
            return self.k + per * (j - back)
        return j * per + (self.k - per * back)

    def reached(self, loop, back=0):
        per = self.loop.per[self.counter] if self.loop and self.per is None else self.per or 0
        if self.loop is not None and self.loop is not loop:
            return self.k + per * (self.loop.n - 1)
        return self.k - per * back


class Last:

    def __init__(self, event, pending=None, name=None):
        self.event, self.pending, self.name = event, pending, name


class Loop:
    def __init__(self, prog, n, chunks):
        self.prog, self.n, self.chunks = prog, n, chunks
        self.bodies, self.per, self.base, self.marks, self.heads = {}, {}, {}, {}, {}


class Engine:

    def __init__(self, prog, sem):
        self.prog, self.steps, self.counter = prog, [], Counter(sem)

    def do(self, emit, *waits, counter=None):
        counter = counter or self.counter
        loop = self.prog.loop
        event = self.prog.count(counter)
        for w in waits:
            if isinstance(w, Last) and w.pending and w.event is not None:
                loop.heads.setdefault(self, []).append(w.event)
            elif loop and isinstance(w, Event) and w.loop is not loop:
                loop.heads.setdefault(self, []).append(w)
        if loop:
            waits = [w for w in waits if isinstance(w, Last) or w.loop is loop]

        def step(e, j):
            newest = {}
            for w in waits:
                back = 0
                if isinstance(w, Last):
                    if w.pending:
                        if w.name not in w.pending.marks:
                            continue
                        back, w = 1, w.pending.marks[w.name]
                    elif w.event is None:
                        continue
                    else:
                        w = w.event
                value, at = w.value(j, loop, back), w.reached(loop, back)
                if w.counter not in newest or at > newest[w.counter][0]:
                    newest[w.counter] = at, value
            for c, (_, value) in newest.items():
                if not isinstance(value, int) or value > 0:
                    e.wait_ge(c.sem, value)
            emit(e, j).then_inc(counter.sem, counter.step)

        (loop.bodies.setdefault(self, []) if loop else self.steps).append(step)
        return event

    def run(self, e):
        for s in self.steps:
            s(e, 0)


class Program:
    def __init__(self):
        self.loop, self.marks, self.chunk = None, {}, 0

    def count(self, counter):
        loop = self.loop
        if loop is None:
            counter.n += counter.step
            return Event(counter, counter.n)
        loop.base.setdefault(counter, counter.n)
        loop.per[counter] = loop.per.get(counter, 0) + counter.step
        return Event(counter, loop.base[counter] + loop.per[counter], loop)

    def mark(self, name, event):
        (self.loop.marks if self.loop else self.marks)[name] = event
        return event

    def last(self, name):
        if self.loop is None:
            return Last(self.marks.get(name))
        if name in self.loop.marks:
            return Last(self.loop.marks[name])
        return Last(self.marks.get(name), pending=self.loop, name=name)

    def loop_of(self, n, chunks, describe):
        if n == 0:
            return
        loop = self.loop = Loop(self, n, chunks)
        first = self.chunk
        describe()
        assert self.chunk == first + chunks and chunks % SLOTS == 0
        self.chunk = first + chunks * n
        self.loop = None
        for counter, per in loop.per.items():
            counter.n = loop.base[counter] + per * n
        self.marks.update(loop.marks)
        for engine, body in loop.bodies.items():
            def run(e, _, body=body, engine=engine):
                heads = {}
                for w in loop.heads.get(engine, []):
                    heads[w.counter] = max(heads.get(w.counter, 0), w.value(0, None))
                for c, value in heads.items():
                    if value > 0:
                        e.wait_ge(c.sem, value)
                if n == 1:
                    for s in body:
                        s(e, 0)
                else:
                    with e.Fori(0, n) as j:
                        for s in body:
                            s(e, j)
            engine.steps.append(run)


class Machine:

    def __init__(self, nc, total_chunks, stream):
        self.nc, self.prog, self.total, self.stream, self.loaded = nc, Program(), total_chunks, stream, 0
        sem = nc.alloc_semaphore
        self.pe, self.act, self.dve = (Engine(self.prog, sem(n)) for n in ("pe_done", "act_done", "dve_done"))
        self.pool, self.sp = (Engine(self.prog, sem(n)) for n in ("pool_done", "sp_done"))
        self.raw_in = [Counter(sem(f"raw_in{s}"), 16) for s in range(SLOTS)]
        self.hi_split, self.lo_split, self.used = (Counter(sem(n)) for n in ("hi_split", "lo_split", "chunk_used"))
        self.base = -(-nc.sbuf_base // 32) * 32 if isinstance(nc.sbuf_base, int) else 16896
        at = self.place
        self.raw = [at(f"raw{s}", 4 * s, [P, CHUNK]) for s in range(SLOTS)]
        self.whi = [at(f"whi{s}", 16 + 4 * s, [P, CHUNK], F32R) for s in range(SLOTS)]
        self.wlo = [at(f"wlo{s}", 32 + 4 * s, [P, CHUNK], F32R) for s in range(SLOTS)]
        self.bank = [nc.alloc_psum_tensor(f"bank{b}", [P, 512], F32) for b in range(8)]

    def place(self, name, kib, shape, dtype=F32):
        return self.nc.alloc_sbuf_tensor_at(name, shape, dtype, offset=self.base + int(kib * 1024))


    def chunk_event(self, counter, c):
        loop = self.prog.loop
        return Event(counter, c + 1, loop, loop.chunks if loop else 0) if loop else Event(counter, c + 1)

    def split_high(self, c):
        loop, slot = self.prog.loop, c % SLOTS
        raw = Event(self.raw_in[slot], 16 * (c // SLOTS + 1), loop, 16 * loop.chunks // SLOTS if loop else None)
        self.act.do(lambda e, j: e.activation(self.whi[slot][:], self.raw[slot][:], ACT.Copy),
                    raw, self.chunk_event(self.used, c - SLOTS), counter=self.hi_split)

    def take(self, matmuls, *waits, later=None):
        c, slot = self.prog.chunk, self.prog.chunk % SLOTS
        self.prog.chunk += 1
        if self.prog.loop or c + LEAD < self.total:
            if later is None:
                self.split_high(c + LEAD)
            else:
                later.append(lambda: self.split_high(c + LEAD))
        return self.pe.do(lambda e, j: matmuls(e, j, self.whi[slot], self.wlo[slot]),
                          self.chunk_event(self.lo_split, c), *waits, counter=self.used)

    def start_stream(self):
        for c in range(LEAD):
            self.split_high(c)

        def low_parts(e, _):
            with e.Fori(0, self.total // SLOTS) as j:
                for s in range(SLOTS):
                    e.wait_ge(self.hi_split.sem, j * SLOTS + (s + 1))
                    i = e.tensor_tensor(self.wlo[s][:], self.raw[s][:], self.whi[s][:].bitcast(F32), ALU.subtract)
                    i.then_inc(self.lo_split.sem, 1)
        self.pool.steps.append(low_parts)

    def load_chunks(self, upto):
        first, upto = self.loaded, min(upto, self.total)
        while self.loaded < min(SLOTS, upto) or (self.loaded < upto and self.loaded % SLOTS):
            c, s = self.loaded, self.loaded % SLOTS

            def one(e, _, c=c, s=s):
                if c >= SLOTS:
                    e.wait_ge(self.lo_split.sem, c - SLOTS + 1)
                e.dma_start(self.raw[s][:], self.stream[c]).then_inc(self.raw_in[s].sem, 16)
            self.sp.steps.append(one)
            self.loaded += 1
        rounds = (upto - self.loaded) // SLOTS
        if rounds > 0:
            def many(e, _, first=self.loaded, rounds=rounds):
                with e.Fori(0, rounds) as j:
                    for s in range(SLOTS):
                        e.wait_ge(self.lo_split.sem, j * SLOTS + (first - SLOTS + s + 1))
                        e.dma_start(self.raw[s][:], self.stream[j * SLOTS + (first + s)]).then_inc(self.raw_in[s].sem, 16)
            self.sp.steps.append(many)
            self.loaded += rounds * SLOTS
        while self.loaded < upto:
            c, s = self.loaded, self.loaded % SLOTS

            def one(e, _, c=c, s=s):
                e.wait_ge(self.lo_split.sem, c - SLOTS + 1)
                e.dma_start(self.raw[s][:], self.stream[c]).then_inc(self.raw_in[s].sem, 16)
            self.sp.steps.append(one)
            self.loaded += 1

    def fetch(self, name, dst, src, *waits):
        self.load_chunks(self.prog.chunk + SLOTS)
        return self.sp.do(lambda e, j: e.dma_start(dst, src), *waits, counter=Counter(self.nc.alloc_semaphore(name), 16))


    def bank_free(self, b):
        return self.prog.last(f"bank{b} free")

    def free_bank(self, b, event):
        self.prog.mark(f"bank{b} free", event)

    def product_tile(self, b, hi, lo, *waits, cols=S, later=None):
        def mm(e, j, whi, wlo):
            out = self.bank[b][:, 0:cols]
            for k in range(KT):
                w = slice(k * P, (k + 1) * P)
                e.matmul(out, whi[:, w], hi[:, k, 0:cols], start=(k == 0), stop=False)
                e.matmul(out, whi[:, w], lo[:, k, 0:cols], start=False, stop=False)
                i = e.matmul(out, wlo[:, w], hi[:, k, 0:cols], start=False, stop=(k == KT - 1))
            return i
        return self.take(mm, self.bank_free(b), *waits, later=later)

    def before_group(self):
        self.split_high(self.prog.chunk + LEAD)

    def product_group(self, hi, lo, ready, cols=S):
        c, slots = self.prog.chunk, [(self.prog.chunk + i) % SLOTS for i in range(4)]
        self.prog.chunk += 4
        free = [self.bank_free(b) for b in slots]

        def mm(k, slot):
            def one(e, j):
                out, w = self.bank[slot][:, 0:cols], slice(k * P, (k + 1) * P)
                e.matmul(out, self.whi[slot][:, w], hi[:, k, 0:cols], start=(k == 0), stop=False)
                e.matmul(out, self.whi[slot][:, w], lo[:, k, 0:cols], start=False, stop=False)
                return e.matmul(out, self.wlo[slot][:, w], hi[:, k, 0:cols], start=False, stop=(k == KT - 1))
            return one
        order = [(k, i) for k in range(2) for i in range(3)] + [(0, 3), (1, 3)] + [(k, i) for k in range(2, KT - 1) for i in range(4)]
        for k, i in order:
            first = [Event(self.lo_split, c + i + 1), free[i]] if k == 0 else []
            self.pe.do(mm(k, slots[i]), ready[k], *first)
        used = [(slot, self.pe.do(mm(KT - 1, slot), ready[KT - 1], counter=self.used)) for slot in slots]
        for i in range(4, 4 + LEAD):
            if c + i < self.total:
                self.split_high(c + i)
        return used

    def product_rows(self, banks, hi, lo, k0, nk, width, total_k, *waits, later=None):
        def mm(e, j, whi, wlo):
            for t, b in enumerate(banks):
                tok = slice(t * P, (t + 1) * P)
                out = self.bank[b][:, 0:width]
                for n in range(nk):
                    k, w = k0 + n, slice(n * width, (n + 1) * width)
                    e.matmul(out, hi[:, k, tok], whi[:, w], start=(k == 0), stop=False)
                    e.matmul(out, lo[:, k, tok], whi[:, w], start=False, stop=False)
                    i = e.matmul(out, hi[:, k, tok], wlo[:, w], start=False, stop=(k == total_k - 1))
            return i
        if k0 == 0:
            waits = (*waits, *(self.bank_free(b) for b in banks))
        return self.take(mm, *waits, later=later)

    def split(self, hi, lo, src, *waits):
        a = self.act.do(lambda e, j: e.activation(hi(j), src(j), ACT.Copy), *waits)
        return self.dve.do(lambda e, j: e.tensor_tensor(lo(j), src(j), hi(j).bitcast(F32), ALU.subtract), a)


def program(nc, t):
    plan = stream_plan()
    m = Machine(nc, len(plan), t["stream"])
    pe, act, dve, pool, sp = m.pe, m.act, m.dve, m.pool, m.sp
    prog, last, mark, place, bank = m.prog, m.prog.last, m.prog.mark, m.place, m.bank

    consts = place("consts", 48, [P, len(CONSTS), P])
    cols = place("cols", 53.5, [P, NCOLS])
    small = place("small", 55, [P, 256])
    C = {n: consts[:, i, :] for i, n in enumerate(CONSTS)}
    ident, ones = C["ident"], C["ones"]
    epsc = small[:, 255:256]

    def col(name, i=0):
        return cols[:, COL_AT[name] + i:COL_AT[name] + i + 1]

    hhi, hlo = place("hhi", 56, [P, KT, S], F32R), place("hlo", 72, [P, KT, S], F32R)
    resid = place("resid", 88, [P, KT, S])
    sig = [place(f"sig{i}", 184.5 + 2 * i, [P, S]) for i in range(2)]
    prod = place("prod", 188.5, [P, S])
    crhs = place("crhs", 206.5, [P, KT, 4], F32R)
    mod_row = place("mod_row", 172.75, [P, 256])
    mod_row_sb, mod_row_x = place("mod_row_sb", 183.25, [P, 256]), place("mod_row_x", 203, [P, 256])
    mod = place("mod", 206.625, [P, 48, 2])

    got_consts = m.fetch("in_consts", consts[:], t["consts"])
    got_cols = m.fetch("in_cols", cols[:], t["cols"])
    x0 = place("x0", 104, [P, KT, S])
    got_x = [m.fetch(f"in_x{i}", x0[:, 2 * i:2 * i + 2, :], t["xT"][:, 2 * i:2 * i + 2, :]) for i in range(KT // 2)]
    m.start_stream()
    eps_set = dve.do(lambda e, j: e.memset(epsc, EPS))

    class Norm:

        def __init__(self, name, src, n, at, bufs=2, sums=7):
            self.name, self.src, self.n, self.bank, self.squared = name, src, n, sums, []
            self.sq = [place(f"{name}_sq{i}", at + i * n / 256, [P, n]) for i in range(bufs)]
            self.r = place(f"{name}_r", at + bufs * n / 256, [P, n])

        def square(self, k, *ready):
            q = self.sq[k % len(self.sq)]
            self.squared.append((k, act.do(lambda e, j: e.activation(q[:], self.src[:, k, 0:self.n], ACT.Square),
                                           *ready, last(f"{self.name} sq{k % len(self.sq)} read"))))

        def add(self):
            k, a = self.squared.pop(0)
            q = self.sq[k % len(self.sq)]
            self.sum = pe.do(lambda e, j: e.matmul(bank[self.bank][:, 0:self.n], ones, q[:], start=(k == 0), stop=(k == KT - 1)),
                             a, got_consts, m.bank_free(self.bank))
            mark(f"{self.name} sq{k % len(self.sq)} read", self.sum)

        def root(self):
            n, r = self.n, self.r
            a = act.do(lambda e, j: e.activation(r[:], bank[self.bank][:, 0:n], ACT.Sqrt, bias=epsc, scale=1.0 / D), self.sum, eps_set)
            m.free_bank(self.bank, a)
            self.rr = dve.do(lambda e, j: e.reciprocal(r[:], r[:]), a, got_cols)

        def tile(self, k, hi, lo, gain, shift, *waits):
            q, n, src, r, g = self.sq[k % len(self.sq)], self.n, self.src, self.r, gain(k)
            s = None if shift is None else shift(k)
            x = dve.do(lambda e, j: e.scalar_tensor_tensor(q[:], src[:, k, 0:n], g, r[:], ALU.mult, ALU.mult),
                       self.rr, last(f"{self.name} sq{k % len(self.sq)} read"))
            if shift is None:
                a = act.do(lambda e, j: e.activation(hi[:, k, 0:n], q[:], ACT.Copy), x, *waits)
            else:
                a = act.do(lambda e, j: e.activation(hi[:, k, 0:n], q[:], ACT.Identity, bias=s), x, *waits)

            def low():
                if shift is None:
                    x = dve.do(lambda e, j: e.tensor_tensor(lo[:, k, 0:n], q[:], hi[:, k, 0:n].bitcast(F32), ALU.subtract), a)
                else:
                    x = dve.do(lambda e, j: e.scalar_tensor_tensor(lo[:, k, 0:n], q[:], s, hi[:, k, 0:n].bitcast(F32), ALU.add, ALU.subtract), a)
                return mark(f"{self.name} sq{k % len(self.sq)} read", x)
            return low

        def tiles(self, hi, lo, gain, shift, *waits, after={}, ks=range(KT)):
            events, low = [], None
            for k in ks:
                following = self.tile(k, hi, lo, gain, shift, *waits)
                if low:
                    events.append(low())
                low = following
                for step in after.get(k, ()):
                    step()
            return events + [low()]

    cin = cols[:, COL_AT["c"]:COL_AT["c"] + 16].rearrange("p (w k) -> p k w", w=2)
    cact, csg = (small[:, i:i + 16].rearrange("p (k w) -> p k w", w=2) for i in (184, 200))
    a = act.do(lambda e, j: e.activation(csg, cin, ACT.Sigmoid), got_cols)
    x = dve.do(lambda e, j: e.tensor_tensor(cact, csg, cin, ALU.mult), a)
    a = act.do(lambda e, j: e.activation(crhs[:, :, 0:2], cact, ACT.Copy), x)
    c_ready = dve.do(lambda e, j: e.tensor_tensor(crhs[:, :, 2:4], cact, crhs[:, :, 0:2].bitcast(F32), ALU.subtract), a)

    def mod_pair(b, row, at, *waits, later=None):
        for c in range(2):
            def mm(e, j, whi, wlo, c=c):
                for n in range(4):
                    k, w = 4 * c + n, slice(n * 256, (n + 1) * 256)
                    e.matmul(bank[b][0:4, 0:256], crhs[:, k, :], whi[:, w], start=(k == 0), stop=False, skip_group_check=True)
                    i = e.matmul(bank[b][0:2, 0:256], crhs[:, k, 0:2], wlo[:, w], start=False, stop=(k == KT - 1), skip_group_check=True)
                return i
            used = m.take(mm, c_ready, *([m.bank_free(b)] if c == 0 else []), later=later)
        made = []

        def copy():
            made.append(dve.do(lambda e, j: e.tensor_copy(row[0:4, :], bank[b][0:4, 0:256]), used, last("mod row read"), *waits))

        def turn():
            def both(e, j):
                for i in range(2):
                    ins = e.matmul(bank[b][:, 256 + 4 * i:260 + 4 * i], row[:, i * P:(i + 1) * P], ident[:, 0:4], start=True, stop=True)
                return ins
            made.append(mark("mod row read", pe.do(both, made[0], got_consts)))

        def add():
            m.free_bank(b, dve.do(lambda e, j: e.tensor_reduce(mod[:, bass.ds(at(j), 2), :], bank[b][:, 256:264].rearrange("p (t s w) -> p t w s", t=2, s=2),
                                                               AX, ALU.add), made[1]))
        return copy, turn, add

    def run_all(steps):
        for step in steps:
            step()
        steps.clear()

    def raw_tile(b, dst, *waits, on_act=None):
        w = m.product_tile(b, hhi, hlo, h_ready, later=on_act)
        store = lambda: m.free_bank(b, act.do(lambda e, j: e.activation(dst(j), bank[b][:], ACT.Copy), w, *waits))
        if on_act is None:
            store()
        else:
            on_act.append(store)

    def dve_now():
        return Event(dve.counter, dve.counter.n)

    def act_now():
        return Event(act.counter, act.counter.n)

    def pe_now():
        return Event(pe.counter, pe.counter.n)

    def used_now():
        return Event(m.used, m.used.n)

    norm = Norm("norm_mix", x0, S, 136)
    m.before_group()
    for k in range(KT):
        norm.square(k, got_x[k // 2])
        norm.add()
    norm.root()
    h_tiles = norm.tiles(hhi, hlo, lambda k: col("g_mix", k), None)
    h_ready = h_tiles[-1]

    q = place("sb_q", 104, [P, KT, S])
    kv = place("sb_kv", 120, [P, KT * S + TT * D])
    k_ = kv[:, 0:KT * S].rearrange("p (k s) -> p k s", k=KT)
    k_ahead = kv[:, S:(KT + 1) * S].rearrange("p (k s) -> p k s", k=KT)
    v = kv[:, KT * S:].rearrange("p (t d) -> p t d", t=TT)
    yhi, ylo = place("sb_yhi", 104, [P, KT, S], F32R), place("sb_ylo", 120, [P, KT, S], F32R)
    spl = place("sb_sp", 152, [P, 1280])
    att = place("sb_att", 157, [P, 1280])
    tmp = place("sb_tmp", 162, [P, 1280])

    def tiles_to(dst, scale, hi, lo, base=0):
        for u in range(SLOTS):
            b = prog.chunk % 4
            w = m.product_tile(b, hi, lo, h_ready)
            ev = act.do(lambda e, j, u=u, b=b: e.activation(dst[:, j * SLOTS + (u + base), :], bank[b][:], ACT.Copy, scale=scale), w)
            m.free_bank(b, ev)

    def rows_to(hi, lo, width, toks, store):
        nk = CHUNK // width
        for k0 in range(0, KT, nk):
            w = m.product_rows(list(range(toks)), hi, lo, k0, nk, width, KT, h_ready)
        for tt in range(toks):
            m.free_bank(tt, store(tt, bank[tt][:, 0:width], w))

    for u, (b, w) in enumerate(m.product_group(hhi, hlo, h_tiles)):
        m.free_bank(b, act.do(lambda e, j, u=u, b=b: e.activation(q[:, u, :], bank[b][:], ACT.Copy, scale=SB_HD ** -0.5), w, h_ready))
    tiles_to(q, SB_HD ** -0.5, hhi, hlo, base=4)
    prog.loop_of(2, SLOTS, lambda: tiles_to(k_, 1.0, hhi, hlo))
    prog.loop_of(2, SLOTS, lambda: rows_to(hhi, hlo, 512, TT, lambda tt, ps, w: act.do(
        lambda e, j: e.activation(v[:, tt, bass.ds(j * 512, 512)], ps, ACT.Copy), w)))
    sb_in = act_now()

    CUT = [0, 512, 896, 1152, 1280]
    mo = place("ml_o", 190.5, [P, KT, S])
    kst = place("sb_kst", 172, [P, S])
    vst = place("sb_vst", 174, [P, TT, P])

    def span(c):
        return slice(CUT[c], CUT[c + 1])

    def diag(c):
        return slice(CUT[c], CUT[c] + P)

    def sb_head():
        vs = dve.do(lambda e, j: e.tensor_copy(vst[:], v[:, :, bass.ds(j * P, P)]), sb_in, last("sb vst read"))
        for c in range(TT):
            z = pe.do(lambda e, j, c=c: e.matmul(bank[4 + c][:, 0:S - P * c], kst[:, c * P:(c + 1) * P], q[:, j, c * P:S],
                                                 start=True, stop=False, skip_group_check=True), last("sb kst made"), m.bank_free(4 + c))
        on_act = []
        raw_tile(0, lambda j: resid[:, j, :], on_act=on_act)
        raw_tile(1, lambda j: mo[:, j, :], on_act=on_act)
        for c in range(TT):
            a = act.do(lambda e, j, c=c: e.activation(tmp[:, span(c)], bank[4 + c][:, 0:S - P * c], ACT.Abs), z, last("sb tmp read"))
        a = act.do(lambda e, j: e.activation(tmp[:], tmp[:], ACT.Exp, scale=-1.0), a)
        a = act.do(lambda e, j: e.activation(tmp[:], tmp[:], ACT.Ln, bias=1.0), a)
        run_all(on_act)
        for c in range(TT):
            s1 = dve.do(lambda e, j, c=c: e.scalar_tensor_tensor(spl[:, span(c)], bank[4 + c][:, 0:S - P * c], 0.0, tmp[:, span(c)],
                                                                 ALU.max, ALU.add), a, last("sb spl read"))
        mark("sb tmp read", s1)
        for c in range(TT):
            s2 = dve.do(lambda e, j, c=c: e.tensor_tensor(spl[:, diag(c)], spl[:, diag(c)], C["keep_before"], ALU.mult), s1, got_consts)
        for c in range(TT):
            def sums(e, j, c=c):
                out = bank[4 + c]
                e.matmul(out[:, 0:P], ident, C["hide_not_before"], start=False, stop=False, skip_group_check=True)
                for jj in range(c, TT):
                    i = e.matmul(out[:, (jj - c) * P:S - P * c], C["neg_lower"] if jj == c else C["neg_ones"], spl[:, span(jj)],
                                 start=False, stop=(jj == TT - 1), skip_group_check=True)
                return i
            r = pe.do(sums, s2)
            x = act.do(lambda e, j, c=c: e.activation(att[:, span(c)], bank[4 + c][:, 0:S - P * c], ACT.Exp), r, last("sb att read"))
            m.free_bank(4 + c, x)
        mark("sb spl read", r)
        mark("sb kst made", dve.do(lambda e, j: e.tensor_copy(kst[:], k_ahead[:, j, :]), r))
        copy, turn, add = mod_pair(2, mod_row_sb, lambda j: j * 2, later=on_act)
        copy()
        for c in range(TT):
            y = pe.do(lambda e, j, c=c: e.matmul(bank[3][:, c * P:S], vst[:, c, :], att[:, span(c)], start=(c == 0), stop=(c == TT - 1),
                                                 skip_group_check=True), x, vs, m.bank_free(3))
        turn()
        mark("sb vst read", y)
        run_all(on_act)
        mark("sb att read", y)
        m.free_bank(3, m.split(lambda j: yhi[:, j, :], lambda j: ylo[:, j, :], lambda j: bank[3][:], y))
        add()

    dve.do(lambda e, j: e.memset(mod_row_sb[:], 0.0))
    mark("sb kst made", dve.do(lambda e, j: e.tensor_copy(kst[:], k_[:, 0, :]), sb_in))
    prog.loop_of(SB_HEADS, SLOTS, sb_head)

    def stored_gates(first, raw, bhi, blo, bias, sig=sig, prod=prod):
        y_ready, raw_in = dve_now(), act_now()

        def body():
            for u in range(SLOTS):
                b, half = prog.chunk % 4, u % 2
                g = act.do(lambda e, j, u=u, half=half: e.activation(sig[half][:], raw[:, j * SLOTS + u, :], ACT.Sigmoid, bias=bias(j * SLOTS + u)),
                           raw_in, y_ready, last(f"sig{half} read"))
                w = m.product_tile(b, bhi, blo, y_ready)
                if first:
                    x = dve.do(lambda e, j, b=b, u=u, half=half: e.tensor_tensor(resid[:, j * SLOTS + u, :], bank[b][:], sig[half][:], ALU.mult), w, g)
                    m.free_bank(b, x)
                else:
                    x = dve.do(lambda e, j, b=b, half=half: e.tensor_tensor(prod[:], bank[b][:], sig[half][:], ALU.mult), w, g, last("prod read"))
                    m.free_bank(b, x)
                    mark("prod read", dve.do(lambda e, j, u=u: e.tensor_tensor(resid[:, j * SLOTS + u, :], resid[:, j * SLOTS + u, :], prod[:], ALU.add), x))
                mark(f"sig{half} read", x)
        prog.loop_of(2, SLOTS, body)

    def colj(name, i):
        return cols[:, bass.ds(i + COL_AT[name], 1)]

    stored_gates(True, resid, yhi, ylo, lambda i: colj("b_gate", i))

    sb_done = used_now()
    mqk = place("ml_qk", 104, [P, 2 * KT, S])
    mq, mk = mqk[:, 0:KT, :], mqk[:, KT:2 * KT, :]
    hm = place("ml_hm", 120, [P, ML_HEADS, TT, ML_HD])
    mv = place("ml_v", 136, [P, TT, ML_HEADS, ML_HD + 1])
    wgt = place("ml_w", 152.25, [P, 1280])
    pmat = place("ml_p", 157.25, [P, 1280])
    kst2 = place("ml_kst", 162.25, [P, 2, S])
    r_i, r_f, r_t, r_a = (place(n, at, [P, S]) for n, at in (("ml_i", 174.5), ("ml_f", 166.25), ("ml_t", 176.5), ("ml_a", 178.5)))
    pad = [place(f"ml_pad{i}", 152.25 + 2.25 * i, [P, S + 3]) for i in range(2)]
    acc = [place(f"ml_acc{i}", 156.75 + 2 * i, [P, S]) for i in range(2)]
    csig = [place(f"ml_csig{i}", 160.75 + 2 * i, [P, S]) for i in range(2)]
    selst = place("ml_sel", 168.25, [P, P])
    dg = place("ml_dg", 168.75, [P, TT, P])
    sqst = [place(f"ml_sq{i}", 170.75 + i, [P, ML_HD]) for i in range(2)]
    mgate = place("ml_gate", 174.5, [P, KT, S])
    hst = place("ml_hst", 152.25, [P, TT, ML_HD])
    rows = [place(f"ml_row{i}", 156.25 + 2 * i, [P, S]) for i in range(2)]
    ml_sig = [place(f"ml_sig{i}", 162.25 + 2 * i, [P, S]) for i in range(2)], place("ml_prod", 166.25, [P, S])
    mhi, mlo = place("ml_yhi", 104, [P, KT, S], F32R), place("ml_ylo", 136, [P, KT, S], F32R)

    for i in range(2):
        zero = dve.do(lambda e, j, i=i: e.memset(pad[i][:, 0:3], 0.0), sb_done)
    onescol = dve.do(lambda e, j: e.memset(mv[:, :, :, ML_HD:ML_HD + 1], 1.0), sb_done)

    bi = prog.chunk % 4
    wi = m.product_tile(bi, hhi, hlo, h_ready)
    bf = prog.chunk % 4
    wf = m.product_tile(bf, hhi, hlo, h_ready)
    f1 = act.do(lambda e, j: e.activation(r_f[:], bank[bf][:], ACT.Identity, bias=col("b_f")), wf, sb_done)
    i1 = act.do(lambda e, j: e.activation(r_i[:], bank[bi][:], ACT.Identity, bias=col("b_i")), wi, sb_done)
    m.free_bank(bi, i1)
    m.free_bank(bf, f1)
    a = act.do(lambda e, j: e.activation(r_t[:], r_f[:], ACT.Abs), f1, i1)
    a = act.do(lambda e, j: e.activation(r_t[:], r_t[:], ACT.Exp, scale=-1.0), a)
    a = act.do(lambda e, j: e.activation(r_t[:], r_t[:], ACT.Ln, bias=1.0), a)
    x = dve.do(lambda e, j: e.scalar_tensor_tensor(r_f[:], r_f[:], 0.0, r_t[:], ALU.min, ALU.subtract), a)
    x1 = dve.do(lambda e, j: e.memset(r_a[:], 1.0), sb_done)
    x = dve.do(lambda e, j: e.tensor_tensor_scan(r_t[:], r_a[:], r_f[:], 0.0, ALU.mult, ALU.add), x, x1)
    x = dve.do(lambda e, j: e.tensor_tensor(r_i[:], r_i[:], r_t[:], ALU.subtract), x)
    x = dve.do(lambda e, j: e.tensor_tensor_scan(r_f[:], r_a[:], r_i[:], 0.0, ALU.mult, ALU.max), x)
    x = dve.do(lambda e, j: e.tensor_tensor(r_t[:], r_t[:], r_f[:], ALU.add), x)
    acol = small[:, 0:16].rearrange("p (t h) -> p t h", t=TT)
    gcol = small[:, 16:32].rearrange("p (t h) -> p t h", t=TT)
    gate_rows = x
    rows_in = act_now()

    def conv_tiles(dst, first):
        for u in range(SLOTS):
            b, p = prog.chunk % 4, u % 2
            w = m.product_tile(b, hhi, hlo, h_ready)
            a = act.do(lambda e, j, b=b, p=p: e.activation(pad[p][:, 3:S + 3], bank[b][:], ACT.Copy), w, zero, last(f"pad{p} read"))
            m.free_bank(b, a)
            x = dve.do(lambda e, j, u=u, p=p: e.tensor_scalar(acc[p][:], pad[p][:, 0:S], colj("conv_w", j * SLOTS + (u + first)),
                                                              colj("conv_b", j * SLOTS + (u + first)), ALU.mult, ALU.add), a, last(f"acc{p} read"))
            for tap in range(1, 4):
                x = dve.do(lambda e, j, u=u, p=p, tap=tap: e.scalar_tensor_tensor(
                    acc[p][:], pad[p][:, tap:tap + S], colj("conv_w", j * SLOTS + (u + first + 16 * tap)), acc[p][:], ALU.mult, ALU.add), x)
            mark(f"pad{p} read", x)

            def finish(u=u, p=p, x=x):
                a = act.do(lambda e, j: e.activation(csig[p][:], acc[p][:], ACT.Sigmoid), x, last(f"csig{p} read"))
                x = dve.do(lambda e, j: e.tensor_tensor(dst[:, j * SLOTS + u, :], acc[p][:], csig[p][:], ALU.mult), a, sb_done)
                mark(f"acc{p} read", x)
                mark(f"csig{p} read", x)
            if u:
                finish_last()
            finish_last = finish
        finish_last()

    prog.loop_of(2, SLOTS, lambda: rows_to(hhi, hlo, 512, TT, lambda tt, ps, w: act.do(
        lambda e, j: e.activation(mv[:, tt, bass.ds(j * 2, 2), 0:ML_HD], ps.rearrange("p (h d) -> p h d", h=2), ACT.Copy), w, sb_done)))

    def with_out_gates():
        conv_tiles(mqk, 0)
        for u in range(2):
            act.do(lambda e, j, u=u: e.activation(mo[:, j * 2 + u, :], mo[:, j * 2 + u, :], ACT.Sigmoid), act_now())
    prog.loop_of(4, SLOTS, with_out_gates)
    conv_done = dve_now()
    for tt in range(TT):
        pe.do(lambda e, j, tt=tt: e.transpose(bank[4][:, tt * P:(tt + 1) * P], r_i[:, tt * P:(tt + 1) * P], ident), gate_rows, m.bank_free(4))
        tg = pe.do(lambda e, j, tt=tt: e.transpose(bank[5][:, tt * P:(tt + 1) * P], r_t[:, tt * P:(tt + 1) * P], ident), gate_rows, m.bank_free(5))
    ac = act.do(lambda e, j: e.activation(acol, bank[4][:].rearrange("p (t c) -> p t c", t=TT)[:, :, 0:ML_HEADS], ACT.Copy), tg)
    m.free_bank(4, ac)
    gc = act.do(lambda e, j: e.activation(gcol, bank[5][:].rearrange("p (t c) -> p t c", t=TT)[:, :, 0:ML_HEADS], ACT.Exp, scale=-1.0), tg)
    m.free_bank(5, gc)
    ml_in = act_now()

    ssq = small[:, 32:48]
    den = small[:, 48:52]
    rden = small[:, 52:56]

    def ml_head():
        sl = dve.do(lambda e, j: e.tensor_copy(selst[:], consts[:, j + CONSTS.index("sel0"), :]), last("selst read"))
        ks = dve.do(lambda e, j: e.tensor_copy(kst2[:], mk[:, bass.ds(j * 2, 2), :]), conv_done, last("ml kst read"))
        mx = pe.do(lambda e, j: e.matmul(bank[3][:], selst[:], r_f[:], start=True, stop=True), sl, ml_in, m.bank_free(3))
        mark("selst read", mx)
        for c in range(TT):
            def scores(e, j, c=c):
                for k in range(2):
                    i = e.matmul(bank[4 + c][:, 0:S - P * c], kst2[:, k, c * P:(c + 1) * P], mq[:, j * 2 + k, c * P:S],
                                 start=(k == 0), stop=(k == 1))
                return i
            sc = pe.do(scores, ks, m.bank_free(4 + c))
        mark("ml kst read", sc)
        on_act = []
        raw_tile(0, lambda j: mgate[:, j * 2, :], rows_in, on_act=on_act)
        for c in range(TT):
            d = dve.do(lambda e, j, c=c: e.tensor_tensor(dg[:, c, :], bank[3][:, c * P:(c + 1) * P], C["hide_after"], ALU.add), mx, last("dg read"))
        for c in range(TT):
            a = act.do(lambda e, j, c=c: e.activation(wgt[:, diag(c)], dg[:, c, :], ACT.Exp, bias=small[:, bass.ds(j + c * 4, 1)]),
                       d, ac, last("wgt read"))
            if c < TT - 1:
                a = act.do(lambda e, j, c=c: e.activation(wgt[:, CUT[c] + P:CUT[c + 1]], bank[3][:, (c + 1) * P:S], ACT.Exp,
                                                          bias=small[:, bass.ds(j + c * 4, 1)]))
        mark("dg read", a)
        m.free_bank(3, a)
        for c in range(TT):
            x = dve.do(lambda e, j, c=c: e.scalar_tensor_tensor(pmat[:, span(c)], bank[4 + c][:, 0:S - P * c], ML_HD ** -0.5, wgt[:, span(c)],
                                                                ALU.mult, ALU.mult), sc, a, last("pmat read"))
        mark("wgt read", x)
        run_all(on_act)
        for i in range(TT):
            def sums(e, j, i=i):
                for c in range(i + 1):
                    at = CUT[c] + (i - c) * P
                    ins = e.matmul(bank[4 + i][:, 0:ML_HD + 1], pmat[:, at:at + P], mv[:, c, j, :], start=(c == 0), stop=(c == i))
                return ins
            n = pe.do(sums, x, onescol)
            d = act.do(lambda e, j, i=i: e.activation(den[:, i:i + 1], bank[4 + i][:, ML_HD:ML_HD + 1], ACT.Abs), n, last("den read"))
            d = dve.do(lambda e, j, i=i: e.tensor_scalar(den[:, i:i + 1], den[:, i:i + 1], small[:, bass.ds(j + (16 + i * 4), 1)], None, ALU.max), d, gc)
            d = dve.do(lambda e, j, i=i: e.reciprocal(rden[:, i:i + 1], den[:, i:i + 1]), d, last("rden read"))
            a = act.do(lambda e, j, i=i: e.activation(hm[:, j, i, :], bank[4 + i][:, 0:ML_HD], ACT.Copy, scale=rden[:, i:i + 1]), d, ks)
            m.free_bank(4 + i, a)
            a2 = act.do(lambda e, j, i=i: e.activation(sqst[i % 2][:], hm[:, j, i, :], ACT.Square, accum_out=small[:, bass.ds(j + (32 + i * 4), 1)]), a, last(f"sqst{i % 2}"))
            mark(f"sqst{i % 2}", a2)
        copy, turn, add = mod_pair(2, mod_row, lambda j: j * 2 + 16)
        copy()
        raw_tile(1, lambda j: mgate[:, j * 2 + 1, :], rows_in)
        turn()
        add()
        mark("rden read", a)
        mark("den read", d)
        mark("pmat read", n)

    dve.do(lambda e, j: e.memset(mod_row[:], 0.0), conv_done)
    prog.loop_of(ML_HEADS, SLOTS, ml_head)
    a = act.do(lambda e, j: e.activation(ssq, ssq, ACT.Sqrt, bias=epsc, scale=1.0 / ML_HD), act_now())
    rms = dve.do(lambda e, j: e.reciprocal(ssq, ssq), a)
    v_read = pe_now()

    def ml_out():
        pairs = [mod_pair(i, mod_row, lambda j, i=i: j * 4 + (24 + 2 * i)) for i in range(2)]
        for hh in range(2):
            for i in range(TT):
                x = dve.do(lambda e, j, i=i, hh=hh: e.tensor_scalar(hst[:, i, :], hm[:, j * 2 + hh, i, :], small[:, bass.ds(j * 2 + (32 + i * 4 + hh), 1)], None, ALU.mult),
                           rms, v_read, last("hst turned"))
            pairs[hh][0]()
            scaled = []
            for c in range(2):
                b = 4 + 2 * hh + c

                def turn(e, j, b=b, c=c):
                    for i in range(TT):
                        ins = e.transpose(bank[b][:, i * P:(i + 1) * P], hst[:, i, c * P:(c + 1) * P], ident)
                    return ins
                tr = pe.do(turn, x, m.bank_free(b))
                tile = lambda j, hh=hh, c=c: j * 4 + (2 * hh + c)
                y = dve.do(lambda e, j, c=c, b=b, tile=tile: e.scalar_tensor_tensor(rows[c][:], bank[b][:], colj("ml_norm_g", tile(j)), mo[:, tile(j), :],
                                                                                    ALU.mult, ALU.mult), tr, v_read, last(f"row{c} read"))
                m.free_bank(b, y)
                scaled.append((c, tile, y))
            mark("hst turned", tr)
            for c, tile, y in scaled:
                mark(f"row{c} read", m.split(lambda j, tile=tile: mhi[:, tile(j), :], lambda j, tile=tile: mlo[:, tile(j), :], lambda j, c=c: rows[c][:], y))
            pairs[hh][1]()
            pairs[hh][2]()

    prog.loop_of(ML_HEADS // 2, SLOTS, ml_out)
    stored_gates(False, mgate, mhi, mlo, lambda i: colj("b_gate", i + 8), *ml_sig)

    ml_done = used_now()
    mem = place("x_mem", 104, [P, KT, M])
    memhi, memlo = place("x_memhi", 112, [P, KT, M], F32R), place("x_memlo", 120, [P, KT, M], F32R)
    xk = place("x_k", 128, [P, KT, M])
    xv = place("x_v", 136, [P, MT, D])
    xq = place("x_q", 144, [P, KT, S])
    xhi, xlo = place("x_yhi", 144, [P, KT, S], F32R), place("x_ylo", 160, [P, KT, S], F32R)
    xsq = [place(f"x_sq{i}", 176 + 4 * i, [P, 2, S]) for i in range(2)]
    xsqk = place("x_sqk", 200, [P, 2, M])
    xqst = place("x_qst", 180, [P, 2, S])
    xvst = place("x_vst", 184, [P, MT, X_HD])
    xp = place("x_p", 186, [P, TT, M])
    xpt = place("x_pt", 190, [P, MT, S])
    xr = place("x_r", 194, [P, S])
    got_mem = m.fetch("in_mem", mem[:], t["memT"], ml_done)
    row_zero = dve.do(lambda e, j: e.memset(mod_row_x[:], 0.0), ml_done)
    norm = Norm("norm_mem", mem, M, 196)
    for h in range(X_HEADS):
        for k in range(2):
            b = 2 * (h % 2) + k
            raw_tile(b, lambda j, i=2 * h + k: xq[:, i, :], ml_done)
            squared = act.do(lambda e, j, k=k, b=b, h=h: e.activation(xsq[h % 2][:, k, :], bank[b][:], ACT.Square), last(f"xsq{h % 2} read"))
            m.free_bank(b, squared)
        copy, turn, add = mod_pair(4, mod_row_x, lambda j, h=h: 32 + 2 * h, ml_done, row_zero)
        if 1 <= h < 3:
            for k in range(4 * (h - 1), 4 * h):
                norm.square(k, got_mem)
                norm.add()
        if h == 2:
            norm.root()
        copy()

        def columns(e, j, h=h):
            for tt in range(TT):
                for k in range(2):
                    i = e.matmul(bank[5][:, tt:tt + 1], xsq[h % 2][:, k, tt * P:(tt + 1) * P], ones[:, 0:1], start=(k == 0), stop=(k == 1))
            return i
        c = mark(f"xsq{h % 2} read", pe.do(columns, squared, m.bank_free(5)))
        m.free_bank(5, act.do(lambda e, j, h=h: e.activation(small[:, 68 + 4 * h:72 + 4 * h], bank[5][:, 0:TT], ACT.Sqrt, bias=epsc, scale=1.0 / X_HD), c))
        turn()
        add()
    m.before_group()
    mem_tiles = norm.tiles(memhi, memlo, lambda k: col("g_mem", k), None, ml_done)
    mem_ready = mem_tiles[-1]

    gqk = small[:, 64:66]
    x = dve.do(lambda e, j: e.tensor_tensor(gqk, cols[:, COL_AT["q_norm_g"]:COL_AT["q_norm_g"] + 2],
                                            cols[:, COL_AT["k_norm_g"]:COL_AT["k_norm_g"] + 2], ALU.mult))
    gqk_set = dve.do(lambda e, j: e.tensor_scalar(gqk, gqk, X_HD ** -0.5, None, ALU.mult), x)
    group = m.product_group(memhi, memlo, mem_tiles, cols=M)
    for i in range(KT):
        b, w = group[i] if i < 4 else (prog.chunk % 4, m.product_tile(prog.chunk % 4, memhi, memlo, mem_ready, cols=M))
        stored = act.do(lambda e, j, i=i, b=b: e.activation(xk[:, i, :], bank[b][:, 0:M], ACT.Copy), w, ml_done)
        m.free_bank(b, stored)

    def key_norm(h):
        a = act.do(lambda e, j: e.activation(xsqk[:], xk[:, 2 * h:2 * h + 2, :], ACT.Square), stored, last("xsqk read"))

        def over_head(e, j):
            for k in range(2):
                i = e.matmul(bank[4][:, 0:M], ones, xsqk[:, k, :], start=(k == 0), stop=(k == 1))
            return i
        s_ = mark("xsqk read", pe.do(over_head, a, m.bank_free(4)))
        a = act.do(lambda e, j: e.activation(xr[:, 0:M], bank[4][:, 0:M], ACT.Sqrt, bias=epsc, scale=1.0 / X_HD), s_, last("xr read"))
        m.free_bank(4, a)
        x = dve.do(lambda e, j: e.reciprocal(xr[:, 0:M], xr[:, 0:M]), a)
        for k in range(2):
            x = dve.do(lambda e, j, k=k: e.scalar_tensor_tensor(xk[:, 2 * h + k, :], xk[:, 2 * h + k, :], gqk[:, k:k + 1], xr[:, 0:M],
                                                                ALU.mult, ALU.mult), x, gqk_set)
        mark("xr read", x)

    for half in range(2):
        for k0 in range(0, KT, 2):
            w = m.product_rows([2 * half, 2 * half + 1], memhi, memlo, k0, 2, 512, KT, mem_ready)
            if k0 % 4 == 0:
                key_norm(2 * half + k0 // 4)
        for tt in range(MT):
            b = 2 * half + tt
            m.free_bank(b, act.do(lambda e, j, tt=tt, b=b, half=half: e.activation(xv[:, tt, half * 512:(half + 1) * 512], bank[b][:], ACT.Copy), w, ml_done))
    mem_done = used_now()
    xgate = place("x_gate", 104, [P, KT, S])
    rq_set = dve.do(lambda e, j: e.reciprocal(small[:, 68:84], small[:, 68:84]), act_now())

    mxs, nb, rsum, rinv = small[:, 84:88], small[:, 88:92], small[:, 92:96], small[:, 96:100]

    def x_head():
        qs = dve.do(lambda e, j: e.tensor_copy(xqst[:], xq[:, bass.ds(j * 2, 2), :]), rq_set, last("xqst read"))
        vs = dve.do(lambda e, j: e.tensor_copy(xvst[:], xv[:, :, bass.ds(j * X_HD, X_HD)]), last("xvst read"))
        for tt in range(TT):
            def logits(e, j, tt=tt):
                for k in range(2):
                    i = e.matmul(bank[4 + tt][:, 0:M], xqst[:, k, tt * P:(tt + 1) * P], xk[:, j * 2 + k, :], start=(k == 0), stop=(k == 1))
                return i
            lg = pe.do(logits, qs, m.bank_free(4 + tt))
            x = dve.do(lambda e, j, tt=tt: e.tensor_reduce(mxs[:, tt:tt + 1], bank[4 + tt][:, 0:M], AX, ALU.max), lg, last("mxs read"))
        mark("xqst read", lg)
        on_act = []
        raw_tile(0, lambda j: xgate[:, j * 2, :], mem_done, on_act=on_act)
        x = dve.do(lambda e, j: e.scalar_tensor_tensor(nb, mxs, -1.0, small[:, bass.ds(j * 4 + 68, 4)], ALU.mult, ALU.mult), x, last("nb read"))
        mark("mxs read", x)
        for tt in range(TT):
            a = act.do(lambda e, j, tt=tt: e.activation(xp[:, tt, :], bank[4 + tt][:, 0:M], ACT.Exp, bias=nb[:, tt:tt + 1],
                                                        scale=small[:, bass.ds(j * 4 + (68 + tt), 1)], accum_out=rsum[:, tt:tt + 1]), x, last("xp read"))
            m.free_bank(4 + tt, a)
        mark("nb read", a)
        run_all(on_act)
        x = dve.do(lambda e, j: e.reciprocal(rinv, rsum), a)
        for tt in range(TT):
            x2 = dve.do(lambda e, j, tt=tt: e.tensor_scalar(xp[:, tt, :], xp[:, tt, :], rinv[:, tt:tt + 1], None, ALU.mult), x)
        for mt in range(MT):
            def turn(e, j, mt=mt):
                for tt in range(TT):
                    i = e.transpose(bank[4 + mt][:, tt * P:(tt + 1) * P], xp[:, tt, mt * P:(mt + 1) * P], ident)
                return i
            tr = pe.do(turn, x2, m.bank_free(4 + mt))
            a = act.do(lambda e, j, mt=mt: e.activation(xpt[:, mt, :], bank[4 + mt][:], ACT.Copy), tr, last("xpt read"))
            m.free_bank(4 + mt, a)
        mark("xp read", tr)
        copy, turn, add = mod_pair(2, mod_row_x, lambda j: j * 2 + 40, later=on_act)
        copy()
        run_all(on_act)
        for c in range(2):
            def out(e, j, c=c):
                for mt in range(MT):
                    i = e.matmul(bank[6 + c][:], xvst[:, mt, c * P:(c + 1) * P], xpt[:, mt, :], start=(mt == 0), stop=(mt == MT - 1))
                return i
            y = pe.do(out, a, vs, m.bank_free(6 + c))
            m.free_bank(6 + c, m.split(lambda j, c=c: xhi[:, j * 2 + c, :], lambda j, c=c: xlo[:, j * 2 + c, :], lambda j, c=c: bank[6 + c][:], y))
        turn()
        add()
        raw_tile(1, lambda j: xgate[:, j * 2 + 1, :], mem_done)
        mark("xpt read", y)
        mark("xvst read", y)
    prog.loop_of(X_HEADS, SLOTS, x_head)
    stored_gates(False, xgate, xhi, xlo, lambda i: colj("b_gate", i + 16))

    x_done = used_now()
    mixhi, mixlo = place("mixhi", 104, [P, KT, S], F32R), place("mixlo", 120, [P, KT, S], F32R)

    m.before_group()
    gated = dve_now()
    mix_tiles = [m.split(lambda j, k=k: mixhi[:, k, :], lambda j, k=k: mixlo[:, k, :], lambda j, k=k: resid[:, k, :], gated, x_done) for k in range(KT)]
    mix_ready = mix_tiles[-1]
    got_x = m.fetch("in_x_again", resid[:], t["xT"], mix_ready)

    gsc = small[:, 100:148]
    x = dve_now()
    for w in range(2):
        x = dve.do(lambda e, j, w=w: e.tensor_tensor(mod[:, :, w], mod[:, :, w], cols[:, COL_AT["b_mod"]:COL_AT["b_mod"] + 48], ALU.add), x)
    SH1, SC1, G1, SH2, SC2, G2 = range(0, 48, 8)
    for at, which, gain, scale in ((0, 0, "norm1_g", SC1), (8, 1, "norm1_g", SC1), (16, 0, "norm2_g", SC2)):
        mod_ready = dve.do(lambda e, j, at=at, which=which, gain=gain, scale=scale: e.scalar_tensor_tensor(
            gsc[:, at:at + 8], mod[:, scale:scale + 8, which], 1.0, cols[:, COL_AT[gain]:COL_AT[gain] + 8], ALU.add, ALU.mult), x)

    ctx = place("ctx", 136, [P, KT, M])
    chi, clo = place("ctxhi", 144, [P, KT, M], F32R), place("ctxlo", 152, [P, KT, M], F32R)
    kctx = place("kctx", 198.25, [P, 2, M])
    vctx = place("vctx", 200.25, [P, MT, MIX])
    got_ctx = m.fetch("in_ctx", ctx[:], t["ctxT"], x_done, dve_now(), act_now())
    ctx_norm, norm = Norm("norm_ctx", ctx, M, 160, sums=6), Norm("norm_mlp", resid, S, 164)
    group = m.product_group(mixhi, mixlo, mix_tiles)
    for i in range(KT):
        if i < 4:
            b, w = group[i]
        else:
            b = prog.chunk % 4
            w = m.product_tile(b, mixhi, mixlo, mix_ready)
        if i in (1, 2):
            for k in range(4 * (i - 1), 4 * i):
                ctx_norm.square(k, got_ctx)
                ctx_norm.add()
        x = dve.do(lambda e, j, i=i, b=b: e.tensor_tensor(resid[:, i, :], bank[b][:], resid[:, i, :], ALU.add), w, got_x)
        m.free_bank(b, x)
        if i:
            norm.add()
        norm.square(i, x)
        if i == 2:
            ctx_norm.root()
        elif 3 <= i < 7:
            ctx_tiles = ctx_norm.tiles(chi, clo, lambda k: gsc[:, 8 + k:9 + k], lambda k: mod[:, SH1 + k, 1:2], mod_ready,
                                       ks=(2 * (i - 3), 2 * (i - 3) + 1))
    norm.add()

    out_done = used_now()
    norm.root()
    splits, stores, ctx_banks = [], [], (2, 3)
    for b in range(2):
        w = m.product_tile(b, chi, clo, ctx_tiles[-1], cols=M, later=splits)
        stores.append(lambda b=b, w=w: m.free_bank(b, act.do(lambda e, j: e.activation(kctx[:, b, :], bank[b][:, 0:M], ACT.Copy), w)))
    for k0 in (0, 4):
        w = m.product_rows(ctx_banks, chi, clo, k0, 4, MIX, KT, ctx_tiles[-1], later=splits)
    for tt, b in enumerate(ctx_banks):
        stores.append(lambda tt=tt, b=b, w=w: m.free_bank(b, act.do(lambda e, j: e.activation(vctx[:, tt, :], bank[b][:, 0:MIX], ACT.Copy), w)))
    splits[0]()
    h_tiles = norm.tiles(hhi, hlo, lambda k: col("g_mlp", k), None, out_done,
                         after={0: [splits[1]], 1: [stores[0]], 2: [splits[2]], 3: [stores[1], splits[3]], 4: [m.before_group], 5: stores[2:]})
    h_ready = h_tiles[-1]
    HALF = FF_TILES // 2
    uhi, ulo = place("ff_uhi", 104, [P, HALF, S], F32R), place("ff_ulo", 136, [P, HALF, S], F32R)
    fr = [place(f"ff_r{i}", 168 + 2 * i, [P, S]) for i in range(2)]
    ft = [place(f"ff_t{i}", 172 + 2 * i, [P, S]) for i in range(2)]

    def up_tiles(ready, free, first=0, group=None):
        for u in range(SLOTS):
            b, p = prog.chunk % 4, u % 2
            if group:
                b, w = group[u]
            else:
                w = m.product_tile(b, hhi, hlo, ready)
            a = act.do(lambda e, j, b=b, p=p: e.activation(fr[p][:], bank[b][:], ACT.Relu), w, last(f"fr{p} read"))
            m.free_bank(b, a)
            x = dve.do(lambda e, j, p=p: e.tensor_tensor(ft[p][:], fr[p][:], fr[p][:], ALU.mult), a, last(f"ft{p} read"))
            mark(f"fr{p} read", x)
            mark(f"ft{p} read", m.split(lambda j, u=u: uhi[:, j * SLOTS + (first + u), :], lambda j, u=u: ulo[:, j * SLOTS + (first + u), :], lambda j, p=p: ft[p][:], x, free))

    def down(hi, lo, nk, ready, finish, beside=()):
        for n in range(nk // 2):
            def mm(e, j, whi, wlo, n=n):
                for o in range(4):
                    for kk in range(2):
                        k, w = 2 * n + kk, slice((kk * 4 + o) * P, (kk * 4 + o + 1) * P)
                        e.matmul(bank[o][:], whi[:, w], hi[:, k, :], start=(k == 0), stop=False)
                        e.matmul(bank[o][:], whi[:, w], lo[:, k, :], start=False, stop=False)
                        i = e.matmul(bank[o][:], wlo[:, w], hi[:, k, :], start=False, stop=(k == nk - 1))
                return i
            w = m.take(mm, ready, *([m.bank_free(o) for o in range(4)] if n == 0 else []))
            if n == 1:
                for step in beside:
                    step()
        for o in range(4):
            m.free_bank(o, finish(o, w))

    for half in range(2):
        free = used_now()
        if half == 0:
            up_tiles(h_ready, free, group=m.product_group(hhi, hlo, h_tiles))
            up_tiles(h_ready, free, first=SLOTS)
            prog.loop_of(HALF // SLOTS - 2, SLOTS, lambda: up_tiles(h_ready, free, first=2 * SLOTS))
        else:
            prog.loop_of(HALF // SLOTS, SLOTS, lambda: up_tiles(h_ready, free))
        u_ready = dve_now()
        if half == 0:
            prog.loop_of(2, HALF // 2, lambda: down(uhi, ulo, HALF, u_ready, lambda o, w: dve.do(
                lambda e, j: e.tensor_tensor(resid[:, j * 4 + o, :], bank[o][:], resid[:, j * 4 + o, :], ALU.add), w)))
    norm = Norm("norm_tokens", resid, S, 182, bufs=4)

    def add_squared(group):
        def one(o, w):
            i = 4 * group + o
            x = dve.do(lambda e, j: e.tensor_tensor(resid[:, i, :], bank[o][:], resid[:, i, :], ALU.add), w)
            norm.square(i, x)
            return x
        return one
    down(uhi, ulo, HALF, u_ready, add_squared(0))
    down(uhi, ulo, HALF, u_ready, add_squared(1), beside=[norm.add] * 4)
    for _ in range(4):
        norm.add()
    ff_done = used_now()

    feats = place("feats", 156, [33, S])
    fw1, fw2, fw3 = place("fw1", 158, [33, 64]), place("fw2", 158.25, [64, 64]), place("fw3", 158.5, [65, 1024])
    fh1, fh2 = place("fh1", 162.5, [64, S]), place("fh2", 164.5, [65, S])
    fa, fb = place("fa", 166.5, [64, S]), place("fb", 168.5, [64, S])
    filt = place("filt", 138, [P, TT, 1024])
    window = place("window", 192, [P, TT, MIX])
    fabs = place("fabs", 188, [P, 1024])
    fnorm = place("fnorm", 154, [P, 512])
    psum_, pdif = place("fsum", 164, [P, TT, 512]), place("fdif", 180, [P, TT, 512])
    fsh, fsl, fdh, fdl = (place(n, k, [P, TT, 512], F32R) for n, k in (("fsh", 156), ("fsl", 164), ("fdh", 172), ("fdl", 180)))
    kr, ks_ = place("hy_kr", 138, [P, TT, 512]), place("hy_ks", 146, [P, TT, 512])
    kt_ = place("hy_kt", 196, [P, 512])
    got_f = [m.fetch(f"in_f{i}", dst, t[src], ff_done) for i, (dst, src) in enumerate(
        ((feats[:], "feats"), (fw1[:], "filt_w1"), (fw2[:], "filt_w2"), (fw3[:], "filt_w3"), (window[:], "window")))]
    one_row = dve.do(lambda e, j: e.memset(fh2[64:65, :], 1.0), ff_done)

    def sine(dst, ps, bias, *waits):
        f = cols[0:64, COL_AT["freq"]:COL_AT["freq"] + 1]
        x = dve.do(lambda e, j: e.tensor_scalar(fa[:], ps, bias, f, ALU.add, ALU.mult), *waits)
        x = dve.do(lambda e, j: e.tensor_scalar(fb[:], fa[:], 1.0 / TWO_PI, ROUND, ALU.mult, ALU.add), x)
        x = dve.do(lambda e, j: e.tensor_scalar(fb[:], fb[:], -ROUND, None, ALU.add), x)
        for part in TWO_PI_PARTS:
            x = dve.do(lambda e, j, part=part: e.scalar_tensor_tensor(fa[:], fb[:], -part, fa[:], ALU.mult, ALU.add), x)
        x = dve.do(lambda e, j: e.tensor_scalar(fa[:], fa[:], PI_BELOW, -PI_BELOW, ALU.min, ALU.max), x)
        return act.do(lambda e, j: e.activation(dst, fa[:], ACT.Sin), x)

    def filters(made):
        p1 = pe.do(lambda e, j: e.matmul(bank[4][0:64, :], fw1[:], feats[:], start=True, stop=True), got_f[0], got_f[1], m.bank_free(4))
        s1 = sine(fh1[:], bank[4][0:64, :], cols[0:64, COL_AT["filt_b1"]:COL_AT["filt_b1"] + 1], p1)
        yield
        p2 = pe.do(lambda e, j: e.matmul(bank[5][0:64, :], fw2[:], fh1[:], start=True, stop=True), s1, got_f[2], m.bank_free(5))
        s2 = sine(fh2[0:64, :], bank[5][0:64, :], cols[0:64, COL_AT["filt_b2"]:COL_AT["filt_b2"] + 1], p2)
        m.free_bank(4, s2)
        m.free_bank(5, s2)
        yield

        def absolute_sum(tt, ready):
            for half in range(2):
                b = 6 + half
                n = pe.do(lambda e, j, half=half, b=b: e.matmul(bank[b][:], ones, fabs[:, half * 512:(half + 1) * 512],
                                                                start=(tt == 0), stop=(tt == TT - 1)), ready, *([m.bank_free(b)] if tt == 0 else []))
            mark("fabs read", n)
            return n
        for tt in range(TT):
            for half in range(2):
                b = 4 + half
                p3 = pe.do(lambda e, j, tt=tt, half=half, b=b: e.matmul(bank[b][:], fh2[:, tt * P:(tt + 1) * P], fw3[:, half * 512:(half + 1) * 512],
                                                                        start=True, stop=True), s2, one_row, got_f[3], m.bank_free(b))
                for dd in range(2):
                    x = dve.do(lambda e, j, tt=tt, half=half, b=b, dd=dd: e.tensor_tensor(
                        filt[:, tt, half * 512 + dd * MIX:half * 512 + (dd + 1) * MIX], bank[b][:, dd * MIX:(dd + 1) * MIX], window[:, tt, :], ALU.mult), p3, got_f[4])
                m.free_bank(b, x)
            a = act.do(lambda e, j, tt=tt: e.activation(fabs[:], filt[:, tt, :], ACT.Abs), x, last("fabs read"))
            yield
            n = absolute_sum(tt, a)
        filt_made = x
        for o in range(2):
            a = act.do(lambda e, j, o=o: e.activation(fnorm[:, o * MIX:(o + 1) * MIX], bank[6 + o][:, 0:MIX], ACT.Copy), n)
            x = dve.do(lambda e, j, o=o: e.scalar_tensor_tensor(fnorm[:, o * MIX:(o + 1) * MIX], bank[6 + o][:, MIX:2 * MIX], EPS,
                                                                fnorm[:, o * MIX:(o + 1) * MIX], ALU.add, ALU.add), a)
            m.free_bank(6 + o, x)
        yield
        inv = dve.do(lambda e, j: e.reciprocal(fnorm[:], fnorm[:]), x)
        for o in range(2):
            z0 = dve.do(lambda e, j, o=o: e.memset(filt[0:1, 0, o * 512 + MIX:(o + 1) * 512], 0.0), n, filt_made)
        yield
        pooled = (pe_now(),)
        for tt in range(TT):
            for o in range(2):
                cs = slice(o * MIX, (o + 1) * MIX)
                fo, ba = slice(o * 512, o * 512 + MIX), slice(o * 512 + MIX, (o + 1) * 512)
                x = dve.do(lambda e, j, tt=tt, cs=cs, fo=fo, ba=ba: e.tensor_tensor(psum_[:, tt, cs], filt[:, tt, fo], filt[:, tt, ba], ALU.add), z0)
                x = dve.do(lambda e, j, tt=tt, cs=cs, fo=fo, ba=ba: e.tensor_tensor(pdif[:, tt, cs], filt[:, tt, fo], filt[:, tt, ba], ALU.subtract), z0, *pooled)
        yield
        m.split(lambda j: fsh[:], lambda j: fsl[:], lambda j: psum_[:], x)
        split_done = m.split(lambda j: fdh[:], lambda j: fdl[:], lambda j: pdif[:], x)
        norm_done = act.do(lambda e, j: e.activation(kt_[:], fnorm[:], ACT.Copy, scale=1.0 / S), inv)
        made.extend((split_done, norm_done))

    def spectrum(dst, hi, lo):
        for n in range(2):
            def mm(e, j, whi, wlo, n=n):
                for f in range(2):
                    for k in range(TT):
                        w = slice((f * TT + k) * P, (f * TT + k + 1) * P)
                        e.matmul(bank[2 * n + f][:], whi[:, w], hi[:, k, :], start=(k == 0), stop=False)
                        e.matmul(bank[2 * n + f][:], whi[:, w], lo[:, k, :], start=False, stop=False)
                        i = e.matmul(bank[2 * n + f][:], wlo[:, w], hi[:, k, :], start=False, stop=(k == TT - 1))
                return i
            w = m.take(mm, sd, *[m.bank_free(2 * n + f) for f in range(2)])
            for f in range(2):
                m.free_bank(2 * n + f, dve.do(lambda e, j, n=n, f=f: e.tensor_tensor(dst[:, 2 * n + f, :], bank[2 * n + f][:], kt_[:], ALU.mult), w, kn_set))

    norm.root()
    m.before_group()
    h_tiles = norm.tiles(hhi, hlo, lambda k: gsc[:, k:k + 1], lambda k: mod[:, SH1 + k, 0:1], ff_done)
    h_ready = h_tiles[-1]
    pj = place("proj", 104, [P, 14, S])
    nv = place("na_v", 132, [P, TT, MIX])
    POOL, FNET, HY, NQ, NK = 0, 2, 4, 10, 12
    LEFT = 8
    plin = [place(f"pl{i}", 172 + 2.25 * i, [P, S + 2 * LEFT]) for i in range(3)]
    counts = place("counts", 178.75, [P, S])
    pw = place("pool_w", 180.75, [P, 2, P])
    got_counts = [m.fetch("in_counts", counts[:], t["pool_counts"][0], ff_done)]
    got_pw = m.fetch("in_pw", pw[:], t["pool_w"], ff_done)

    def pooling(i, stored):
        pin, s2t, s4t = plin
        x = dve.do(lambda e, j: e.memset(pin[:, 0:LEFT], 0.0), stored, last("pool read"))
        x = dve.do(lambda e, j: e.memset(pin[:, S + LEFT:S + 2 * LEFT], 0.0), last("pool read"))
        x = dve.do(lambda e, j, i=i: e.tensor_copy(pin[:, LEFT:S + LEFT], pj[:, POOL + i, :]), x)
        pn = S + 2 * LEFT

        def twice(dst, a_, w, x):
            return dve.do(lambda e, j: e.tensor_tensor(dst[:, 2 * w - 1:pn], a_[:, 2 * w - 1:pn], a_[:, w - 1:pn - w], ALU.add), x)
        if i == 0:
            x = twice(s2t, pin, 1, x)
            x4 = twice(s4t, s2t, 2, x)
            lo_, lo_off, hi_, hi_off = s2t, 0, s4t, 1
        else:
            x = twice(s2t, pin, 1, x)
            x = twice(s4t, s2t, 2, x)
            x = twice(s2t, s4t, 4, x)
            x4 = twice(s4t, s2t, 8, x)
            lo_, lo_off, hi_, hi_off = s2t, 3, s4t, 7
        x = x4
        for part, buf, off in ((slice(0, 64), lo_, lo_off), (slice(64, P), hi_, hi_off)):
            x = dve.do(lambda e, j, part=part, buf=buf, off=off: e.tensor_tensor(
                counts[part, :], buf[part, LEFT + off:LEFT + off + S], counts[part, :], ALU.mult), x, got_counts[i])
        x = dve.do(lambda e, j, i=i: e.tensor_tensor(counts[:], counts[:], pj[:, POOL + i, :], ALU.subtract), x)
        yield
        yield
        y = pe.do(lambda e, j: e.matmul(bank[4 + i][:], pw[:, i, :], counts[:], start=True, stop=True), x, got_pw, m.bank_free(4 + i))
        x = dve.do(lambda e, j, i=i: e.tensor_scalar(pj[:, POOL + i, :], bank[4 + i][:], col("pool_scale", i), None, ALU.mult), y)
        m.free_bank(4 + i, x)
        mark("pool read", x)
        if i == 0:
            got_counts.append(m.fetch("in_counts1", counts[:], t["pool_counts"][1], y))
        yield

    hpad = place("hy_pad", 203, [P, S + 2])
    dve.do(lambda e, j: e.memset(hpad[:, 0:1], 0.0), ff_done)
    pad_zero = dve.do(lambda e, j: e.memset(hpad[:, S + 1:S + 2], 0.0), ff_done)

    def short_convolution(i, stored):
        x = dve.do(lambda e, j: e.tensor_scalar(pj[:, HY + i, :], hpad[:, 0:S], col("hy_conv_w", i), col("hy_conv_b", i), ALU.mult, ALU.add), stored)
        for tap in (1, 2):
            x = dve.do(lambda e, j, tap=tap: e.scalar_tensor_tensor(pj[:, HY + i, :], hpad[:, tap:tap + S], col("hy_conv_w", 6 * tap + i),
                                                                    pj[:, HY + i, :], ALU.mult, ALU.add), x)
        mark("hpad read", x)

    made = []
    filter_steps = filters(made)
    beside = [filter_steps]
    for i in range(14):
        if i == 0:
            group = m.product_group(hhi, hlo, h_tiles)
        for steps in list(beside) if i >= 3 else ():
            if next(steps, "done") == "done":
                beside.remove(steps)
        if i < 4:
            b, w = group[i]
        else:
            b = prog.chunk % 4
            w = m.product_tile(b, hhi, hlo, h_ready)
        if HY <= i < NQ:
            stored = act.do(lambda e, j, b=b: e.activation(hpad[:, 1:S + 1], bank[b][:], ACT.Copy), w, pad_zero, last("hpad read"))
            short_convolution(i - HY, stored)
        else:
            stored = act.do(lambda e, j, i=i, b=b: e.activation(pj[:, i, :], bank[b][:], ACT.Copy), w)
        m.free_bank(b, stored)
        if i == POOL:
            beside.append(pooling(0, stored))
        elif i == POOL + 4:
            beside.append(pooling(1, tile1_stored))
        elif i == POOL + 1:
            tile1_stored = stored
    for k0 in (0, 4):
        w = m.product_rows([0, 1, 2, 3], hhi, hlo, k0, 4, MIX, KT, h_ready)
    for tt in range(TT):
        m.free_bank(tt, act.do(lambda e, j, tt=tt: e.activation(nv[:, tt, :], bank[tt][:, 0:MIX], ACT.Copy), w))
    pj_done = act_now()

    sd, kn_set = made
    spectrum(kr, fsh, fsl)
    spectrum(ks_, fdh, fdl)

    spec_done = used_now()
    cs64 = place("cs64", 172, [P, 2 * P])
    got_cs = m.fetch("in_cs", cs64[:], t["cs64"], spec_done, pj_done)

    NE = 2 * ROWS - 2
    bias = place("na_bias", 178, [P, NA_HEADS, NE * GRID])
    hide = place("na_hide", 192, [P, NE * GRID])
    got_hide = m.fetch("in_hide", hide[:], t["na_hide"], pj_done, spec_done)
    got_bias = m.fetch("in_bias", bias[:], t["rpb"], pj_done, spec_done)
    vh, vl = place("fn_vh", 164, [P, TT, 512], F32R), place("fn_vl", 154, [P, TT, 512], F32R)
    for tt in range(TT):
        for i in range(2):
            y = pe.do(lambda e, j, tt=tt, i=i: e.matmul(bank[4 + tt][:, i * 256:(i + 1) * 256], pj[:, FNET + i, tt * P:(tt + 1) * P], cs64[:],
                                                        start=(i == 0), stop=(i == 1), skip_group_check=True), pj_done, got_cs, m.bank_free(4 + tt))
        m.free_bank(4 + tt, m.split(lambda j, tt=tt: vh[:, tt, :], lambda j, tt=tt: vl[:, tt, :], lambda j, tt=tt: bank[4 + tt][:], y))
    v_ready = dve_now()
    for h in range(NA_HEADS):
        x = dve.do(lambda e, j, h=h: e.tensor_tensor(bias[:, h, :], bias[:, h, :], hide[:], ALU.add), got_hide, got_bias)
    mix_in = x

    def position_chunk(s, n, parts, ready, later=None):
        def mm(e, j, whi, wlo):
            for i in range(2):
                for kk in range(2):
                    w = slice(kk * 512, (kk + 1) * 512)
                    vhi, vlo = parts(2 * n + kk, i)
                    e.matmul(bank[i][:], vhi, whi[:, w], start=(s == 0 and n == 0 and kk == 0), stop=False)
                    e.matmul(bank[i][:], vlo, whi[:, w], start=False, stop=False)
                    ins = e.matmul(bank[i][:], vhi, wlo[:, w], start=False, stop=(s == 1 and n == 1 and kk == 1))
            return ins
        return m.take(mm, ready, *([m.bank_free(0), m.bank_free(1)] if s == n == 0 else []), later=later)

    def fourier_part(s):
        def part(k, i):
            w = slice(i * 256 + s * P, i * 256 + (s + 1) * P)
            return vh[:, k, w], vl[:, k, w]
        return part
    for s in range(2):
        for n in range(2):
            w = position_chunk(s, n, fourier_part(s), v_ready)
    for i in range(2):
        fnet_out = act.do(lambda e, j, i=i: e.activation(pj[:, FNET + i, :], bank[i][:], ACT.Copy), w)
        m.free_bank(i, fnet_out)
    fnet_done = used_now()

    zh, zl = place("hy_zh", 154, [P, TT, MIX], F32R), place("hy_zl", 158, [P, TT, MIX], F32R)
    ych, ycl, yc = place("hy_ych", 154, [P, TT, MIX], F32R), place("hy_ycl", 158, [P, TT, MIX], F32R), place("hy_yc", 158, [P, TT, MIX])
    ysh, ysl, ys = place("hy_ysh", 162, [P, TT, MIX], F32R), place("hy_ysl", 166, [P, TT, MIX], F32R), place("hy_ys", 166, [P, TT, MIX])
    zc, zs = place("hy_zc", 170, [P, TT, MIX]), place("hy_zs", 174, [P, TT, MIX])
    t2 = place("hy_t2", 51, [P, 2, MIX])
    nvst = place("na_nvst", 49.5, [P, TT + MT, NA_HD])
    qz = [[place(f"na_q{hh}{i}", 136 + 0.5 * (2 * hh + i), [P, P]) for i in range(2)] for hh in range(2)]
    sc = place("na_sc", 192, [P, S + M])
    pr = place("na_p", 195, [P, S + M])
    prt = place("na_pt", 202.5, [P, TT + MT, P])
    nmx, nnb, nsum, ninv = (small[:, i:i + 1] for i in (160, 161, 162, 163))

    def hyena_order():
        turned = []
        for i, b in enumerate((2, 0)):
            def turn(e, j, i=i, b=b):
                for tt in range(TT):
                    ins = e.transpose(bank[b][:, tt * P:(tt + 1) * P], pj[:, HY + i, tt * P:(tt + 1) * P], ident)
                return ins
            turned.append(pe.do(turn, mix_in, last("hyena z made"), m.bank_free(b)))
        yield
        for i, b in enumerate((2, 0)):
            zsrc = lambda j, b=b: bank[b][:].rearrange("p (t c) -> p t c", t=TT)
            m.free_bank(b, m.split(lambda j, i=i: zh[:, :, i * P:(i + 1) * P], lambda j, i=i: zl[:, :, i * P:(i + 1) * P], zsrc,
                                   turned[i], fnet_done, last("hyena y read")))
        z_ready = dve_now()
        yield
        for dst in (zc, zs):
            on_act, used = [], []
            for n in range(2):
                def mm(e, j, whi, wlo, n=n):
                    for f in range(2):
                        for k in range(TT):
                            w = slice((f * TT + k) * P, (f * TT + k + 1) * P)
                            out = bank[n][:, f * MIX:(f + 1) * MIX]
                            e.matmul(out, whi[:, w], zh[:, k, :], start=(k == 0), stop=False, skip_group_check=True)
                            e.matmul(out, whi[:, w], zl[:, k, :], start=False, stop=False, skip_group_check=True)
                            ins = e.matmul(out, wlo[:, w], zh[:, k, :], start=False, stop=(k == TT - 1), skip_group_check=True)
                    return ins
                used.append(m.take(mm, z_ready, m.bank_free(n), later=on_act))
            yield
            for n in range(2):
                m.free_bank(n, act.do(lambda e, j, dst=dst, n=n: e.activation(dst[:, 2 * n:2 * n + 2, :], bank[n][:].rearrange("p (f c) -> p f c", f=2), ACT.Copy),
                                      used[n], fnet_done, last("spectrum read")))
            run_all(on_act)
            zdone, w = act_now(), used[-1]
            yield

        def times(y, a1, b1, a2, b2, op, g, *waits):
            cs = lambda j: bass.ds(j * MIX, MIX)
            x = dve.do(lambda e, j: e.tensor_tensor(y[:, g, :], a1[:, g, :], b1[:, g, cs(j)], ALU.mult), *waits)
            x = dve.do(lambda e, j: e.tensor_tensor(t2[:], a2[:, g, :], b2[:, g, cs(j)], ALU.mult), x)
            mark("spectrum read", x)
            return dve.do(lambda e, j: e.tensor_tensor(y[:, g, :], y[:, g, :], t2[:], op), x)

        def product(a1, b1, a2, b2, op, hi, lo, y):
            for g in (slice(0, 2), slice(2, 4)):
                x = times(y, a1, b1, a2, b2, op, g, zdone, w, last("hyena y read"))
            return m.split(lambda j: hi[:], lambda j: lo[:], lambda j: y[:], x)

        def part(hi, lo):
            return lambda k, i: (hi[:, k, i * P:(i + 1) * P], lo[:, k, i * P:(i + 1) * P])
        yield
        ready = product(zc, kr, zs, ks_, ALU.subtract, ych, ycl, yc)
        yield
        on_act = []
        for n in range(2):
            position_chunk(0, n, part(ych, ycl), ready, on_act)
        yield
        run_all(on_act)
        ready = product(zc, ks_, zs, kr, ALU.add, ysh, ysl, ys)
        yield
        for n in range(2):
            w_out = position_chunk(1, n, part(ysh, ysl), ready, on_act)
            yield
            run_all(on_act)
            if n == 0:
                yield
        mark("hyena y read", w_out)
        for i in range(2):
            x = dve.do(lambda e, j, i=i: e.scalar_tensor_tensor(pj[:, HY + i, :], pj[:, HY + i, :], colj("hy_skip", j * 2 + i), bank[i][:],
                                                                ALU.mult, ALU.add), w_out)
            m.free_bank(i, x)
            x = dve.do(lambda e, j, i=i: e.tensor_tensor(pj[:, HY + i, :], pj[:, HY + i, :], pj[:, j * 2 + (HY + 2 + i), :], ALU.mult), x)
        mark("hyena z made", x)
        yield

    for hh in range(2):
        for i in range(2):
            q_zero = dve.do(lambda e, j, hh=hh, i=i: e.memset(qz[hh][i][:], 0.0), pj_done, spec_done)

    def mixers():
        def stage_queries(hh, tq):
            ph, at, q = slice(64 * hh, 64 * hh + 64), slice(tq * P, (tq + 1) * P), qz[hh][tq % 2]
            return dve.do(lambda e, j: e.tensor_copy(q[ph, :], pj[ph, j + NQ, at]), mix_in, q_zero, last(f"q{hh}{tq % 2} read"))

        def scores(hh, tq, qs):
            q = qz[hh][tq % 2]
            s1 = pe.do(lambda e, j: e.matmul(bank[4][:], q[:], pj[:, j + NK, :], start=True, stop=True), qs, m.bank_free(4))
            s2 = pe.do(lambda e, j: e.matmul(bank[5][:, 0:M], q[:], kctx[:, j, :], start=True, stop=True), qs, m.bank_free(5))
            mark(f"q{hh}{tq % 2} read", s2)
            return s1, s2

        def stage_values(hh):
            act.do(lambda e, j: e.activation(nvst[:, 0:TT, :], nv[:, :, bass.ds(j * 2 * NA_HD + hh * NA_HD, NA_HD)], ACT.Copy), last("nvst read"))
            return act.do(lambda e, j: e.activation(nvst[:, TT:TT + MT, :], vctx[:, :, bass.ds(j * 2 * NA_HD + hh * NA_HD, NA_HD)], ACT.Copy))

        def softmax(hh, tq, s1, s2):
            rows_at = (TT - 1 - tq) * 2 * GRID
            x = dve.do(lambda e, j: e.scalar_tensor_tensor(sc[:, 0:S], bank[4][:], NA_HD ** -0.5, bias[:, j * 2 + hh, rows_at:rows_at + S],
                                                           ALU.mult, ALU.add), s1, mix_in, last("na sc read"))
            m.free_bank(4, x)
            x = dve.do(lambda e, j: e.tensor_scalar(sc[:, S:S + M], bank[5][:, 0:M], NA_HD ** -0.5, None, ALU.mult), s2)
            m.free_bank(5, x)
            x = dve.do(lambda e, j: e.tensor_reduce(nmx, sc[:], AX, ALU.max), x)
            x = dve.do(lambda e, j: e.tensor_scalar(nnb, nmx, -1.0, None, ALU.mult), x, last("na sc read"))
            a = act.do(lambda e, j: e.activation(pr[:], sc[:], ACT.Exp, bias=nnb, accum_out=nsum), x, last("na p read"))
            mark("na sc read", a)
            x = dve.do(lambda e, j: e.reciprocal(ninv, nsum), a)
            return dve.do(lambda e, j: e.tensor_scalar(pr[:], pr[:], ninv, None, ALU.mult), x)

        def outputs(hh, tq, probs):
            ph, at = slice(64 * hh, 64 * hh + 64), slice(tq * P, (tq + 1) * P)
            for b, k0, nk in ((6, 0, TT), (7, TT, MT)):
                def turn(e, j, b=b, k0=k0, nk=nk):
                    for k in range(nk):
                        ins = e.transpose(bank[b][:, k * P:(k + 1) * P], pr[:, (k0 + k) * P:(k0 + k + 1) * P], ident)
                    return ins
                tr = pe.do(turn, probs, m.bank_free(b))
                a = act.do(lambda e, j, b=b, k0=k0, nk=nk: e.activation(prt[:, k0:k0 + nk, :], bank[b][:, 0:nk * P].rearrange("p (k c) -> p k c", k=nk), ACT.Copy),
                           tr, last("prt read"), mix_in)
                m.free_bank(b, a)
            mark("na p read", tr)
            return a

        def weighted(hh, tq, staged):
            ph, at = slice(64 * hh, 64 * hh + 64), slice(tq * P, (tq + 1) * P)

            def out(e, j):
                for k in range(TT + MT):
                    ins = e.matmul(bank[3][ph, at], nvst[:, k, :], prt[:, k, :], start=(k == 0), stop=(k == TT + MT - 1), skip_group_check=True)
                return ins
            y = pe.do(out, staged, m.bank_free(3))
            mark("prt read", y)
            mark("nvst read", y)
            return y

        hyena = hyena_order()
        steps = [(hh, tq) for hh in range(2) for tq in range(TT)]
        scored = scores(*steps[0], stage_queries(*steps[0]))
        for n, (hh, tq) in enumerate(steps):
            next(hyena, None)
            if tq == 0:
                stage_values(hh)
            if n + 1 < len(steps):
                qs = stage_queries(*steps[n + 1])
            probs = softmax(hh, tq, *scored)
            if n + 1 < len(steps):
                scored = scores(*steps[n + 1], qs)
            staged = outputs(hh, tq, probs)
            next(hyena, None)
            y = weighted(hh, tq, staged)
        m.free_bank(3, act.do(lambda e, j: e.activation(pj[:, j + NQ, :], bank[3][:], ACT.Copy), y))
        for _ in hyena:
            pass

    prog.loop_of(2, 8, mixers)
    mixed, mixed_pe = (dve_now(), act_now()), (used_now(), pe_now())
    yhi2, ylo2 = place("yhi2", 154, [P, 8, S], F32R), place("ylo2", 170, [P, 8, S], F32R)
    for i, src in enumerate((POOL, POOL + 1, FNET, FNET + 1, HY, HY + 1, NQ, NQ + 1)):
        m.split(lambda j, i=i: yhi2[:, i, :], lambda j, i=i: ylo2[:, i, :], lambda j, src=src: pj[:, src, :], *mixed, *mixed_pe)
    y_ready = dve_now()

    mghi, mglo = place("mghi", 104, [P, KT, S], F32R), place("mglo", 120, [P, KT, S], F32R)
    gs = [place(f"gate{b}", 138 + 2 * b, [P, S]) for b in range(GATES2)]
    mg, mp = place("mg", 146, [P, S]), place("mgp", 148, [P, S])
    na_done = act_now()

    def merge_tiles():
        for u in range(4):
            for b in range(GATES2):
                w = m.product_tile(b, hhi, hlo, h_ready)
                g = act.do(lambda e, j, b=b: e.activation(gs[b][:], bank[b][:], ACT.Sigmoid), w, y_ready, last(f"gate{b} read"))
                m.free_bank(b, g)

            def mm(e, j, whi, wlo):
                for b in range(GATES2):
                    for k in range(2):
                        wt = slice((2 * b + k) * P, (2 * b + k + 1) * P)
                        e.matmul(bank[4 + b][:], whi[:, wt], yhi2[:, 2 * b + k, :], start=(k == 0), stop=False)
                        e.matmul(bank[4 + b][:], whi[:, wt], ylo2[:, 2 * b + k, :], start=False, stop=False)
                        ins = e.matmul(bank[4 + b][:], wlo[:, wt], yhi2[:, 2 * b + k, :], start=False, stop=(k == 1))
                return ins
            w = m.take(mm, y_ready, *[m.bank_free(4 + b) for b in range(GATES2)])
            x = dve.do(lambda e, j: e.tensor_tensor(mg[:], bank[4][:], gs[0][:], ALU.mult), w, g, last("mg read"))
            m.free_bank(4, x)
            mark("gate0 read", x)
            for b in range(1, GATES2):
                x = dve.do(lambda e, j, b=b: e.tensor_tensor(mp[:], bank[4 + b][:], gs[b][:], ALU.mult), x)
                m.free_bank(4 + b, x)
                mark(f"gate{b} read", x)
                x = dve.do(lambda e, j: e.tensor_tensor(mg[:], mg[:], mp[:], ALU.add), x)
            merged_tiles[u] = mark("mg read", m.split(lambda j, u=u: mghi[:, j * 4 + u, :], lambda j, u=u: mglo[:, j * 4 + u, :], lambda j: mg[:], x, na_done))
    merged_tiles = {}
    prog.loop_of(2, 20, merge_tiles)
    mg_ready = dve_now()

    def gated_add(gate, i, b, w):
        return dve.do(lambda e, j: e.scalar_tensor_tensor(resid[:, i, :], bank[b][:], mod[:, gate + i, 0:1], resid[:, i, :], ALU.mult, ALU.add), w)

    norm = Norm("norm_ffn", resid, S, 138)
    m.before_group()
    group = m.product_group(mghi, mglo, [merged_tiles[max(k - 4, 0)] for k in range(KT)])
    for i in range(KT):
        b, w = group[i] if i < 4 else (prog.chunk % 4, m.product_tile(prog.chunk % 4, mghi, mglo, mg_ready))
        x = gated_add(G1, i, b, w)
        m.free_bank(b, x)
        if i:
            norm.add()
        norm.square(i, x)
    norm.add()

    merged = used_now()
    norm.root()
    m.before_group()
    h_tiles = norm.tiles(hhi, hlo, lambda k: gsc[:, 16 + k:17 + k], lambda k: mod[:, SH2 + k, 0:1], merged)
    h_ready = h_tiles[-1]
    fhi, flo = place("ffn_hi", 104, [P, FFN_TILES, S], F32R), place("ffn_lo", 148, [P, FFN_TILES, S], F32R)
    gpad = [place(f"gpad{i}", 192 + 2.25 * i, [P, S + 2]) for i in range(2)]
    gacc = [place(f"gacc{i}", 196.5 + 2 * i, [P, S]) for i in range(2)]
    gsg, gu = place("gsg", 200.5, [P, S]), place("gu", 203, [P, S])
    for i in range(2):
        x = dve.do(lambda e, j, i=i: e.memset(gpad[i][:, 0:1], 0.0), h_ready)
        gz = dve.do(lambda e, j, i=i: e.memset(gpad[i][:, S + 1:S + 2], 0.0), h_ready)

    def ffn_up(first, group=None):
        for p in range(2):
            if group:
                b, w = group[2 * p]
            else:
                b = prog.chunk % 4
                w = m.product_tile(b, hhi, hlo, h_ready)
            a = act.do(lambda e, j, b=b, p=p: e.activation(gpad[p][:, 1:S + 1], bank[b][:], ACT.Copy), w, gz, last(f"gpad{p} read"))
            m.free_bank(b, a)
            x = dve.do(lambda e, j, p=p: e.tensor_scalar(gacc[p][:], gpad[p][:, 0:S], colj("ffn_conv_w", j * 2 + (p + first)), colj("ffn_conv_b", j * 2 + (p + first)), ALU.mult, ALU.add),
                       a, last(f"gacc{p} read"))
            for tap in (1, 2):
                x = dve.do(lambda e, j, p=p, tap=tap: e.scalar_tensor_tensor(gacc[p][:], gpad[p][:, tap:tap + S], colj("ffn_conv_w", j * 2 + (p + first + tap * FFN_TILES)),
                                                                             gacc[p][:], ALU.mult, ALU.add), x)
            mark(f"gpad{p} read", x)
            a = act.do(lambda e, j, p=p: e.activation(gsg[:], gacc[p][:], ACT.Sigmoid), x, last("gsg read"))
            x = dve.do(lambda e, j, p=p: e.tensor_tensor(gacc[p][:], gacc[p][:], gsg[:], ALU.mult), a)
            mark("gsg read", x)
            if group:
                b, w = group[2 * p + 1]
            else:
                b = prog.chunk % 4
                w = m.product_tile(b, hhi, hlo, h_ready)
            x = dve.do(lambda e, j, b=b, p=p: e.tensor_tensor(gu[:], bank[b][:], gacc[p][:], ALU.mult), w, x, last("gu read"))
            m.free_bank(b, x)
            mark(f"gacc{p} read", x)
            mark("gu read", m.split(lambda j, p=p: fhi[:, j * 2 + (p + first), :], lambda j, p=p: flo[:, j * 2 + (p + first), :], lambda j: gu[:], x))
    ffn_up(0, m.product_group(hhi, hlo, h_tiles))
    ffn_up(2)
    prog.loop_of(FFN_TILES // 2 - 2, SLOTS, lambda: ffn_up(4))
    f_ready = dve_now()
    norm = Norm("norm_final", resid, S, 192, bufs=4)

    def finish(group):
        def one(o, w):
            x = gated_add(G2, 4 * group + o, o, w)
            norm.square(4 * group + o, x)
            return x
        return one
    down(fhi, flo, FFN_TILES, f_ready, finish(0))
    down(fhi, flo, FFN_TILES, f_ready, finish(1), beside=[norm.add] * 4)
    for _ in range(4):
        norm.add()

    done = used_now()
    result = place("result", 112, [P, KT, S])
    norm.root()
    stored = []
    for k in range(0, KT, 2):
        for kk in (k, k + 1):
            x = dve.do(lambda e, j, kk=kk: e.scalar_tensor_tensor(result[:, kk, :], resid[:, kk, :], col("final_g", kk), norm.r[:], ALU.mult, ALU.mult),
                       norm.rr, done)
        stored.append(m.fetch(f"out_done{k}", t["out"][:, k:k + 2, :], result[:, k:k + 2, :], x))
    m.load_chunks(m.total)
    assert prog.chunk == m.total, (prog.chunk, m.total)

    with nc.Block() as block:
        block.tensor(pe.run)
        block.scalar(act.run)
        block.vector(dve.run)
        block.gpsimd(pool.run)

        @block.sync
        def _(e):
            sp.run(e)
            for out in stored:
                e.wait_ge(out.counter.sem, 16)



def stream_plan():
    plan = []
    full = list(range(KT))

    def tiles(w, first, n, ks=full):
        for i in range(n):
            plan.append((w, ks, first + i * P, P))

    def rows(w, first, width, n, k_tiles=KT):
        nk = CHUNK // width
        for i in range(n):
            for k0 in range(0, k_tiles, nk):
                plan.append((w, list(range(k0, k0 + nk)), first + i * width, width))

    sbq, sbk, sbv, mq, mk, mv, mo = (i * D for i in range(7))
    mi = 7 * D
    xq = mi + 2 * ML_HEADS
    gate = xq + D
    tiles("w_in", sbq, 8)
    tiles("w_in", sbk, 8)
    rows("w_in", sbv, 512, 2)
    for h in range(SB_HEADS):
        tiles("w_in", gate + h * P, 1)
        tiles("w_in", mo + h * P, 1)
        rows("w_mod", h * 256, 256, 1)
    tiles("w_sb_proj", 0, 8)
    tiles("w_i", 0, 1)
    tiles("w_f", 0, 1)
    rows("w_in", mv, 512, 2)
    tiles("w_in", mq, 8)
    tiles("w_in", mk, 8)
    for h in range(ML_HEADS):
        tiles("w_in", gate + D + h * ML_HD, 1)
        rows("w_mod", 16 * P + h * 256, 256, 1)
        tiles("w_in", gate + D + h * ML_HD + P, 1)
    rows("w_mod", 24 * P, 256, 4)
    tiles("w_ml_proj", 0, 8)
    for h in range(X_HEADS):
        tiles("w_in", xq + h * X_HD, 2)
        rows("w_mod", 32 * P + h * 256, 256, 1)
    tiles("w_mem_kv", 0, 8)
    rows("w_mem_kv", D, 512, 2)
    for h in range(X_HEADS):
        tiles("w_in", gate + 2 * D + h * X_HD, 1)
        rows("w_mod", 40 * P + h * 256, 256, 1)
        tiles("w_in", gate + 2 * D + h * X_HD + P, 1)
    tiles("w_x_proj", 0, 8)
    tiles("w_out", 0, 8)
    k_at = MIX * 6
    tiles("w_in_2", k_at, 2)
    rows("w_in_2", k_at + MIX, MIX, 1)
    for half in range(2):
        tiles("w_ff1", half * 2 * D, 16)
        for g in range(2):
            for n in range(FF_TILES // 4):
                k = half * (FF_TILES // 2) + 2 * n
                plan.append(("w_ff2", [k, k + 1], g * 512, 512))
    tiles("w_in_2", 0, 14)
    rows("w_in_2", k_at + MIX, MIX, 1)
    for mat in ("cos0", "sin0"):
        for n in range(2):
            plan.append((mat, "pairs", 2 * n, P))
    for mat in ("fcos", "fsin"):
        rows(mat, 0, 512, 1, TT)
    for order in range(2):
        for mat in ("cos1", "sin1"):
            for n in range(2):
                plan.append((mat, "pairs", 2 * n, P))
        for mat in ("cos1", "sin1"):
            rows(mat, 0, 512, 1, TT)
    for i in range(KT):
        for b in range(GATES2):
            tiles("w_in_2", 8 * MIX + b * D + i * P, 1)
        plan.append(("w_branch", full, i * P, P))
    tiles("w_out_2", 0, 8)
    for i in range(FFN_TILES):
        tiles("w_up", FFN + i * P, 1)
        tiles("w_up", i * P, 1)
    for g in range(2):
        for n in range(FFN_TILES // 2):
            plan.append(("w_down", [2 * n, 2 * n + 1], g * 512, 512))
    return plan


def shape_constants():
    f = np.float32
    r = np.arange(P)
    before = (r[:, None] < r[None, :])
    sel = [np.where(r[:, None] == h, -1.0, 0.0) * np.ones((1, P)) for h in range(ML_HEADS)]
    consts = [np.eye(P), np.ones((P, P)), -np.ones((P, P)), np.where(r[:, None] >= r[None, :], -1.0, 0.0),
              np.where(before, 1.0, 0.0), np.where(before, 0.0, NEG), np.where(r[:, None] <= r[None, :], 0.0, NEG), *sel]
    out = {"consts": np.stack(consts, 1).astype(f)}
    n = np.arange(S)
    for name, a, b in (("0", 0.0, 0.5), ("1", 0.5, 0.5)):
        arg = 2 * np.pi * (n[:, None] + a) * (n[None, :] + b) / (2 * S)
        out["cos" + name], out["sin" + name] = np.cos(arg).astype(f), np.sin(arg).astype(f)
    arg = 2 * np.pi * (n[:, None] * n[None, :] % S) / S
    out["fcos"], out["fsin"] = np.cos(arg).astype(f), (-np.sin(arg)).astype(f)
    g = np.arange(64)
    arg = 2 * np.pi * (g[:, None] * g[None, :] % 64) / 64
    two = lambda a: np.kron(np.eye(2), a)
    out["cs64"] = (np.concatenate([two(np.cos(arg)), two(np.sin(arg))], 1) / np.sqrt(S * 64.0)).astype(f)
    win = np.array([2, 4, 8, 16])
    lo, hi = np.clip(n[None] - win[:, None] // 2, 0, S), np.clip(n[None] - win[:, None] // 2 + win[:, None], 0, S)
    out["pool_counts"] = np.repeat(1.0 / (hi - lo), 64, axis=0).reshape(2, P, S).astype(f)
    t = np.linspace(0.0, 1.0, S, dtype=f)[:, None]
    bands = np.linspace(1e-4, 15, 16, dtype=f)[None, :]
    ang = (f(2.0 * np.pi / S) * n.astype(f)[:, None] * bands).astype(f)
    out["feats"] = np.ascontiguousarray(np.concatenate([t, np.cos(ang), -np.sin(ang)], 1).T).astype(f)
    deltas = np.linspace(np.log(1e-2) / 1.5, np.log(1e-2) / 0.3, MIX, dtype=f)
    window = np.exp(-t * np.abs(deltas)) + f(0.05)
    out["window"] = np.ascontiguousarray(window.reshape(TT, P, MIX).transpose(1, 0, 2)).astype(f)
    c0 = np.clip(g - 8, 0, GRID - 16)
    ok = (g[None, :] >= c0[:, None]) & (g[None, :] < c0[:, None] + 16)
    out["na_hide"] = np.tile(np.where(ok, 0.0, NEG), (2, 2 * ROWS - 2)).astype(f)
    return out


def kernel(**inputs):
    from concourse import bacc
    from concourse.bass_utils import run_bass_kernel_spmd

    f = np.float32
    a = {k: np.asarray(v) for k, v in inputs.items()}
    const = shape_constants()

    def columns(v, n):
        return v.reshape(n, P).T

    def padded(v):
        out = np.zeros((P, 1), f)
        out[:v.size, 0] = v.reshape(-1)
        return out
    parts = {
        "g_mix": columns(a["g_mix"], 8), "b_gate": columns(a["b_gate"], 24), "conv_w": columns(a["conv_w"], 64),
        "conv_b": columns(a["conv_b"], 16), "ml_norm_g": columns(a["ml_norm_g"], 8), "g_mem": columns(a["g_mem"], 8),
        "q_norm_g": columns(a["q_norm_g"], 2), "k_norm_g": columns(a["k_norm_g"], 2), "g_mlp": columns(a["g_mlp"], 8),
        "norm1_g": columns(a["norm1_g_2"], 8), "norm2_g": columns(a["norm2_g_2"], 8), "b_mod": columns(a["b_mod_2"], 48),
        "c": columns(a["c_2"], 8), "c_ctx": columns(a["c_ctx_2"], 8), "pool_scale": columns(a["pool_scale_2"], 2),
        "hy_conv_w": columns(a["hyena_conv_w_2"], 18), "hy_conv_b": columns(a["hyena_conv_b_2"], 6),
        "hy_skip": columns(a["hyena_skip_2"], 4), "ffn_conv_w": columns(a["ffn_conv_w_2"], 66),
        "ffn_conv_b": columns(a["ffn_conv_b_2"], 22), "final_g": columns(a["final_norm_g_2"], 8),
        "b_i": padded(a["b_if"][0, :ML_HEADS]), "b_f": padded(a["b_if"][0, ML_HEADS:]),
        "filt_b1": padded(a["hyena_filt_b1_2"]), "filt_b2": padded(a["hyena_filt_b2_2"]), "freq": padded(a["hyena_freq_2"]),
    }
    gates_at = 7 * D
    w_i, w_f = np.zeros((D, P), f), np.zeros((D, P), f)
    w_i[:, :ML_HEADS] = a["w_in"][0][:, gates_at:gates_at + ML_HEADS]
    w_f[:, :ML_HEADS] = a["w_in"][0][:, gates_at + ML_HEADS:gates_at + 2 * ML_HEADS]
    mats = {"w_i": w_i, "w_f": w_f, "w_in_2": a["w_in_2"][0], "w_out_2": a["w_out_2"][0], "w_mod": a["w_mod_2"][0],
            "w_branch": a["w_branch_2"][0].reshape(GATES2 * MIX, D), "w_up": a["ffn_w_up_2"][0], "w_down": a["ffn_w_down_2"][0],
            **{n: a[n][0] for n in ("w_in", "w_mem_kv", "w_sb_proj", "w_ml_proj", "w_x_proj", "w_out", "w_ff1", "w_ff2")},
            **{n: const.pop(n) for n in ("cos0", "sin0", "cos1", "sin1", "fcos", "fsin")}}
    plan = stream_plan()
    stream = np.empty((len(plan), P, CHUNK), f)
    for dst, (name, ks, first, width) in zip(stream, plan):
        w = mats[name]
        if ks == "pairs":
            block = w.reshape(TT, P, TT, P)[:, :, first:first + 2].transpose(1, 2, 0, 3)
        else:
            block = w[ks[0] * P:(ks[-1] + 1) * P, first:first + width].reshape(len(ks), P, width).transpose(1, 0, 2)
        dst[:] = block.reshape(P, CHUNK)

    def turned(x, n):
        return np.ascontiguousarray(x.reshape(n, KT, P).transpose(2, 1, 0))
    pool_w = np.zeros((P, 2, P), f)
    for g in range(4):
        at = 64 * (g % 2)
        pool_w[at:at + 64, g // 2, at:at + 64] = a["pool_w_2"][0, g]
    table = np.zeros((NA_HEADS, 2 * ROWS - 1, 2 * GRID - 1), f)
    table[:, :, GRID - 16:GRID + 15] = a["na_rpb_2"][0]
    rpb = np.stack([table[:, 1 - low:2 * ROWS - 1 - low, GRID - 1 - cq:2 * GRID - 1 - cq] for low in range(2) for cq in range(GRID)])
    rpb = np.ascontiguousarray(rpb.reshape(P, NA_HEADS, (2 * ROWS - 2) * GRID))
    arrays = {
        "stream": stream, "xT": turned(a["x"], S), "memT": turned(a["mem"], M), "ctxT": turned(a["ctx_2"], M),
        "cols": np.ascontiguousarray(np.concatenate([parts[n] for n, _ in COLS], 1)), "pool_w": pool_w, "rpb": rpb,
        "filt_w1": a["hyena_filt_w1_2"][0], "filt_w2": a["hyena_filt_w2_2"][0],
        "filt_w3": np.concatenate([a["hyena_filt_w3_2"][0], a["hyena_filt_b3_2"]], 0), **const}
    nc = bacc.Bacc("TRN2", target_bir_lowering=False, num_devices=1)
    t = {n: nc.dram_tensor(f"in_{n}_dram", v.shape, mybir.dt.from_np(v.dtype), kind="ExternalInput").ap() for n, v in arrays.items()}
    t["out"] = nc.dram_tensor("out_dram", (P, KT, S), F32, kind="ExternalOutput").ap()
    program(nc, t)
    r = run_bass_kernel_spmd(nc, [{f"in_{n}_dram": v for n, v in arrays.items()}], core_ids=[0])
    out = r.results[0]["out_dram"]
    return np.ascontiguousarray(out.transpose(2, 1, 0)).reshape(1, S, D)
```
